# Optimizing a Trainium2 kernel written in Bass

```python
import jax, jax.numpy as jnp
from jax import lax
import numpy as np

D_MODEL = 1024
BATCH = 1
SEQ = 256
DEPTH = 1

CHUNK = 64
PLE_DIM = 256
HEAD_DIM = 64
SWA_HEADS = 8
SWA_KV_HEADS = 2
SWA_GROUP = SWA_HEADS // SWA_KV_HEADS
WINDOW = 128
SWA_BLOCK = WINDOW
FOX_HEADS = 8
FOX_BLOCK = 128
D_FF = 4 * D_MODEL
N_BRANCH = 2
RMS_EPS = 1e-6

SWA_Q = SWA_HEADS * HEAD_DIM
SWA_KV = SWA_KV_HEADS * HEAD_DIM
FOX_W = FOX_HEADS * HEAD_DIM
GATE_W = N_BRANCH * D_MODEL
SPLIT_POINTS = tuple(np.cumsum([SWA_Q, SWA_KV, SWA_KV, FOX_W, FOX_W, FOX_W, FOX_HEADS]).tolist())
D_IN = SPLIT_POINTS[-1] + GATE_W


def alibi_slopes(n_heads):
    return jnp.asarray(np.array([2.0 ** (-8.0 * (h + 1) / n_heads) for h in range(n_heads)], dtype=np.float32))

def rms_norm(x, g):
    x32 = x.astype(jnp.float32)
    y = x32 * lax.rsqrt(jnp.mean(jnp.square(x32), axis=-1, keepdims=True) + RMS_EPS)
    return (y * g.astype(jnp.float32)).astype(x.dtype)

def sliding_window_attention(q, k, v, sinks):
    B, S = q.shape[0], q.shape[1]
    nb = S // SWA_BLOCK
    SB = SWA_BLOCK
    qb = q.reshape(B, nb, SB, SWA_KV_HEADS, SWA_GROUP, HEAD_DIM)
    kb = k.reshape(B, nb, SB, SWA_KV_HEADS, HEAD_DIM)
    vb = v.reshape(B, nb, SB, SWA_KV_HEADS, HEAD_DIM)

    def band(t):
        prev = jnp.pad(t[:, :-1], ((0, 0), (1, 0), (0, 0), (0, 0), (0, 0)))
        return jnp.concatenate([prev, t], axis=2)

    k_band, v_band = band(kb), band(vb)
    s = jnp.einsum('bnqkgd,bnskd->bnkgqs', qb, k_band).astype(jnp.float32) * (HEAD_DIM ** -0.5)

    qi = jnp.arange(SB)[:, None] + SB
    si = jnp.arange(2 * SB)[None, :]
    chunk_diff = qi // CHUNK - si // CHUNK
    band_ok = (chunk_diff >= 0) & (chunk_diff <= WINDOW // CHUNK)
    real_key = (jnp.arange(nb)[:, None, None] > 0) | (si >= SB)[None]
    mask = band_ok[None] & real_key

    slopes = alibi_slopes(SWA_HEADS).reshape(SWA_KV_HEADS, SWA_GROUP)
    alibi = -slopes[:, :, None, None] * jnp.abs(qi - si).astype(jnp.float32)
    s = jnp.where(mask[None, :, None, None], s + alibi[None, None], -jnp.inf)

    sink = jnp.broadcast_to(sinks.astype(jnp.float32).reshape(SWA_KV_HEADS, SWA_GROUP)[None, None, :, :, None, None],
                            s.shape[:-1] + (1,))
    probs = jax.nn.softmax(jnp.concatenate([s, sink], axis=-1), axis=-1)[..., :-1]
    out = jnp.einsum('bnkgqs,bnskd->bnqkgd', probs.astype(v.dtype), v_band)
    return out.reshape(B, S, SWA_Q)

def forgetting_attention(q, k, v, f_logit):
    B, S = q.shape[0], q.shape[1]
    nb = S // FOX_BLOCK
    log_f = jax.nn.log_sigmoid(f_logit.astype(jnp.float32))
    c = jnp.cumsum(log_f, axis=1)
    c_k = c.transpose(0, 2, 1)
    kh = k.transpose(0, 2, 1, 3)
    vh = v.transpose(0, 2, 1, 3)
    q_blocks = q.reshape(B, nb, FOX_BLOCK, FOX_HEADS, HEAD_DIM).transpose(1, 0, 3, 2, 4)
    c_blocks = c.reshape(B, nb, FOX_BLOCK, FOX_HEADS).transpose(1, 0, 3, 2)
    k_pos = jnp.arange(S)
    scale = HEAD_DIM ** -0.5

    def one_block(args):
        qb, cq, n = args
        s = jnp.einsum('bhqd,bhsd->bhqs', qb, kh).astype(jnp.float32) * scale
        s = s + cq[..., None] - c_k[:, :, None, :]
        q_pos = n * FOX_BLOCK + jnp.arange(FOX_BLOCK)
        s = jnp.where((k_pos[None, :] <= q_pos[:, None])[None, None], s, -jnp.inf)
        probs = jax.nn.softmax(s, axis=-1)
        return jnp.einsum('bhqs,bhsd->bhqd', probs.astype(vh.dtype), vh)

    out = lax.map(one_block, (q_blocks, c_blocks, jnp.arange(nb, dtype=jnp.int32)))
    return out.transpose(1, 0, 3, 2, 4).reshape(B, S, FOX_W)

def first_inputs(seed: int = 0) -> dict:
    key = jax.random.key(seed)
    ks = jax.random.split(key, 18)

    def dense(k, fan_in, fan_out):
        return jax.random.normal(k, (DEPTH, fan_in, fan_out), jnp.float32) * fan_in ** -0.5

    def gain(k, shape):
        return 1.0 + 0.02 * jax.random.normal(k, shape, jnp.float32)

    return {
        "x": jax.random.normal(ks[0], (BATCH, SEQ, D_MODEL), jnp.float32),
        "p": jax.random.normal(ks[1], (DEPTH, BATCH, SEQ, PLE_DIM), jnp.float32),
        "g_mix": gain(ks[2], (DEPTH, D_MODEL)),
        "w_in": dense(ks[3], D_MODEL, D_IN),
        "b_forget": 3.0 + 0.5 * jax.random.normal(ks[4], (DEPTH, FOX_HEADS), jnp.float32),
        "swa_sinks": 0.5 * jax.random.normal(ks[5], (DEPTH, SWA_HEADS), jnp.float32),
        "w_br_swa": dense(ks[6], SWA_Q, D_MODEL),
        "w_br_fox": dense(ks[7], FOX_W, D_MODEL),
        "w_mix_out": dense(ks[8], D_MODEL, D_MODEL),
        "g_mlp": gain(ks[9], (DEPTH, D_MODEL)),
        "w_ff1": dense(ks[10], D_MODEL, D_FF),
        "w_ff2": dense(ks[11], D_FF, D_MODEL),
        "g_ple": gain(ks[12], (DEPTH, D_MODEL)),
        "w_ple_gate": dense(ks[13], D_MODEL, D_MODEL),
        "w_ple_proj": dense(ks[14], PLE_DIM, D_MODEL),
        "g_final": gain(ks[15], (D_MODEL,)),
    }

def first_block(x, p, g_mix, w_in, b_forget, swa_sinks, w_br_swa, w_br_fox, w_mix_out,
              g_mlp, w_ff1, w_ff2, g_ple, w_ple_gate, w_ple_proj, g_final):
    B, S = x.shape[0], x.shape[1]
    h = x
    for i in range(DEPTH):
        u = rms_norm(h, g_mix[i])
        z = u @ w_in[i]
        q_a, k_a, v_a, q_b, k_b, v_b, f_b, gate_logits = jnp.split(z, SPLIT_POINTS, axis=-1)
        y_a = sliding_window_attention(
            q_a.reshape(B, S, SWA_HEADS, HEAD_DIM),
            k_a.reshape(B, S, SWA_KV_HEADS, HEAD_DIM),
            v_a.reshape(B, S, SWA_KV_HEADS, HEAD_DIM),
            swa_sinks[i]) @ w_br_swa[i]
        y_b = forgetting_attention(
            q_b.reshape(B, S, FOX_HEADS, HEAD_DIM),
            k_b.reshape(B, S, FOX_HEADS, HEAD_DIM),
            v_b.reshape(B, S, FOX_HEADS, HEAD_DIM),
            f_b + b_forget[i]) @ w_br_fox[i]
        gates = jax.nn.sigmoid(gate_logits).reshape(B, S, N_BRANCH, D_MODEL)
        mixed = gates[:, :, 0] * y_a + gates[:, :, 1] * y_b
        h = h + mixed @ w_mix_out[i]
        u = rms_norm(h, g_mlp[i])
        h = h + jnp.square(jax.nn.relu(u @ w_ff1[i])) @ w_ff2[i]
        ple_gate = jax.nn.sigmoid(rms_norm(h, g_ple[i]) @ w_ple_gate[i])
        h = h + ple_gate * (p[i] @ w_ple_proj[i])
    return rms_norm(h, g_final)


N_HEADS_A = 8
HEAD_DIM_A = 64
ROT_DIM = HEAD_DIM_A // 4
ROPE_THETA = 500000.0
N_HEADS_IDX = 8
HEAD_DIM_IDX = 64
TOPK_MAX = 256
Q_BLOCK = 128
N_HEADS_R = 4
HEAD_DIM_RK = 128
HEAD_DIM_RV = 256
RET_CHUNK = 128
RET_THETA = 10000.0
D_FF_2 = 2816
NORM_EPS = 1e-6
NEG = -1e30

SPLIT_SIZES = (
    N_HEADS_A * HEAD_DIM_A,
    N_HEADS_A * HEAD_DIM_A,
    N_HEADS_A * HEAD_DIM_A,
    N_HEADS_IDX * HEAD_DIM_IDX,
    HEAD_DIM_IDX,
    N_HEADS_IDX,
    N_HEADS_R * HEAD_DIM_RK,
    N_HEADS_R * HEAD_DIM_RK,
    N_HEADS_R * HEAD_DIM_RV,
    N_HEADS_R * HEAD_DIM_RV,
    D_MODEL,
    D_MODEL,
)
D_IN_2 = sum(SPLIT_SIZES)


def _rmsnorm(x, w):
    xf = x.astype(jnp.float32)
    y = xf * lax.rsqrt(jnp.mean(xf * xf, axis=-1, keepdims=True) + NORM_EPS)
    return (y * w.astype(jnp.float32)).astype(x.dtype)

def _rope_tables(seq_len, dim, theta):
    inv = 1.0 / (theta ** (jnp.arange(0, dim, 2, dtype=jnp.float32) / dim))
    ang = jnp.arange(seq_len, dtype=jnp.float32)[:, None] * inv[None, :]
    return jnp.cos(ang), jnp.sin(ang)

def _rotate(x, cos, sin):
    x1, x2 = jnp.split(x, 2, axis=-1)
    cs, sn = cos[:, None, :], sin[:, None, :]
    return jnp.concatenate([x1 * cs - x2 * sn, x1 * sn + x2 * cs], axis=-1).astype(x.dtype)

def _partial_rope(x, cos, sin):
    return jnp.concatenate([_rotate(x[..., :ROT_DIM], cos, sin), x[..., ROT_DIM:]], axis=-1)

def _dsa_attention(q, k, v, iq, ik, iw, topk):
    B, S, H, Dh = q.shape
    n_blk = S // Q_BLOCK
    kpos = jnp.arange(S)
    ikf = ik.astype(jnp.float32)
    idx_scale = HEAD_DIM_IDX ** -0.5
    w_scale = N_HEADS_IDX ** -0.5
    att_scale = Dh ** -0.5

    def block(i):
        start = i * Q_BLOCK
        qb = lax.dynamic_slice_in_dim(q, start, Q_BLOCK, axis=1)
        iqb = lax.dynamic_slice_in_dim(iq, start, Q_BLOCK, axis=1).astype(jnp.float32)
        iwb = lax.dynamic_slice_in_dim(iw, start, Q_BLOCK, axis=1).astype(jnp.float32)
        qpos = start + jnp.arange(Q_BLOCK)
        causal = kpos[None, :] <= qpos[:, None]
        s_h = jnp.einsum('bqhd,bsd->bqhs', iqb, ikf) * idx_scale
        score = jnp.einsum('bqh,bqhs->bqs', iwb * w_scale, jax.nn.relu(s_h))
        score = jnp.where(causal[None], score, NEG)
        _, idx = lax.top_k(score, topk)
        valid = idx <= qpos[None, :, None]
        kg = jax.vmap(lambda kb, ib: kb[ib])(k, idx)
        vg = jax.vmap(lambda vb, ib: vb[ib])(v, idx)
        logits = jnp.einsum('bqhd,bqkhd->bqhk', qb, kg).astype(jnp.float32) * att_scale
        logits = jnp.where(valid[:, :, None, :], logits, NEG)
        p = jax.nn.softmax(logits, axis=-1).astype(v.dtype)
        return jnp.einsum('bqhk,bqkhd->bqhd', p, vg)

    out = lax.map(block, jnp.arange(n_blk))
    return jnp.moveaxis(out, 0, 1).reshape(B, S, H, Dh)

def _retention(q, k, v):
    B, S, H, Dk = q.shape
    Dv = v.shape[-1]
    C = RET_CHUNK
    N = S // C
    log_g = jnp.log(1.0 - 2.0 ** (-5.0 - jnp.arange(H, dtype=jnp.float32)))
    qc = q.astype(jnp.float32).reshape(B, N, C, H, Dk)
    kc = k.astype(jnp.float32).reshape(B, N, C, H, Dk)
    vc = v.astype(jnp.float32).reshape(B, N, C, H, Dv)
    j = jnp.arange(C, dtype=jnp.float32)
    diff = j[:, None] - j[None, :]
    dmask = jnp.where(diff[None] >= 0,
                      jnp.exp(log_g[:, None, None] * jnp.maximum(diff, 0.0)[None]), 0.0)
    inner = jnp.einsum('bnihd,bnjhd->bnhij', qc, kc) * dmask[None, None]
    o_in = jnp.einsum('bnhij,bnjhe->bnihe', inner, vc)
    kdec = jnp.exp(log_g[:, None] * (C - 1.0 - j)[None, :])
    u = jnp.einsum('bnjhd,hj,bnjhe->bnhde', kc, kdec, vc)
    cdec = jnp.exp(log_g * C)[None, :, None, None]

    def step(r, u_n):
        return r * cdec + u_n, r

    _, r_prev = lax.scan(step, jnp.zeros((B, H, Dk, Dv), jnp.float32), jnp.moveaxis(u, 1, 0))
    r_prev = jnp.moveaxis(r_prev, 0, 1)
    qdec = jnp.exp(log_g[None, :] * (j + 1.0)[:, None])
    o_x = jnp.einsum('bnihd,bnhde->bnihe', qc, r_prev) * qdec[None, None, :, :, None]
    return (o_in + o_x).reshape(B, S, H, Dv).astype(v.dtype)

def _head_groupnorm(o, w):
    of = o.astype(jnp.float32)
    mu = jnp.mean(of, axis=-1, keepdims=True)
    var = jnp.mean(jnp.square(of - mu), axis=-1, keepdims=True)
    y = (of - mu) * lax.rsqrt(var + NORM_EPS)
    B, S, H, Dv = o.shape
    return (y.reshape(B, S, H * Dv) * w.astype(jnp.float32)).astype(o.dtype)

def second_inputs(seed: int = 0) -> dict:
    key = jax.random.key(seed)
    ks = jax.random.split(key, 16)
    f32 = jnp.float32
    D = D_MODEL

    def lin(k, fi, fo):
        return jax.random.normal(k, (fi, fo), f32) * fi ** -0.5

    def gain(k, n):
        return 1.0 + 0.02 * jax.random.normal(k, (n,), f32)

    return {
        "x": jax.random.normal(ks[0], (BATCH, SEQ, D), f32),
        "c": jax.random.normal(ks[1], (BATCH, D), f32),
        "w_ada": lin(ks[2], D, 6 * D) * 0.5,
        "b_ada": 0.01 * jax.random.normal(ks[3], (6 * D,), f32),
        "norm1_w": gain(ks[4], D),
        "w_in": lin(ks[5], D, D_IN_2),
        "w_attn_proj": lin(ks[6], N_HEADS_A * HEAD_DIM_A, D),
        "w_ret_proj": lin(ks[7], N_HEADS_R * HEAD_DIM_RV, D),
        "gn_w": gain(ks[8], N_HEADS_R * HEAD_DIM_RV),
        "w_out": lin(ks[9], D, D),
        "norm2_w": gain(ks[10], D),
        "w_ffn_gate": lin(ks[11], D, D_FF_2),
        "w_ffn_up": lin(ks[12], D, D_FF_2),
        "w_ffn_down": lin(ks[13], D_FF_2, D),
        "final_norm_w": gain(ks[14], D),
    }

def second_block(x, c, w_ada, b_ada, norm1_w, w_in, w_attn_proj, w_ret_proj, gn_w, w_out,
              norm2_w, w_ffn_gate, w_ffn_up, w_ffn_down, final_norm_w):
    B, S, D = x.shape
    topk = min(TOPK_MAX, S // 4)
    cos_a, sin_a = _rope_tables(S, ROT_DIM, ROPE_THETA)
    cos_r, sin_r = _rope_tables(S, HEAD_DIM_RK, RET_THETA)

    mod = jnp.dot(jax.nn.silu(c), w_ada) + b_ada
    shift1, scale1, gate1, shift2, scale2, gate2 = [m[:, None, :] for m in jnp.split(mod, 6, axis=-1)]

    for _ in range(DEPTH):
        h = _rmsnorm(x, norm1_w) * (1.0 + scale1) + shift1
        proj = jnp.dot(h, w_in)
        (qa, ka, va, iq, ik, iw, qr, kr, vr, gr, ga, gb) = jnp.split(
            proj, np.cumsum(SPLIT_SIZES)[:-1], axis=-1)

        qa = _partial_rope(qa.reshape(B, S, N_HEADS_A, HEAD_DIM_A), cos_a, sin_a)
        ka = _partial_rope(ka.reshape(B, S, N_HEADS_A, HEAD_DIM_A), cos_a, sin_a)
        va = va.reshape(B, S, N_HEADS_A, HEAD_DIM_A)
        iq = _partial_rope(iq.reshape(B, S, N_HEADS_IDX, HEAD_DIM_IDX), cos_a, sin_a)
        ik = _partial_rope(ik[:, :, None, :], cos_a, sin_a)[:, :, 0, :]
        att = _dsa_attention(qa, ka, va, iq, ik, iw, topk)
        y_a = jnp.dot(att.reshape(B, S, N_HEADS_A * HEAD_DIM_A), w_attn_proj)

        qr = _rotate(qr.reshape(B, S, N_HEADS_R, HEAD_DIM_RK), cos_r, sin_r)
        kr = _rotate(kr.reshape(B, S, N_HEADS_R, HEAD_DIM_RK), cos_r, sin_r) * (HEAD_DIM_RK ** -0.5)
        ret = _retention(qr, kr, vr.reshape(B, S, N_HEADS_R, HEAD_DIM_RV))
        y_r = jnp.dot(jax.nn.silu(gr) * _head_groupnorm(ret, gn_w), w_ret_proj)

        merged = jax.nn.sigmoid(ga) * y_a + jax.nn.sigmoid(gb) * y_r
        x = x + gate1 * jnp.dot(merged, w_out)

        h2 = _rmsnorm(x, norm2_w) * (1.0 + scale2) + shift2
        ffn = jnp.dot(jax.nn.silu(jnp.dot(h2, w_ffn_gate)) * jnp.dot(h2, w_ffn_up), w_ffn_down)
        x = x + gate2 * ffn

    return _rmsnorm(x, final_norm_w)


def setup_inputs(seed=0):
    out = dict(first_inputs(seed))
    for name, value in second_inputs(seed + 1).items():
        if name != "x":
            out[name + "_2"] = value
    return out


def reference(
    x, p, g_mix, w_in, b_forget, swa_sinks, w_br_swa, w_br_fox, w_mix_out, g_mlp, w_ff1, w_ff2,
    g_ple, w_ple_gate, w_ple_proj, g_final, c_2, w_ada_2, b_ada_2, norm1_w_2, w_in_2,
    w_attn_proj_2, w_ret_proj_2, gn_w_2, w_out_2, norm2_w_2, w_ffn_gate_2, w_ffn_up_2,
    w_ffn_down_2, final_norm_w_2,
):
    x = first_block(
        x, p, g_mix, w_in, b_forget, swa_sinks, w_br_swa, w_br_fox, w_mix_out, g_mlp, w_ff1,
        w_ff2, g_ple, w_ple_gate, w_ple_proj, g_final,
    )
    return second_block(
        x, c_2, w_ada_2, b_ada_2, norm1_w_2, w_in_2, w_attn_proj_2, w_ret_proj_2, gn_w_2,
        w_out_2, norm2_w_2, w_ffn_gate_2, w_ffn_up_2, w_ffn_down_2, final_norm_w_2,
    )


_drawn_inputs = setup_inputs


def setup_inputs(seed=0):
    import zlib

    import numpy as np

    out = dict(_drawn_inputs(seed))
    spreads = {}
    factors = {'g_mix': 6.805,
     'swa_sinks': 8.0,
     'g_mlp': 3.138,
     'g_ple': 132.809,
     'g_final': 2.716,
     'b_ada_2': 4.975,
     'norm1_w_2': 8.0,
     'gn_w_2': 8.0,
     'norm2_w_2': 8.0,
     'final_norm_w_2': 24.104}
    for name, (base, spread) in spreads.items():
        noise = np.random.default_rng([zlib.crc32(name.encode()), seed]).standard_normal(out[name].shape)
        drawn = base * np.exp(spread * noise) if base else spread * noise
        out[name] = __import__('jax').numpy.asarray(drawn.astype(out[name].dtype))
    for name, factor in factors.items():
        out[name] = (out[name] * factor).astype(out[name].dtype)
    return out
```

```python
from contextlib import ExitStack

import numpy as np

import concourse.bass as bass
from concourse import mybir

P = 128
F32 = mybir.dt.float32
F32R = mybir.dt.float32r
BF16 = mybir.dt.bfloat16
ALU = mybir.AluOpType
ACT = mybir.ActivationFunctionType
AX = mybir.AxisListType

SEQ = 256
TILES = SEQ // P
D = 1024
KT = D // P
HD = 64
HEADS = 8
EPS = 1e-6
BIG = 1e30
TAKEN = -3e38
FAR = float(2.0 ** 100)
D_FF = 4096
D_FF_2 = 2816
R_HEADS = 4
R_DK = 128
R_DV = 256
TOPK = 64
KEYS = P + SEQ
TILE_KEYS = [(0, P), (P, KEYS)]

RAW = 8
SPLIT = 4
AHEAD = 3
FFN_RAW = 6
FFN_AHEAD = 2

V_GMIX, V_GMLP, V_GPLE, V_NORM1, V_NORM2, V_GN, V_BADA, V_C = 0, 8, 16, 24, 32, 40, 48, 96
V_ROWS = 104

C_IDENT = 0
C_SWA = 128
C_CAUSAL = C_SWA + KEYS
C_UPPER = C_CAUSAL + KEYS
C_COS_A = C_UPPER + P
C_SIN_A = C_COS_A + 16
C_COS_R = C_SIN_A + 16
C_SIN_R = C_COS_R + P
C_COLS = C_SIN_R + P


def constants():
    q = np.arange(P)[:, None]
    c = np.zeros((P, C_COLS), np.float32)
    c[:, C_IDENT:C_IDENT + P] = np.eye(P)
    for t, (k0, k1) in enumerate(TILE_KEYS):
        k = np.arange(k1 - k0)[None, :]
        a = q + t * P
        chunk = a // 64 - k // 64
        c[:, C_SWA + k0:C_SWA + k1] = np.where((chunk >= 0) & (chunk <= 2), np.abs(a - k), FAR)
        c[:, C_CAUSAL + k0:C_CAUSAL + k1] = np.where(k <= a, 0.0, BIG)
    c[:, C_UPPER:C_UPPER + P] = q <= np.arange(P)[None, :]
    for dim, theta, c0, s0 in ((16, 500000.0, C_COS_A, C_SIN_A), (R_DK, 10000.0, C_COS_R, C_SIN_R)):
        inv = (np.float32(1.0) / (np.float32(theta) ** (np.arange(0, dim, 2, dtype=np.float32) / np.float32(dim)))).astype(np.float32)
        ang = np.arange(SEQ, dtype=np.float32)[:, None] * inv[None, :]
        h = dim // 2
        for t in range(TILES):
            c[:, c0 + t * h:c0 + (t + 1) * h] = np.cos(ang[t * P:(t + 1) * P])
            c[:, s0 + t * h:s0 + (t + 1) * h] = np.sin(ang[t * P:(t + 1) * P])
    decay = np.zeros((P, R_HEADS, KEYS), np.float64)
    for h in range(R_HEADS):
        log_g = np.log(1.0 - 2.0 ** (-5.0 - h))
        i0 = np.arange(SEQ)[None, :] - q
        decay[:, h, :SEQ] = np.where(i0 >= 0, np.exp(log_g * np.maximum(i0, 0)), 0.0)
        i1 = np.arange(P)[None, :] - q
        decay[:, h, SEQ:] = np.where(i1 >= 0, np.exp(log_g * np.maximum(i1, 0)), 0.0)
    decay = (decay * R_DK ** -0.5).astype(np.float32).reshape(P, R_HEADS * KEYS)
    return c, decay


class Stream:

    def __init__(self):
        self.slot, self.landed, self.loads = [], [], []
        self.count = [0] * RAW

    def add(self, loads, slot=None):
        u = len(self.slot)
        s = u % RAW if slot is None else slot
        self.count[s] += 16 * len(loads)
        self.slot.append(s)
        self.landed.append(self.count[s])
        self.loads.append(loads)
        return u

    def previous(self, u):
        for v in range(u - 1, -1, -1):
            if self.slot[v] == self.slot[u]:
                return v
        return None


def build(nc, x, p, g_mix, w_in, b_forget, swa_sinks, w_br_swa, w_br_fox, w_mix_out, g_mlp, w_ff1, w_ff2,
          g_ple, w_ple_gate, w_ple_proj, g_final, c_2, w_ada_2, b_ada_2, norm1_w_2, w_in_2, w_attn_proj_2,
          w_ret_proj_2, gn_w_2, w_out_2, norm2_w_2, w_ffn_gate_2, w_ffn_up_2, w_ffn_down_2, final_norm_w_2,
          consts, decay_dram, out):

    def pair(w, kp, c0, n):
        return w.rearrange("(k p) n -> p k n", p=P)[:, 2 * kp:2 * kp + 2, c0:c0 + n]

    def wide(w, kt):
        return w.rearrange("(k p) (h n) -> p k h n", p=P, n=512)[:, kt, :, :]

    w_in1, ff1, ff2 = w_in[0], w_ff1[0], w_ff2[0]
    st = Stream()
    CH1 = [(264, [(0, 512, 256), (256, 2304, 8)]), (512, [(0, 0, 512)]), (512, [(0, 768, 512)]),
           (512, [(0, 1280, 512)]), (512, [(0, 1792, 512)])] + [(512, [(0, 2312 + 512 * i, 512)]) for i in range(4)]
    for _, parts in CH1:
        for kp in range(4):
            st.add([(d, n, pair(w_in1, kp, c, n)) for d, c, n in parts])
    U_BR = len(st.slot)
    for w in (w_br_swa[0], w_br_fox[0]):
        for half in range(2):
            for kp in range(2):
                st.add([(0, 512, pair(w, kp, 512 * half, 512))])
    U_MO = len(st.slot)
    for half in range(2):
        for kp in range(4):
            st.add([(0, 512, pair(w_mix_out[0], kp, 512 * half, 512))])
    U_FF = len(st.slot)
    for kp in range(4):
        st.add([(0, 512, pair(ff1, kp, 0, 512))])
    U_FFL = len(st.slot)
    FF_CHUNKS = D_FF // 512
    for j in range(1, FF_CHUNKS):
        for kp in range(4):
            st.add([(0, 512, pair(ff1, kp, 512 * j, 512))])
        for kk in range(4):
            st.add([(0, 512, wide(ff2, 4 * (j - 1) + kk))])
    U_FFE = len(st.slot)
    for kk in range(4):
        st.add([(0, 512, wide(ff2, 4 * (FF_CHUNKS - 1) + kk))])
    U_PP = len(st.slot)
    for kk in range(2):
        st.add([(0, 512, wide(w_ple_proj[0], kk))])
    U_PG = len(st.slot)
    for half in range(2):
        for kp in range(4):
            st.add([(0, 512, pair(w_ple_gate[0], kp, 512 * half, 512))])
    U_IN2 = len(st.slot)
    CH2 = [(512, 1536), (72, 2048), (512, 0), (512, 512), (512, 1024)] + [(512, 2120 + 512 * i) for i in range(10)]
    for n, c in CH2:
        for kp in range(4):
            st.add([(0, n, pair(w_in_2, kp, c, n))])
    U_BR2 = len(st.slot)
    for half in range(2):
        for kp in range(2):
            st.add([(0, 512, pair(w_attn_proj_2, kp, 512 * half, 512))])
    U_RP = len(st.slot)
    for half in range(2):
        for kp in range(4):
            st.add([(0, 512, pair(w_ret_proj_2, kp, 512 * half, 512))])
    U_WO = len(st.slot)
    for half in range(2):
        for kp in range(4):
            st.add([(0, 512, pair(w_out_2, kp, 512 * half, 512))])
    U_FN = len(st.slot)
    FN_CHUNKS = D_FF_2 // 256

    def fn_slot():
        return (len(st.slot) - U_FN) % FFN_RAW

    for j in range(FN_CHUNKS + 1):
        if j < FN_CHUNKS:
            for kp in range(4):
                st.add([(0, 256, pair(w_ffn_gate_2, kp, 256 * j, 256)), (256, 256, pair(w_ffn_up_2, kp, 256 * j, 256))],
                       fn_slot())
        if j:
            for kk in range(2):
                src = wide(w_ffn_down_2, 2 * (j - 1) + kk)
                st.add([(0, 512, src)] if j < FN_CHUNKS else [(d, 256, src[:, :, d:d + 256]) for d in (0, 256)], fn_slot())
    U_END = len(st.slot)
    U_FNL = U_FN + 4
    U_FNE = U_END - 2
    for u in range(U_FN, U_FN + FFN_RAW):
        assert st.previous(u) <= u - FFN_RAW
    assert U_FFL % RAW == 0 and 12 % SPLIT == 0

    with ExitStack() as ctx:
        def sb(name, shape, dt=F32):
            return ctx.enter_context(nc.sbuf_tensor(name, shape, dt))

        sems = {}

        def sem(name):
            if name not in sems:
                sems[name] = ctx.enter_context(nc.semaphore(name))
            return sems[name]

        raw = sb("raw", [P, RAW, 2, 512])
        w_hi = sb("w_hi", [P, SPLIT, 2, 512], F32R)
        w_lo = sb("w_lo", [P, SPLIT, 2, 512], F32R)
        xT_hi = sb("xT_hi", [P, KT, SEQ], F32R)
        xT_lo = sb("xT_lo", [P, KT, SEQ], F32R)
        sT_hi = sb("sT_hi", [P, KT, SEQ], F32R)
        sT_lo = sb("sT_lo", [P, KT, SEQ], F32R)
        h = sb("h", [P, TILES, D])
        nat = sb("nat", [P, 2, TILES, 512])
        junk = sb("junk", [P, D], BF16)
        cst = sb("cst", [P, C_COLS])
        zero_r = sb("zero_r", [P, P], F32R)
        identr = sb("identr", [P, P], F32R)
        slope_id = sb("slope_id", [P, HEADS, P], F32R)
        swa_dist = sb("swa_dist", [P, KEYS], F32R)
        causal_r = sb("causal_r", [P, KEYS], F32R)
        pick = sb("pick", [HEADS, HEADS, P], F32R)
        cum = sb("cum", [HEADS, 4, SEQ], F32R)
        ones = sb("ones", [P, P])
        vrows = sb("vrows", [P, P])
        vec = sb("vec", [P, V_ROWS])
        small = sb("small", [P, 640])
        gate_b = sb("gate_b", [P, 2, D])
        Z = sb("Z", [P, 15560])

        ident = cst[:, C_IDENT:C_IDENT + P]
        causal = cst[:, C_CAUSAL:C_CAUSAL + KEYS]
        upper = cst[:, C_UPPER:C_UPPER + P]

        at = [0]

        def sm(n):
            at[0] += n
            assert at[0] <= 640
            return small[:, at[0] - n:at[0]]

        rstd = sm(14).rearrange("p (k t) -> p k t", t=2)
        ssq = sm(14).rearrange("p (k t) -> p k t", t=2)
        nr8 = sm(2)
        neg_half = sm(2)
        done_mark = sm(1)
        half_rstd = sm(4).rearrange("p (k t) -> p k t", t=2)
        sink = sm(8)
        nsink = sm(8)
        bf = sm(8)
        rmin = sm(48).rearrange("p (n t) -> p n t", t=2)
        psum_e = sm(48).rearrange("p (n t) -> p n t", t=2)
        rden = sm(48).rearrange("p (n t) -> p n t", t=2)
        esink = sm(16).rearrange("p (n t) -> p n t", t=2)
        fz = sm(16).rearrange("p (t n) -> p t n", t=2)
        fa = sm(16).rearrange("p (t n) -> p t n", t=2)
        lf = sm(16).rearrange("p (t n) -> p t n", t=2)
        silu_c = sm(8)
        silu_now = sm(1)
        ctmp = sm(8)
        ada_col = sm(32)
        iw = sm(16).rearrange("p (t n) -> p t n", t=2)
        top8 = sm(16).rearrange("p (t n) -> p t n", t=2)
        gate_a1 = sm(8)
        gate_a2 = sm(8)
        bns = sm(48).rearrange("p (r t s) -> p r t s", r=4, t=2)
        mv = sm(16).rearrange("p (r t s) -> p r t s", r=4, t=2)
        gvar = sm(8).rearrange("p (r t) -> p r t", r=4)
        grstd = sm(8).rearrange("p (r t) -> p r t", r=4)
        gshift = sm(8).rearrange("p (r t) -> p r t", r=4)

        def z(c0, *dims):
            n = int(np.prod(dims))
            assert c0 + n <= Z.shape[1]
            v = Z[:, c0:c0 + n]
            if len(dims) == 2:
                v = v.rearrange("p (a b) -> p a b", a=dims[0])
            if len(dims) == 3:
                v = v.rearrange("p (a b c) -> p a b c", a=dims[0], b=dims[1])
            return v

        prob = z(0, 2, KEYS)
        probT = z(768, 2, KEYS)
        qaT = z(1536, 4, SEQ)
        kaT = z(2560, 2, SEQ)
        va = z(3072, TILES, P)
        qbT = z(3328, 4, SEQ)
        kbT = z(4352, 4, SEQ)
        vb = z(5376, TILES, 512)
        gates = z(6400, TILES, 2, D)
        ada_acc = z(0, 6 * D)
        ada_raw = z(6 * D, 4, 1536)
        p_sb = z(6 * D + 6144, TILES, SEQ)
        pp = z(6 * D, TILES, D)
        pg = z(8 * D, TILES, D)
        g_row = z(12800, D)

        gate_bias = z(10240, 2 * D)
        iqT = z(1536, 4, SEQ)
        ikT = z(2560, 1, SEQ)
        score = z(2816, KEYS)
        work = z(3200, KEYS)
        decay = z(1536, R_HEADS, KEYS)
        qsT = z(3584, 4, SEQ)
        ksT = z(4608, 4, SEQ)
        vs = z(5632, TILES, 512)
        qrT = z(6656, 4, SEQ)
        krT = z(7680, 4, SEQ)
        vr = z(8704, TILES, D)
        gr = z(10752, TILES, D)
        gates2 = {(0, 0): z(3584, TILES, 512), (0, 1): z(4608, TILES, 512), (1, 0): z(5632, TILES, 512), (1, 1): z(12800, TILES, 512)}
        temp = z(13824, 3, 512)
        grow2 = z(10752, D)
        ffn_gate = z(0, 2, 2 * 256)
        ffn_hid = z(1024, 2, 2 * 256)
        selected = swa_dist

        B = ctx.enter_context(nc.psum_tensor("B", [P, 8, 512], F32))

        landed = [sem(f"landed{i}") for i in range(RAW)]
        hi_done, lo_done, units_used = sem("hi_done"), sem("lo_done"), sem("units_used")
        block = ctx.enter_context(nc.Block())

        def spans(u):
            return max(d + n for d, n, _ in st.loads[u])

        @block.sync
        def _(sp):
            def load(u):
                prev = st.previous(u)
                if prev is not None:
                    sp.wait_ge(lo_done, prev + 1)
                for d, n, src in st.loads[u]:
                    sp.dma_start(raw[:, st.slot[u], :, d:d + n], src).then_inc(landed[st.slot[u]], 16)

            sp.dma_start(h[:, :, :], x[0].rearrange("(t p) n -> p t n", p=P)).then_inc(sem("x_in"), 16)
            for i, v in enumerate((g_mix[0], g_mlp[0], g_ple[0], norm1_w_2, norm2_w_2, gn_w_2)):
                sp.dma_start(vrows[8 * i:8 * i + 8, :], v.rearrange("(k p) -> k p", p=P)).then_inc(sem("vectors_in"), 16)
            sp.dma_start(vrows[V_BADA:V_BADA + 48, :], b_ada_2.rearrange("(k p) -> k p", p=P)).then_inc(sem("vectors_in"), 16)
            sp.dma_start(vrows[V_C:V_C + 8, :], c_2[0].rearrange("(k p) -> k p", p=P)).then_inc(sem("vectors_in"), 16)
            sp.dma_start(cst[:, :], consts).then_inc(sem("consts_in"), 16)
            for u in range(U_FFL):
                load(u)
            with sp.Fori(1, FF_CHUNKS) as j:
                for r in range(8):
                    sp.wait_ge(lo_done, j * 8 + (U_FFL + r - RAW - 7))
                    if r < 4:
                        src = ff1.rearrange("(k p) n -> p k n", p=P)[:, 2 * r:2 * r + 2, bass.ds(j * 512, 512)]
                    else:
                        src = ff2.rearrange("(k p) (h n) -> p k h n", p=P, n=512)[:, bass.ds(j * 4 + (r - 8), 1), :, :].rearrange("p k h n -> p (k h) n")
                    sp.dma_start(raw[:, st.slot[U_FFL + r], :, :], src).then_inc(landed[st.slot[U_FFL + r]], 16)
            for u in range(U_FFE, U_FNL):
                load(u)
            with sp.Fori(0, (FN_CHUNKS - 1) // 2) as i:
                for q in range(12):
                    u = U_FNL + q
                    j0, e = 1 + q // 6, q % 6
                    sp.wait_ge(lo_done, i * 12 + (u - FFN_RAW + 1))
                    if e < 4:
                        for d, w in ((0, w_ffn_gate_2), (256, w_ffn_up_2)):
                            src = w.rearrange("(k p) n -> p k n", p=P)[:, 2 * e:2 * e + 2, bass.ds(i * 512 + 256 * j0, 256)]
                            sp.dma_start(raw[:, st.slot[u], :, d:d + 256], src).then_inc(landed[st.slot[u]], 16)
                    else:
                        src = w_ffn_down_2.rearrange("(k p) (h n) -> p k h n", p=P, n=512)[
                            :, bass.ds(i * 4 + (2 * (j0 - 1) + e - 4), 1), :, :].rearrange("p k h n -> p (k h) n")
                        sp.dma_start(raw[:, st.slot[u], :, :], src).then_inc(landed[st.slot[u]], 16)
            for u in range(U_FNE, U_END):
                load(u)
            for t in range(TILES):
                sp.wait_ge(sem("y_ready"), TILES + t + 1)
                sp.dma_start(out[0, t * P:(t + 1) * P, :], h[:, t, :]).then_inc(sem("stored"), 16)
            sp.wait_ge(sem("stored"), 32)

        @block.gpsimd
        def _(pool):
            pool.dma_start(sink, swa_sinks.partition_broadcast(P).rearrange("p a n -> p (a n)")).then_inc(sem("sinks_in"), 16)
            pool.dma_start(bf, b_forget.partition_broadcast(P).rearrange("p a n -> p (a n)")).then_inc(sem("forget_in"), 16)
            pool.dma_start(g_row, g_final[None, :].partition_broadcast(P).rearrange("p a n -> p (a n)")).then_inc(sem("g_row_in"), 16)

            def root(k):
                pool.wait_ge(sem("ms_done"), k + 1)
                nc.gpsimd.tensor_tensor(rstd[:, k, :], ssq[:, k, :], neg_half, ALU.pow).then_inc(sem("rstd_done"), 1)

            nc.gpsimd.memset(neg_half, -0.5).then_inc(sem("neg_half"), 1)
            pool.wait_ge(sem("neg_half"), 1)
            root(0)
            pool.wait_ge(sem("mixed_done"), 4)
            pool.dma_start(p_sb, p[0, 0].rearrange("(t p) n -> p t n", p=P)).then_inc(sem("p_in"), 16)
            wa = w_ada_2.rearrange("(k p) n -> p k n", p=P)
            for q in range(4):
                pool.dma_start(ada_raw[:, q, :], wa[:, 0, 1536 * q:1536 * (q + 1)]).then_inc(sem(f"ada_in{q}"), 16)
            root(1)
            with pool.Fori(1, KT) as kt:
                for q in range(4):
                    pool.wait_ge(sem("ada_used"), kt * 4 + (q - 3))
                    pool.dma_start(ada_raw[:, q, :], wa[:, bass.ds(kt, 1), 1536 * q:1536 * (q + 1)].rearrange("p k n -> p (k n)")).then_inc(sem(f"ada_in{q}"), 16)
            pool.wait_ge(sem("ada_used"), 4 * KT)
            for i, v in enumerate((2, 5)):
                pool.dma_start(gate_bias[0:1, i * D:(i + 1) * D], b_ada_2[None, v * D:(v + 1) * D]).then_inc(sem("gate_bias_in"), 16)
            for k in range(2, 5):
                root(k)
            pool.wait_ge(sem("selected"), 1)
            pool.dma_start(decay.rearrange("p r n -> p (r n)"), decay_dram).then_inc(sem("decay_in"), 16)
            for i in range(R_HEADS):
                pool.wait_ge(sem("gvar"), i + 1)
                nc.gpsimd.tensor_tensor(grstd[:, i, :], gvar[:, i, :], neg_half, ALU.pow).then_inc(sem("grstd"), 1)
            pool.wait_ge(sem("mixed_done"), 8)
            pool.dma_start(grow2, final_norm_w_2[None, :].partition_broadcast(P).rearrange("p a n -> p (a n)")).then_inc(sem("grow2_in"), 16)
            root(5)
            root(6)

        @block.scalar
        def _(act):
            done = [0]

            def split_hi(u, n, landed_at, used_at):
                act.wait_ge(landed[st.slot[u]], landed_at)
                if used_at is not None:
                    act.wait_ge(units_used, used_at)
                nc.scalar.activation(w_hi[:, u % SPLIT, :, 0:n], raw[:, st.slot[u], :, 0:n], ACT.Copy).then_inc(hi_done, 1)

            def split_to(u_last):
                for u in range(done[0], u_last + 1):
                    split_hi(u, spans(u), st.landed[u], u - SPLIT + 1 if u >= SPLIT else None)
                done[0] = max(done[0], u_last + 1)

            wt = [0]

            def wide_hi(banks, dst, kt0, scale=None, bias=None):
                for i, b in enumerate(banks):
                    act.wait_ge(sem("wt_done"), wt[0] + 1)
                    for kk in range(2):
                        kt = kt0 + 2 * i + kk
                        src = B[:, b, kk * SEQ:(kk + 1) * SEQ]
                        if scale is None:
                            if kk == 0:
                                last = nc.scalar.activation(dst[:, kt:kt + 2, :], B[:, b, :].rearrange("p (k n) -> p k n", k=2), ACT.Copy)
                        elif bias is None:
                            last = nc.scalar.activation(dst[:, kt, :], src, ACT.Copy, scale=vec[:, scale + kt:scale + kt + 1])
                        else:
                            last = nc.scalar.activation(dst[:, kt, :], src, ACT.Identity, scale=scale[:, kt:kt + 1], bias=bias[:, kt:kt + 1])
                    last.then_inc(sem("wt_hi"), 1)
                    wt[0] += 1

            def sum_squares(k):
                for t in range(TILES):
                    if k or t:
                        act.wait_ge(sem("ssq_done"), 2 * k + t)
                    nc.scalar.activation(junk[:, :], h[:, t, :], ACT.Square, accum_out=ssq[:, k, t:t + 1]).then_inc(sem("ssq_done"), 1)

            def head_exp(n, swa):
                act.wait_ge(sem("rmin_done"), n + 1)
                if n >= 2:
                    act.wait_ge(sem("pt_done"), n - 1)
                for t, (k0, k1) in enumerate(TILE_KEYS):
                    last = nc.scalar.activation(prob[:, n % 2, k0:k1], B[:, 4 + n % 2, k0:k1], ACT.Exp, scale=-1.0,
                                                bias=rmin[:, n, t:t + 1], accum_out=psum_e[:, n, t:t + 1])
                if swa:
                    last = nc.scalar.activation(esink[:, n, :], rmin[:, n, :], ACT.Exp, bias=sink[:, n:n + 1])
                last.then_inc(sem("exp_done"), 1)

            def head_pt(n):
                act.wait_ge(sem("pt_done"), n + 1)
                if n >= 2:
                    act.wait_ge(sem("pv_done"), n - 1)
                nc.scalar.activation(probT[:, n % 2, :], B[:, 6, 0:KEYS], ACT.Copy).then_inc(sem("pt_copied"), 1)

            def head_out_hi(m, kt):
                act.wait_ge(sem("pv_done"), 2 * m + 2)
                nc.scalar.activation(sT_hi[:, kt, :], B[:, 7, (m % 2) * SEQ:(m % 2 + 1) * SEQ], ACT.Copy).then_inc(sem("aT_hi"), 1)

            def to_nat(k, t, src, scale, dst=None):
                return nc.scalar.activation(nat[:, k % 2, t, 0:512] if dst is None else dst, src, ACT.Copy, scale=scale)

            act.wait_ge(sem("x_in"), 16)
            sum_squares(0)
            act.wait_ge(sem("vec_T"), 1)
            nc.scalar.activation(vec[:, :], B[:, 7, 0:V_ROWS], ACT.Copy).then_inc(sem("vec_done"), 1)
            act.wait_ge(sem("vec_done"), 1)
            wide_hi((0, 1), xT_hi, 0, V_GMIX)
            split_to(0)
            wide_hi((2, 3), xT_hi, 4, V_GMIX)
            split_to(1)
            act.wait_ge(sem("nr8_done"), 1)
            split_to(AHEAD + 3)
            act.wait_ge(units_used, 4)
            for t in range(TILES):
                r = rstd[:, 0, t:t + 1]
                for dup in range(2):
                    to_nat(0, t, B[:, t, 0:P].rearrange("p (g d) -> p g d", g=2), r,
                           nat[:, 0, t, 0:2 * P].rearrange("p (g u d) -> p g u d", g=2, u=2)[:, :, dup, :])
                to_nat(0, t, B[:, t, P:2 * P], r, va[:, t, :])
                last = to_nat(0, t, B[:, t, 2 * P:2 * P + 8], r, fz[:, t, :])
            last.then_inc(sem("evac"), 1)
            for c in range(1, 5):
                split_to(4 * c + 3 + AHEAD)
                act.wait_ge(units_used, 4 * c + 4)
                if 2 <= c < 4:
                    act.wait_ge(sem("natT_bank"), 2 * c - 3)
                for t in range(TILES):
                    bank = B[:, 2 * (c % 2) + t, :]
                    r = rstd[:, 0, t:t + 1]
                    if c == 4:
                        last = to_nat(c, t, bank, r, vb[:, t, :])
                    else:
                        last = to_nat(c, t, bank, nr8[:, t:t + 1] if c < 3 else r)
                last.then_inc(sem("evac"), 1)
                if c == 1:
                    act.wait_ge(sem("f_logit"), 1)
                    nc.scalar.activation(fa, fz, ACT.Abs).then_inc(sem("f_act"), 1)
                    act.wait_ge(sem("f_act"), 1)
                    nc.scalar.activation(fa, fa, ACT.Exp, scale=-1.0).then_inc(sem("f_act"), 1)
                    act.wait_ge(sem("f_act"), 2)
                    nc.scalar.activation(fa, fa, ACT.Ln, bias=1.0).then_inc(sem("f_act"), 1)
                if c == 3:
                    act.wait_ge(sem("cum_done"), 1)
                    nc.scalar.activation(cum[:, 0, :], B[0:HEADS, 7, 0:SEQ], ACT.Copy)
                    nc.scalar.activation(cum[:, 2, :], B[0:HEADS, 7, 0:SEQ], ACT.Copy, scale=-1.0).then_inc(sem("cum_hi"), 1)
            for n in range(2 * HEADS + 4):
                u = 20 + n
                split_to(u + AHEAD)
                if n < 16 and n % 4 == 3:
                    c = 5 + n // 4
                    act.wait_ge(units_used, u + 1)
                    for t in range(TILES):
                        g = n // 4
                        last = nc.scalar.activation(gates[:, t, g // 2, 512 * (g % 2):512 * (g % 2) + 512], B[:, 2 * (c % 2) + t, :],
                                                    ACT.Tanh, scale=half_rstd[:, 0, t:t + 1])
                    last.then_inc(sem("evac"), 1)
                if n < 16:
                    head_exp(n, n < HEADS)
                if 0 <= n - 2 < 16:
                    head_pt(n - 2)
                if 4 <= n < 20 and n % 2 == 0:
                    head_out_hi(n // 2 - 2, n // 2 - 2)
            split_to(U_MO + 2)
            wide_hi((2, 3), xT_hi, 0)
            split_to(U_MO + 1 + AHEAD)
            wide_hi((0, 1), xT_hi, 4)
            split_to(U_MO + 5 + AHEAD)
            wide_hi((2, 3), sT_hi, 0, V_GMLP)
            split_to(U_MO + 7 + AHEAD)
            act.wait_ge(sem("h_done"), 4)
            sum_squares(1)
            nc.scalar.activation(ctmp, vec[:, V_C:V_C + 8], ACT.Tanh, scale=0.5).then_inc(sem("c_tanh"), 1)
            split_to(U_FF + 1 + AHEAD)
            wide_hi((4, 5), sT_hi, 4, V_GMLP)

            def relu2(j_done):
                for t in range(TILES):
                    nc.scalar.activation(nat[:, 0, t, :], B[:, t, :], ACT.Relu, scale=rstd[:, 1, t:t + 1]).then_inc(sem("relu"), 1)
                act.wait_ge(sem("relu"), j_done)
                for t in range(TILES):
                    nc.scalar.activation(nat[:, 1, t, :], nat[:, 0, t, :], ACT.Square).then_inc(sem("squared"), 1)

            def hidden_hi():
                for i, b in enumerate((2, 3)):
                    nc.scalar.activation(xT_hi[:, 2 * i:2 * i + 2, :], B[:, b, :].rearrange("p (k n) -> p k n", k=2),
                                         ACT.Copy).then_inc(sem("hid_hi"), 1)

            split_to(U_FF + 3 + AHEAD)
            act.wait_ge(sem("rstd_done"), 2)
            act.wait_ge(units_used, U_FF + 4)
            relu2(2)
            with act.Fori(1, FF_CHUNKS) as j:
                act.wait_ge(sem("hid_T"), j * 2)
                hidden_hi()

                def loop_split(r):
                    u = U_FFL + r
                    act.wait_ge(landed[st.slot[u]], j * 16 + (st.landed[u] - 16))
                    act.wait_ge(units_used, j * 8 + (u - SPLIT - 7))
                    nc.scalar.activation(w_hi[:, u % SPLIT, :, :], raw[:, st.slot[u], :, :], ACT.Copy).then_inc(hi_done, 1)

                for r in range(AHEAD, 7):
                    loop_split(r)
                act.wait_ge(units_used, j * 8 + (U_FFL - 4))
                relu2(j * 2 + 2)
                for r in range(7, 8 + AHEAD):
                    loop_split(r)
            done[0] = U_FFE + AHEAD
            act.wait_ge(sem("hid_T"), 2 * FF_CHUNKS)
            hidden_hi()
            act.wait_ge(sem("pT_done"), 1)
            nc.scalar.activation(xT_hi[:, 4:6, :], B[:, 0, :].rearrange("p (k n) -> p k n", k=2), ACT.Copy).then_inc(sem("pT_hi"), 1)
            split_to(U_FFE + 3 + AHEAD)
            act.wait_ge(sem("h_done"), 8)
            sum_squares(2)
            split_to(U_PG + 2)
            wide_hi((4, 5), sT_hi, 0, V_GPLE)
            wide_hi((6, 7), sT_hi, 4, V_GPLE)
            act.wait_ge(sem("half_done"), 2)
            for half in range(2):
                split_to(U_PG + 4 * half + 3 + AHEAD)
                act.wait_ge(units_used, U_PG + 4 * half + 4)
                for t in range(TILES):
                    nc.scalar.activation(pg[:, t, 512 * half:512 * half + 512], B[:, 4 + 2 * half + t, :], ACT.Tanh,
                                         scale=half_rstd[:, 1, t:t + 1]).then_inc(sem("pg_exp"), 1)
            act.wait_ge(sem("h_done"), 12)
            sum_squares(3)
            for i in range(4):
                act.wait_ge(sem("gate_sum"), i + 1)
                nc.scalar.activation(gate_b[:, i // 2, 512 * (i % 2):512 * (i % 2) + 512], B[:, (5, 6, 7, 0)[i], :], ACT.Copy,
                                     scale=0.5).then_inc(sem("gate_b"), 1)
            act.wait_ge(sem("y_ready"), TILES)
            sum_squares(4)
            split_to(U_IN2 + 1)
            act.wait_ge(sem("mod_1"), 1)
            wide_hi((2, 3), xT_hi, 0, gate_a1, ada_col[:, 0:8])
            wide_hi((4, 5), xT_hi, 4, gate_a1, ada_col[:, 0:8])

            for q in range(60):
                u = U_IN2 + q
                split_to(u + AHEAD)
                c = q // 4
                if q % 4 == 3:
                    act.wait_ge(units_used, u + 1)
                    if c in (2, 3, 5, 6):
                        act.wait_ge(sem("natT_bank"), {2: 9, 3: 10, 5: 12, 6: 14}[c])
                    for t in range(TILES):
                        bank = B[:, 2 * (c % 2) + t, :]
                        if c == 1:
                            for dup in range(2):
                                to_nat(1, t, bank[:, 0:HD], 1.0, nat[:, 1, t, dup * HD:(dup + 1) * HD])
                            last = to_nat(1, t, bank[:, HD:HD + 8], HEADS ** -0.5, iw[:, t, :])
                        elif c in (0, 2, 3, 5, 6):
                            last = to_nat((0, 1, 0, 1, 0, 0, 1)[c], t, bank, {0: HD ** -0.5, 2: -HD ** -0.5}.get(c, 1.0))
                        elif c == 4:
                            last = to_nat(0, t, bank, 1.0, vs[:, t, :])
                        elif c in (7, 8):
                            last = to_nat(0, t, bank, 1.0, vr[:, t, 512 * (c - 7):512 * (c - 6)])
                        elif c in (9, 10):
                            last = nc.scalar.activation(gr[:, t, 512 * (c - 9):512 * (c - 8)], bank, ACT.Tanh, scale=0.5)
                        else:
                            if c == 11 and t == 0:
                                act.wait_ge(sem("aT_lo"), 12)
                            last = nc.scalar.activation(gates2[(c - 11) // 2, (c - 11) % 2][:, t, :], bank, ACT.Tanh, scale=0.5)
                    last.then_inc(sem("evac"), 1)
                if 13 <= q < 21:
                    i = q - 13
                    act.wait_ge(sem("index_done"), i + 1)
                    if i >= 2:
                        act.wait_ge(sem("index_sum"), i - 1)
                    nc.scalar.activation(prob[:, i % 2, :], B[:, 4 + i % 2, 0:KEYS], ACT.Relu).then_inc(sem("index_relu"), 1)
                if 33 <= q < 41:
                    head_exp(q - 17, False)
                if 35 <= q < 43:
                    head_pt(q - 19)
                if q in (37, 39, 41, 43):
                    head_out_hi((q - 37) // 2 + 8, (q - 37) // 2)
                if q >= 47 and (q - 47) % 3 == 0 and (q - 47) // 3 < R_HEADS:
                    i = (q - 47) // 3
                    act.wait_ge(sem("gshift"), i + 1)
                    if i >= 2:
                        act.wait_ge(sem("y_gated"), 2 * i - 2)
                    for t in range(TILES):
                        last = nc.scalar.activation(nat[:, i % 2, t, 0:R_DV], B[:, 6 + i % 2, t * R_DV:(t + 1) * R_DV], ACT.Identity,
                                                    scale=grstd[:, i, t:t + 1], bias=gshift[:, i, t:t + 1])
                    last.then_inc(sem("og_done"), 1)
            wide_hi((4, 5), xT_hi, 0, V_GN)
            wide_hi((6, 7), xT_hi, 4, V_GN)
            split_to(U_WO + 2)
            wide_hi((2, 3), sT_hi, 0)
            split_to(U_WO + 1 + AHEAD)
            wide_hi((0, 1), sT_hi, 4)
            split_to(U_WO + 7 + AHEAD)
            act.wait_ge(sem("h_done"), 16)
            sum_squares(5)
            act.wait_ge(sem("mod_2"), 1)
            wide_hi((2, 3), xT_hi, 0, gate_a2, ada_col[:, 16:24])
            wide_hi((4, 5), xT_hi, 4, gate_a2, ada_col[:, 16:24])

            def ffn_hi(par, count):
                act.wait_ge(sem("ffn_T"), count)
                nc.scalar.activation(sT_hi[:, 2 * par:2 * par + 2, :], B[:, 2 + par, :].rearrange("p (k n) -> p k n", k=2),
                                     ACT.Copy).then_inc(sem("ffn_hi"), 1)

            def ffn_tanh(par):
                nc.scalar.activation(ffn_gate[:, par, :].rearrange("p (t n) -> p t n", t=2), B[:, 0:2, 0:256], ACT.Tanh,
                                     scale=0.5).then_inc(sem("ffn_tanh"), 1)

            split_to(U_FN + 3 + FFN_AHEAD)
            act.wait_ge(units_used, U_FN + 4)
            ffn_tanh(0)
            with act.Fori(0, (FN_CHUNKS - 1) // 2) as i:
                def ffn_split(q):
                    u = U_FNL + q
                    per = 64 if len(st.loads[u]) == 2 else 32
                    act.wait_ge(landed[st.slot[u]], i * per + st.landed[u])
                    act.wait_ge(units_used, i * 12 + (u - SPLIT + 1))
                    nc.scalar.activation(w_hi[:, u % SPLIT, :, :], raw[:, st.slot[u], :, :], ACT.Copy).then_inc(hi_done, 1)

                for half in range(2):
                    ffn_hi(half, i * 2 + (half + 1))
                    for q in range(FFN_AHEAD, 4 + FFN_AHEAD):
                        ffn_split(6 * half + q)
                    act.wait_ge(units_used, i * 12 + (U_FNL + 6 * half + 4))
                    ffn_tanh(1 - half)
                    for q in range(4 + FFN_AHEAD, 6 + FFN_AHEAD):
                        ffn_split(6 * half + q)
            done[0] = U_FNE + FFN_AHEAD
            ffn_hi(0, FN_CHUNKS)
            split_to(U_END - 1)
            act.wait_ge(sem("h_done"), 20)
            sum_squares(6)

        @block.vector
        def _(dve):
            done = [0]
            chain = [0]

            def link(ins):
                chain[0] += 1
                ins.then_inc(sem("dve_chain"), 1)
                dve.wait_ge(sem("dve_chain"), chain[0])

            def split_to(u_last):
                for u in range(done[0], u_last + 1):
                    dve.wait_ge(hi_done, u + 1)
                    n = spans(u)
                    nc.vector.tensor_tensor(w_lo[:, u % SPLIT, :, 0:n], raw[:, st.slot[u], :, 0:n],
                                            w_hi[:, u % SPLIT, :, 0:n].bitcast(F32), ALU.subtract).then_inc(lo_done, 1)
                done[0] = max(done[0], u_last + 1)

            wt = [0]

            def wide_lo(banks, hi, lo, kt0, scale=None):
                for i, b in enumerate(banks):
                    dve.wait_ge(sem("wt_hi"), wt[0] + 1)
                    k = kt0 + 2 * i
                    if scale is None:
                        last = nc.vector.tensor_tensor(lo[:, k:k + 2, :], B[:, b, :].rearrange("p (k n) -> p k n", k=2),
                                                       hi[:, k:k + 2, :].bitcast(F32), ALU.subtract)
                    else:
                        for kt in (k, k + 1):
                            last = nc.vector.scalar_tensor_tensor(lo[:, kt, :], B[:, b, (kt - k) * SEQ:(kt - k + 1) * SEQ],
                                                                  vec[:, scale + kt:scale + kt + 1], hi[:, kt, :].bitcast(F32),
                                                                  ALU.mult, ALU.subtract)
                    last.then_inc(sem("wt_lo"), 1)
                    wt[0] += 1

            def mean_square(k):
                dve.wait_ge(sem("ssq_done"), 2 * k + 2)
                nc.vector.tensor_scalar(ssq[:, k, :], ssq[:, k, :], 1.0 / D, EPS, ALU.mult, ALU.add).then_inc(sem("ms_done"), 1)

            def copy_T(k, dst, banks, n):
                for i, b in enumerate(banks):
                    dve.wait_ge(sem("natT_bank"), natb[0] + 1)
                    last = nc.vector.tensor_copy(dst[:, 2 * i:2 * i + n, :], B[:, b, 0:n * SEQ].rearrange("p (k n) -> p k n", k=n))
                    natb[0] += 1
                last.then_inc(sem("natT_copied"), 1)

            natb = [0]

            def head_min(n, swa):
                dve.wait_ge(sem("scores_done"), n + 1)
                for t, (k0, k1) in enumerate(TILE_KEYS):
                    last = nc.vector.tensor_reduce(rmin[:, n, t:t + 1], B[:, 4 + n % 2, k0:k1], AX.X, ALU.min)
                if swa:
                    link(last)
                    last = nc.vector.tensor_scalar(rmin[:, n, :], rmin[:, n, :], nsink[:, n:n + 1], None, ALU.min)
                last.then_inc(sem("rmin_done"), 1)

            def head_norm(n, swa):
                dve.wait_ge(sem("exp_done"), n + 1)
                if swa:
                    link(nc.vector.tensor_tensor(psum_e[:, n, :], psum_e[:, n, :], esink[:, n, :], ALU.add))
                link(nc.vector.reciprocal(rden[:, n, :], psum_e[:, n, :]))
                for t, (k0, k1) in enumerate(TILE_KEYS):
                    last = nc.vector.tensor_scalar(prob[:, n % 2, k0:k1], prob[:, n % 2, k0:k1], rden[:, n, t:t + 1], None, ALU.mult)
                last.then_inc(sem("probs_done"), 1)

            def head_out_lo(m, kt):
                dve.wait_ge(sem("aT_hi"), m + 1)
                nc.vector.tensor_tensor(sT_lo[:, kt, :], B[:, 7, (m % 2) * SEQ:(m % 2 + 1) * SEQ],
                                        sT_hi[:, kt, :].bitcast(F32), ALU.subtract).then_inc(sem("aT_lo"), 1)

            nc.vector.memset(zero_r[:, :].bitcast(F32), 0.0)
            nc.vector.memset(ones[:, :], 1.0).then_inc(sem("ones"), 1)
            mean_square(0)
            dve.wait_ge(sem("vec_done"), 1)
            wide_lo((0, 1), xT_hi, xT_lo, 0, V_GMIX)
            split_to(0)
            wide_lo((2, 3), xT_hi, xT_lo, 4, V_GMIX)
            split_to(1)
            dve.wait_ge(sem("rstd_done"), 1)
            nc.vector.tensor_scalar(half_rstd[:, 0, :], rstd[:, 0, :], 0.5, None, ALU.mult).then_inc(sem("half_done"), 1)
            nc.vector.tensor_scalar(nr8, rstd[:, 0, :], -HD ** -0.5, None, ALU.mult).then_inc(sem("nr8_done"), 1)
            split_to(2)
            nc.vector.tensor_copy(identr[:, :], ident)
            nc.vector.tensor_copy(swa_dist[:, :], cst[:, C_SWA:C_SWA + KEYS])
            nc.vector.tensor_copy(causal_r[:, :], causal)
            split_to(3)
            for i in range(HEADS):
                nc.vector.tensor_scalar(slope_id[:, i, :], ident, 2.0 ** -(i + 1), None, ALU.mult)
                last = nc.vector.tensor_copy(pick[:, i, :], cst[0:HEADS, C_IDENT + i:C_IDENT + i + 1].to_broadcast([HEADS, P]))
            last.then_inc(sem("tables"), 1)
            dve.wait_ge(sem("sinks_in"), 16)
            nc.vector.tensor_scalar(nsink, sink, -1.0, None, ALU.mult).then_inc(sem("nsink"), 1)
            dve.wait_ge(sem("nsink"), 1)
            split_to(AHEAD + 3)
            dve.wait_ge(sem("forget_in"), 16)
            dve.wait_ge(sem("evac"), 1)
            for t in range(TILES):
                last = nc.vector.tensor_tensor(fz[:, t, :], fz[:, t, :], bf, ALU.add)
            last.then_inc(sem("f_logit"), 1)
            split_to(7 + AHEAD)
            copy_T(0, kaT, (4,), 2)
            dve.wait_ge(sem("f_act"), 3)
            nc.vector.scalar_tensor_tensor(lf, fz, 0.0, fa, ALU.min, ALU.subtract).then_inc(sem("log_f"), 1)
            for k, dst in ((1, qaT), (2, qbT), (3, kbT)):
                split_to(4 * k + 7 + AHEAD)
                copy_T(k, dst, (4, 5), 2)
                if k == 2:
                    dve.wait_ge(sem("cum_hi"), 1)
                    link(nc.vector.tensor_tensor(cum[:, 1, :], B[0:HEADS, 7, 0:SEQ], cum[:, 0, :].bitcast(F32), ALU.subtract))
                    nc.vector.tensor_scalar(cum[:, 3, :], cum[:, 1, :].bitcast(F32), -1.0, None, ALU.mult).then_inc(sem("cum_lo"), 1)
            for n in range(2 * HEADS + 4):
                split_to(20 + n + AHEAD)
                if n < 16:
                    head_min(n, n < HEADS)
                if 0 <= n - 1 < 16:
                    head_norm(n - 1, n - 1 < HEADS)
                if n >= 4 and n % 2 == 0 and n < 20:
                    head_out_lo(n // 2 - 2, n // 2 - 2)

            def merge(half, bank_a, bank_b, count):
                for t in range(TILES):
                    for g, bank in ((0, bank_a), (1, bank_b)):
                        v = gates[:, t, g, 512 * half:512 * half + 512]
                        nc.vector.scalar_tensor_tensor(v, v, 1.0, B[:, bank + t, :], ALU.add, ALU.mult).then_inc(sem("gated"), 1)
                for t in range(TILES):
                    dve.wait_ge(sem("gated"), count + 2 * t + 2)
                    nc.vector.tensor_tensor(nat[:, half, t, :], gates[:, t, 0, 512 * half:512 * half + 512],
                                            gates[:, t, 1, 512 * half:512 * half + 512], ALU.add).then_inc(sem("mixed_done"), 1)

            def add_h(t, half, bank, factor=1.0):
                v = h[:, t, 512 * half:512 * half + 512]
                nc.vector.scalar_tensor_tensor(v, B[:, bank, :], factor, v, ALU.mult, ALU.add).then_inc(sem("h_done"), 1)

            split_to(U_BR + 5 + AHEAD)
            dve.wait_ge(units_used, U_BR + 6)
            dve.wait_ge(sem("evac"), 9)
            merge(0, 2, 4, 0)
            split_to(U_MO + 2)
            dve.wait_ge(units_used, U_MO)
            merge(1, 0, 6, 4)
            wide_lo((2, 3), xT_hi, xT_lo, 0)
            split_to(U_MO + 1 + AHEAD)
            wide_lo((0, 1), xT_hi, xT_lo, 4)
            split_to(U_MO + 3 + AHEAD)
            dve.wait_ge(units_used, U_MO + 4)
            for t in range(TILES):
                add_h(t, 0, 4 + t, 0.5)
            split_to(U_MO + 5 + AHEAD)
            wide_lo((2, 3), sT_hi, sT_lo, 0, V_GMLP)
            split_to(U_MO + 7 + AHEAD)
            dve.wait_ge(units_used, U_MO + 8)
            for t in range(TILES):
                add_h(t, 1, 6 + t, 0.5)
            mean_square(1)
            dve.wait_ge(sem("c_tanh"), 1)
            link(nc.vector.tensor_scalar(ctmp, ctmp, 0.5, 0.5, ALU.mult, ALU.add))
            link(nc.vector.tensor_tensor(silu_c, ctmp, vec[:, V_C:V_C + 8], ALU.mult))
            split_to(U_FF + 1 + AHEAD)
            wide_lo((4, 5), sT_hi, sT_lo, 4, V_GMLP)
            split_to(U_FF + 3 + AHEAD)
            for q in range(4):
                dve.wait_ge(sem(f"ada_in{q}"), 16)
                nc.vector.tensor_scalar(ada_acc[:, 1536 * q:1536 * (q + 1)], ada_raw[:, q, :], silu_c[:, 0:1], None,
                                        ALU.mult).then_inc(sem("ada_used"), 1)

            def hidden_lo():
                for i, b in enumerate((2, 3)):
                    nc.vector.tensor_tensor(xT_lo[:, 2 * i:2 * i + 2, :], B[:, b, :].rearrange("p (k n) -> p k n", k=2),
                                            xT_hi[:, 2 * i:2 * i + 2, :].bitcast(F32), ALU.subtract).then_inc(sem("hid_lo"), 1)

            with dve.Fori(1, FF_CHUNKS) as j:
                dve.wait_ge(sem("ada_used"), j * 4)
                nc.vector.tensor_copy(silu_now, silu_c[:, bass.ds(j, 1)]).then_inc(sem("silu_now"), 1)
                dve.wait_ge(sem("hid_hi"), j * 2)
                hidden_lo()
                dve.wait_ge(sem("silu_now"), j)
                for r in range(AHEAD, 8 + AHEAD):
                    u = U_FFL + r
                    dve.wait_ge(hi_done, j * 8 + (u - 7))
                    nc.vector.tensor_tensor(w_lo[:, u % SPLIT, :, :], raw[:, st.slot[u], :, :],
                                            w_hi[:, u % SPLIT, :, :].bitcast(F32), ALU.subtract).then_inc(lo_done, 1)
                    if r % 2 == 0:
                        q = r // 2 - 2
                        dve.wait_ge(sem(f"ada_in{q}"), j * 16 + 16)
                        dve.wait_ge(sem("ada_used"), j * 4 + (q - 3))
                        nc.vector.scalar_tensor_tensor(ada_acc[:, 1536 * q:1536 * (q + 1)], ada_raw[:, q, :], silu_now,
                                                       ada_acc[:, 1536 * q:1536 * (q + 1)], ALU.mult, ALU.add).then_inc(sem("ada_used"), 1)
            done[0] = U_FFE + AHEAD
            dve.wait_ge(sem("hid_hi"), 2 * FF_CHUNKS)
            hidden_lo()
            dve.wait_ge(sem("pT_hi"), 1)
            nc.vector.tensor_tensor(xT_lo[:, 4:6, :], B[:, 0, :].rearrange("p (k n) -> p k n", k=2), xT_hi[:, 4:6, :].bitcast(F32),
                                    ALU.subtract).then_inc(sem("pT_lo"), 1)
            split_to(U_FFE + 3 + AHEAD)
            dve.wait_ge(units_used, U_FFE + 4)
            for half in range(2):
                for t in range(TILES):
                    add_h(t, half, 4 + 2 * t + half)
            mean_square(2)
            dve.wait_ge(sem("rstd_done"), 3)
            nc.vector.tensor_scalar(half_rstd[:, 1, :], rstd[:, 2, :], 0.5, None, ALU.mult).then_inc(sem("half_done"), 1)
            split_to(U_PG + 2)
            wide_lo((4, 5), sT_hi, sT_lo, 0, V_GPLE)
            wide_lo((6, 7), sT_hi, sT_lo, 4, V_GPLE)
            for half in range(2):
                split_to(U_PG + 4 * half + 3 + AHEAD)
                for t in range(TILES):
                    v = pg[:, t, 512 * half:512 * half + 512]
                    dve.wait_ge(sem("pg_exp"), 2 * half + t + 1)
                    link(nc.vector.scalar_tensor_tensor(v, v, 1.0, B[:, 2 * t + half, :], ALU.add, ALU.mult))
                    hv = h[:, t, 512 * half:512 * half + 512]
                    nc.vector.scalar_tensor_tensor(hv, v, 0.5, hv, ALU.mult, ALU.add).then_inc(sem("h_done"), 1)
            mean_square(3)
            dve.wait_ge(sem("rstd_done"), 4)
            dve.wait_ge(sem("g_row_in"), 16)
            for t in range(TILES):
                nc.vector.scalar_tensor_tensor(h[:, t, :], h[:, t, :], rstd[:, 3, t:t + 1], g_row, ALU.mult, ALU.mult).then_inc(sem("y_ready"), 1)
            dve.wait_ge(sem("ada_cols"), 1)
            for i, v in enumerate((0, 3)):
                link(nc.vector.tensor_tensor(ada_col[:, 16 * i:16 * i + 16], B[:, 4, 16 * i:16 * i + 16],
                                             vec[:, V_BADA + 8 * v:V_BADA + 8 * v + 16], ALU.add))
                nc.vector.scalar_tensor_tensor((gate_a1, gate_a2)[i], ada_col[:, 16 * i + 8:16 * i + 16], 1.0,
                                               vec[:, (V_NORM1, V_NORM2)[i]:(V_NORM1, V_NORM2)[i] + 8], ALU.add, ALU.mult)\
                    .then_inc(sem(f"mod_{i + 1}"), 1)
            nc.vector.tensor_scalar(vec[:, V_GN:V_GN + 8], vec[:, V_GN:V_GN + 8], 0.5, None, ALU.mult).then_inc(sem("gn_half"), 1)

            def normalise(k):
                dve.wait_ge(sem("rstd_done"), k + 1)
                for half in range(2):
                    for t in range(TILES):
                        nc.vector.tensor_scalar(nat[:, half, t, :], h[:, t, 512 * half:512 * half + 512], rstd[:, k, t:t + 1], None,
                                                ALU.mult).then_inc(sem("normed"), 1)

            def wide_lo_affine(banks, hi, lo, kt0, a, b, count):
                for i, bk in enumerate(banks):
                    for kk in range(2):
                        kt = kt0 + 2 * i + kk
                        v = temp[:, kt % 2, 0:SEQ]
                        if kk == 0:
                            dve.wait_ge(sem("wt_hi"), wt[0] + 1)
                        if count + kt >= 2:
                            dve.wait_ge(sem("affine_lo"), count + kt - 1)
                        nc.vector.tensor_scalar(v, B[:, bk, kk * SEQ:(kk + 1) * SEQ], a[:, kt:kt + 1], b[:, kt:kt + 1], ALU.mult,
                                                ALU.add).then_inc(sem("affine"), 1)
                        dve.wait_ge(sem("affine"), count + kt + 1)
                        last = nc.vector.tensor_tensor(lo[:, kt, :], v, hi[:, kt, :].bitcast(F32), ALU.subtract)
                        last.then_inc(sem("affine_lo"), 1)
                        if kk == 1:
                            dve.wait_ge(sem("affine_lo"), count + kt + 1)
                            nc.vector.tensor_copy(done_mark, ones[:, 0:1]).then_inc(sem("wt_lo"), 1)
                    wt[0] += 1

            mean_square(4)
            normalise(4)
            split_to(U_IN2 + 1)
            wide_lo_affine((2, 3), xT_hi, xT_lo, 0, gate_a1, ada_col[:, 0:8], 0)
            wide_lo_affine((4, 5), xT_hi, xT_lo, 4, gate_a1, ada_col[:, 0:8], 0)

            def rotate(x1, x2, cos, sin, shape):
                n = int(np.prod(shape))
                names = dict(zip("abc", shape))
                v = [temp[:, i, 0:n].rearrange("p (a b c) -> p a b c", **names) for i in range(3)]
                nc.vector.tensor_tensor(v[0], x1, cos, ALU.mult)
                nc.vector.tensor_tensor(v[1], x2, sin, ALU.mult)
                link(nc.vector.tensor_tensor(v[2], x1, sin, ALU.mult))
                nc.vector.tensor_tensor(x1, v[0], v[1], ALU.subtract)
                link(nc.vector.tensor_tensor(x2, x2, cos, ALU.mult))
                nc.vector.tensor_tensor(x2, v[2], x2, ALU.add).then_inc(sem("roped"), 1)

            def rope(k, heads):
                v = nat[:, k % 2, :, 0:heads * HD].rearrange("p t (h d) -> p t h d", d=HD)
                tab = [cst[:, c:c + 16].rearrange("p (t d) -> p t d", t=2)[:, :, None, :].to_broadcast([P, 2, heads, 8]) for c in (C_COS_A, C_SIN_A)]
                rotate(v[:, :, :, 0:8], v[:, :, :, 8:16], *tab, (2, heads, 8))

            def rope_full(k):
                v = nat[:, k % 2, :, :].rearrange("p t (h d) -> p t h d", d=R_DK)
                tab = [cst[:, c:c + P].rearrange("p (t d) -> p t d", t=2)[:, :, None, :].to_broadcast([P, 2, R_HEADS, 64]) for c in (C_COS_R, C_SIN_R)]
                rotate(v[:, :, :, 0:64], v[:, :, :, 64:128], *tab, (2, R_HEADS, 64))

            ROPE = {4: (4, HEADS), 8: (5, 2), 12: (6, HEADS), 16: (7, HEADS)}
            COPY = {8: (4, iqT, (6, 7), 2), 12: (5, ikT, (6,), 1), 16: (6, qsT, (6, 7), 2), 20: (7, ksT, (6, 7), 2),
                    28: (8, qrT, (6, 7), 2), 32: (9, krT, (6, 7), 2)}
            for q in range(60):
                u = U_IN2 + q
                split_to(u + AHEAD)
                c = q // 4
                if q in COPY:
                    copy_T(*COPY[q])
                if q in ROPE:
                    dve.wait_ge(sem("evac"), 9 + c)
                    rope(*ROPE[q])
                if q in (24, 28):
                    dve.wait_ge(sem("evac"), 9 + c)
                    rope_full(8 if q == 24 else 9)
                if q in (40, 44):
                    dve.wait_ge(sem("evac"), 9 + c)
                    for t in range(TILES):
                        v = gr[:, t, 512 * (c - 10):512 * (c - 9)]
                        nc.vector.scalar_tensor_tensor(v, v, 1.0, B[:, 2 * ((c - 1) % 2) + t, :], ALU.add, ALU.mult).then_inc(sem("gr_done"), 1)
                if 13 <= q < 21:
                    i = q - 13
                    if i == 0:
                        link(nc.vector.tensor_scalar(score, causal, -1.0, 0.0, ALU.mult, ALU.add))
                    else:
                        dve.wait_ge(sem("index_sum"), i)
                    dve.wait_ge(sem("index_relu"), i + 1)
                    for t, (k0, k1) in enumerate(TILE_KEYS):
                        last = nc.vector.scalar_tensor_tensor(score[:, k0:k1], prob[:, i % 2, k0:k1], iw[:, t, i:i + 1], score[:, k0:k1],
                                                              ALU.mult, ALU.add)
                    last.then_inc(sem("index_sum"), 1)
                if 21 <= q < 29:
                    i = q - 21
                    if i == 0:
                        dve.wait_ge(sem("index_sum"), HEADS)
                    src = work if i else score
                    for t, (k0, k1) in enumerate(TILE_KEYS):
                        last = nc.vector.max(top8[:, t, :], src[:, k0:k1])
                    link(last)
                    for t, (k0, k1) in enumerate(TILE_KEYS):
                        last = nc.vector.match_replace(work[:, k0:k1], top8[:, t, :], src[:, k0:k1], TAKEN)
                    link(last)
                if q == 29:
                    link(nc.vector.tensor_scalar(work, work, TAKEN / 2, BIG, ALU.is_gt, ALU.mult))
                    nc.vector.tensor_tensor(selected[:, :], work, causal, ALU.max).then_inc(sem("selected"), 1)
                if 33 <= q < 41:
                    head_min(q - 17, False)
                if 34 <= q < 42:
                    head_norm(q - 18, False)
                if q in (37, 39, 41, 43):
                    head_out_lo((q - 37) // 2 + 8, (q - 37) // 2)
                if q >= 44 and (q - 44) % 3 == 0 and (q - 44) // 3 < R_HEADS:
                    i = (q - 44) // 3
                    dve.wait_ge(sem("decay_in"), 16)
                    dve.wait_ge(sem("kq_done"), i + 1)
                    if i >= 2:
                        dve.wait_ge(sem("av_done"), i - 1)
                    nc.vector.tensor_tensor(prob[:, i % 2, :], B[:, 4 + i % 2, 0:KEYS], decay[:, i, :], ALU.mult).then_inc(sem("decayed"), 1)
                if q >= 46 and (q - 46) % 3 == 0 and (q - 46) // 3 < R_HEADS:
                    i = (q - 46) // 3
                    dve.wait_ge(sem("av_done"), i + 1)
                    for t in range(TILES):
                        last = nc.vector.bn_stats(bns[:, i, t, :], B[:, 6 + i % 2, t * R_DV:(t + 1) * R_DV])
                    link(last)
                    for t in range(TILES):
                        last = nc.vector.bn_aggr(mv[:, i, t, :], bns[:, i, t, :])
                    link(last)
                    nc.vector.tensor_scalar(gvar[:, i, :], mv[:, i, :, 1], EPS, None, ALU.add).then_inc(sem("gvar"), 1)
                if q >= 47 and (q - 47) % 3 == 0 and (q - 47) // 3 < R_HEADS:
                    i = (q - 47) // 3
                    dve.wait_ge(sem("grstd"), i + 1)
                    nc.vector.scalar_tensor_tensor(gshift[:, i, :], mv[:, i, :, 0], -1.0, grstd[:, i, :], ALU.mult, ALU.mult)\
                        .then_inc(sem("gshift"), 1)
                if q >= 48 and (q - 48) % 3 == 0 and (q - 48) // 3 < R_HEADS:
                    i = (q - 48) // 3
                    dve.wait_ge(sem("og_done"), i + 1)
                    for t in range(TILES):
                        v = gr[:, t, i * R_DV:(i + 1) * R_DV]
                        nc.vector.tensor_tensor(v, nat[:, i % 2, t, 0:R_DV], v, ALU.mult).then_inc(sem("y_gated"), 1)

            wide_lo((4, 5), xT_hi, xT_lo, 0, V_GN)
            wide_lo((6, 7), xT_hi, xT_lo, 4, V_GN)

            def merge2(half, bank_a, bank_b, count):
                for t in range(TILES):
                    for g, bank in ((0, bank_a), (1, bank_b)):
                        v = gates2[g, half][:, t, :]
                        nc.vector.scalar_tensor_tensor(v, v, 1.0, B[:, bank + t, :], ALU.add, ALU.mult).then_inc(sem("gated"), 1)
                for t in range(TILES):
                    dve.wait_ge(sem("gated"), count + 2 * t + 2)
                    nc.vector.tensor_tensor(nat[:, half, t, :], gates2[0, half][:, t, :], gates2[1, half][:, t, :], ALU.add)\
                        .then_inc(sem("mixed_done"), 1)

            def add_gated(t, half, bank, g, i):
                v = temp[:, i % 2, :]
                if i >= 2:
                    dve.wait_ge(sem("h_done"), 12 + 4 * g + i - 1)
                link(nc.vector.tensor_tensor(v, B[:, bank, :], gate_b[:, g, 512 * half:512 * half + 512], ALU.mult))
                hv = h[:, t, 512 * half:512 * half + 512]
                nc.vector.tensor_tensor(hv, v, hv, ALU.add).then_inc(sem("h_done"), 1)

            split_to(U_RP + 3 + AHEAD)
            dve.wait_ge(units_used, U_RP + 4)
            dve.wait_ge(sem("evac"), 24)
            merge2(0, 2, 4, 8)
            split_to(U_WO + 2)
            dve.wait_ge(units_used, U_WO)
            merge2(1, 0, 6, 12)
            wide_lo((2, 3), sT_hi, sT_lo, 0)
            split_to(U_WO + 1 + AHEAD)
            wide_lo((0, 1), sT_hi, sT_lo, 4)
            split_to(U_WO + 3 + AHEAD)
            dve.wait_ge(units_used, U_WO + 4)
            for t in range(TILES):
                add_gated(t, 0, 4 + t, 0, t)
            split_to(U_WO + 7 + AHEAD)
            dve.wait_ge(units_used, U_WO + 8)
            for t in range(TILES):
                add_gated(t, 1, 6 + t, 0, 2 + t)
            mean_square(5)
            normalise(5)
            wide_lo_affine((2, 3), xT_hi, xT_lo, 0, gate_a2, ada_col[:, 16:24], 8)
            wide_lo_affine((4, 5), xT_hi, xT_lo, 4, gate_a2, ada_col[:, 16:24], 8)

            def ffn_lo(par, count):
                dve.wait_ge(sem("ffn_hi"), count)
                nc.vector.tensor_tensor(sT_lo[:, 2 * par:2 * par + 2, :], B[:, 2 + par, :].rearrange("p (k n) -> p k n", k=2),
                                        sT_hi[:, 2 * par:2 * par + 2, :].bitcast(F32), ALU.subtract).then_inc(sem("ffn_lo"), 1)

            def ffn_hidden(par, count):
                dve.wait_ge(sem("ffn_tanh"), count)
                a = ffn_gate[:, par, :].rearrange("p (t n) -> p t n", t=2)
                nc.vector.scalar_tensor_tensor(a, a, 1.0, B[:, 0:2, 0:256], ALU.add, ALU.mult).then_inc(sem("ffn_silu"), 1)
                dve.wait_ge(sem("ffn_silu"), count)
                nc.vector.tensor_tensor(ffn_hid[:, par, :].rearrange("p (t n) -> p t n", t=2), B[:, 0:2, 256:512], a, ALU.mult)\
                    .then_inc(sem("ffn_hid"), 1)

            split_to(U_FN + 3 + FFN_AHEAD)
            ffn_hidden(0, 1)
            with dve.Fori(0, (FN_CHUNKS - 1) // 2) as i:
                def ffn_split(q):
                    u = U_FNL + q
                    dve.wait_ge(hi_done, i * 12 + (u + 1))
                    nc.vector.tensor_tensor(w_lo[:, u % SPLIT, :, :], raw[:, st.slot[u], :, :],
                                            w_hi[:, u % SPLIT, :, :].bitcast(F32), ALU.subtract).then_inc(lo_done, 1)

                for half in range(2):
                    ffn_lo(half, i * 2 + (half + 1))
                    for q in range(FFN_AHEAD, 4 + FFN_AHEAD):
                        ffn_split(6 * half + q)
                    ffn_hidden(1 - half, i * 2 + (half + 2))
                    for q in range(4 + FFN_AHEAD, 6 + FFN_AHEAD):
                        ffn_split(6 * half + q)
            done[0] = U_FNE + FFN_AHEAD
            ffn_lo(0, FN_CHUNKS)
            split_to(U_END - 1)
            dve.wait_ge(units_used, U_END)
            for half in range(2):
                for t in range(TILES):
                    add_gated(t, half, 4 + 2 * t + half, 1, 2 * half + t)
            mean_square(6)
            dve.wait_ge(sem("rstd_done"), 7)
            dve.wait_ge(sem("grow2_in"), 16)
            for t in range(TILES):
                nc.vector.scalar_tensor_tensor(h[:, t, :], h[:, t, :], rstd[:, 6, t:t + 1], grow2, ALU.mult, ALU.mult).then_inc(sem("y_ready"), 1)

        @block.tensor
        def _(pe):
            def mm3(bank, xh, xl, wh, wl, start, stop):
                nc.tensor.matmul(bank, xh, wh, start=start, stop=False)
                nc.tensor.matmul(bank, xh, wl, start=False, stop=False)
                return nc.tensor.matmul(bank, xl, wh, start=False, stop=stop)

            def unit_pair(u, xh, xl, kt0, banks, first, last, n=None):
                n = spans(u) if n is None else n
                s = u % SPLIT
                for kk in range(2):
                    for t in range(TILES):
                        rows = slice(t * P, (t + 1) * P)
                        m = mm3(B[:, banks[t], 0:n], xh[:, kt0 + kk, rows], xl[:, kt0 + kk, rows],
                                w_hi[:, s, kk, 0:n], w_lo[:, s, kk, 0:n], first and kk == 0, last and kk == 1)
                m.then_inc(units_used, 1)

            def unit_wide(u, xh, xl, kt, banks, first, last):
                s = u % SPLIT
                for t in range(TILES):
                    rows = slice(t * P, (t + 1) * P)
                    for half in range(2):
                        m = mm3(B[:, banks[t][half], :], xh[:, kt, rows], xl[:, kt, rows], w_hi[:, s, half, :], w_lo[:, s, half, :],
                                first, last)
                m.then_inc(units_used, 1)

            def transposes(banks, src, name, nk=2):
                for i, b in enumerate(banks):
                    for kk in range(nk):
                        for t in range(TILES):
                            m = nc.tensor.transpose(B[:, b, kk * SEQ + t * P:kk * SEQ + (t + 1) * P], src(t, 2 * i + kk), ident)
                    m.then_inc(sem(name), 1)

            def head_slices(n):
                return 64 * (n % 2), 64 * (n % 2) + 64, (n % HEADS) // 2

            def head_pt(n):
                pe.wait_ge(sem("probs_done"), n + 1)
                if n:
                    pe.wait_ge(sem("pt_copied"), n)
                for i, (k0, q0) in enumerate(((0, 0), (P, P), (2 * P, 2 * P))):
                    m = nc.tensor.transpose(B[:, 6, i * P:(i + 1) * P], prob[:, n % 2, k0:k0 + P], ident)
                m.then_inc(sem("pt_done"), 1)

            def head_pv(n, v, c0):
                pe.wait_ge(sem("pt_copied"), n + 1)
                m_ = n // 2
                if n % 2 == 0 and m_ >= 1:
                    pe.wait_ge(sem("aT_lo"), m_)
                p0 = 64 * (n % 2)
                f0 = (m_ % 2) * SEQ
                nc.tensor.matmul(B[p0:p0 + 64, 7, f0:f0 + SEQ], v[:, 0, c0:c0 + HD], probT[:, n % 2, 0:SEQ], start=True, stop=False)
                nc.tensor.matmul(B[p0:p0 + 64, 7, f0 + P:f0 + SEQ], v[:, 1, c0:c0 + HD], probT[:, n % 2, SEQ:KEYS],
                                 start=False, stop=True).then_inc(sem("pv_done"), 1)

            pe.wait_ge(sem("consts_in"), 16)
            pe.wait_ge(sem("vectors_in"), 128)
            nc.tensor.transpose(B[:, 7, 0:V_ROWS], vrows[0:V_ROWS, :], ident[0:V_ROWS, 0:V_ROWS]).then_inc(sem("vec_T"), 1)
            pe.wait_ge(sem("x_in"), 16)
            transposes((0, 1), lambda t, k: h[:, t, k * P:(k + 1) * P], "wt_done")
            transposes((2, 3), lambda t, k: h[:, t, (4 + k) * P:(5 + k) * P], "wt_done")
            for c in range(5):
                banks = (2 * (c % 2), 2 * (c % 2) + 1)
                for kp in range(4):
                    u = 4 * c + kp
                    if c == 0:
                        pe.wait_ge(sem("wt_lo"), max(kp + 1, 2))
                    elif c == 1 and kp == 0:
                        pe.wait_ge(sem("wt_lo"), 4)
                    if c >= 2 and kp == 0:
                        pe.wait_ge(sem("evac"), c - 1)
                    pe.wait_ge(lo_done, u + 1)
                    unit_pair(u, xT_hi, xT_lo, 2 * kp, banks, kp == 0, kp == 3)
                if c >= 1:
                    k = c - 1
                    pe.wait_ge(sem("evac"), c)
                    if k:
                        pe.wait_ge(sem("natT_copied"), k)
                    if k == 0:
                        transposes((4,), lambda t, kk: nat[:, 0, t, kk * P:(kk + 1) * P], "natT_bank")
                    else:
                        transposes((4, 5), lambda t, kk: nat[:, k % 2, t, kk * P:(kk + 1) * P], "natT_bank")
                if c == 2:
                    pe.wait_ge(sem("log_f"), 1)
                    pe.wait_ge(sem("ones"), 1)
                    nc.tensor.matmul(B[0:HEADS, 7, 0:P], lf[:, 0, :], upper, start=True, stop=True)
                    nc.tensor.matmul(B[0:HEADS, 7, P:SEQ], lf[:, 0, :], ones[:, :], start=True, stop=False)
                    nc.tensor.matmul(B[0:HEADS, 7, P:SEQ], lf[:, 1, :], upper, start=False, stop=True).then_inc(sem("cum_done"), 1)
            for n in range(2 * HEADS + 4):
                u = 20 + n
                c = u // 4
                kp = u % 4
                if n < 16:
                    if kp == 0:
                        pe.wait_ge(sem("evac"), c - 1)
                    pe.wait_ge(lo_done, u + 1)
                    unit_pair(u, xT_hi, xT_lo, 2 * kp, (2 * (c % 2), 2 * (c % 2) + 1), kp == 0, kp == 3)
                else:
                    i = n - 16
                    if i == 0:
                        pe.wait_ge(sem("aT_lo"), 4)
                        pe.wait_ge(sem("evac"), 8)
                    if i == 2:
                        pe.wait_ge(sem("evac"), 9)
                    pe.wait_ge(lo_done, u + 1)
                    unit_pair(u, sT_hi, sT_lo, 2 * (i % 2), ((2, 3), (0, 1))[i // 2], i % 2 == 0, i % 2 == 1)
                if n < 16:
                    if n == 0:
                        pe.wait_ge(sem("tables"), 1)
                        pe.wait_ge(sem("natT_copied"), 4)
                        pe.wait_ge(sem("cum_lo"), 1)
                    if n >= 2:
                        pe.wait_ge(sem("exp_done"), n - 1)
                    p0, p1, kq = head_slices(n)
                    if n < HEADS:
                        qT, kT, kk = qaT, kaT, n // 4
                    else:
                        qT, kT, kk = qbT, kbT, kq
                    for t, (k0, k1) in enumerate(TILE_KEYS):
                        s = B[:, 4 + n % 2, k0:k1]
                        rows = slice(t * P, (t + 1) * P)
                        nc.tensor.matmul(s, qT[p0:p1, kq, rows], kT[p0:p1, kk, 0:k1 - k0], start=True, stop=False)
                        if n < HEADS:
                            m = nc.tensor.matmul(s, slope_id[:, n, :], swa_dist[:, k0:k1], start=False, stop=True)
                        else:
                            hh = n - HEADS
                            for lohi in range(2):
                                nc.tensor.matmul(s, pick[:, hh, :], cum[:, lohi, 0:k1 - k0], start=False, stop=False)
                                for kb in range(k0, k1, P):
                                    nc.tensor.matmul(B[:, 4 + n % 2, kb:kb + P], cum[:, 2 + lohi, rows], pick[:, hh, :],
                                                     start=False, stop=False)
                            m = nc.tensor.matmul(s, identr[:, :], causal_r[:, k0:k1], start=False, stop=True)
                    m.then_inc(sem("scores_done"), 1)
                if 0 <= n - 2 < 16:
                    head_pt(n - 2)
                if 0 <= n - 3 < 16:
                    k = n - 3
                    if k < HEADS:
                        head_pv(k, va, HD * (k // 4))
                    else:
                        head_pv(k, vb, HD * (k - HEADS))
            pe.wait_ge(sem("aT_lo"), 8)
            for i in range(4):
                u = U_BR + 4 + i
                pe.wait_ge(lo_done, u + 1)
                unit_pair(u, sT_hi, sT_lo, 4 + 2 * (i % 2), ((4, 5), (6, 7))[i // 2], i % 2 == 0, i % 2 == 1)

            def half_rows(src, half):
                return lambda t, k: src[:, t, half * 512 + k * P:half * 512 + (k + 1) * P]

            pe.wait_ge(sem("mixed_done"), 2)
            transposes((2, 3), lambda t, k: nat[:, 0, t, k * P:(k + 1) * P], "wt_done")
            for half in range(2):
                for kp in range(4):
                    u = U_MO + 4 * half + kp
                    if half == 0:
                        pe.wait_ge(sem("wt_lo"), 4 + kp + 1)
                    elif kp == 0:
                        pe.wait_ge(sem("mixed_done"), 4)
                    pe.wait_ge(lo_done, u + 1)
                    unit_pair(u, xT_hi, xT_lo, 2 * kp, (4 + 2 * half, 5 + 2 * half), kp == 0, kp == 3)
                    if half == 0 and kp == 1:
                        pe.wait_ge(sem("mixed_done"), 4)
                        transposes((0, 1), lambda t, k: nat[:, 1, t, k * P:(k + 1) * P], "wt_done")
                    if half == 1 and kp == 1:
                        pe.wait_ge(sem("h_done"), 2)
                        transposes((2, 3), half_rows(h, 0), "wt_done")
            def hidden_T():
                transposes((2, 3), lambda t, k: nat[:, 1, t, k * P:(k + 1) * P], "hid_T")

            for kp in range(4):
                u = U_FF + kp
                pe.wait_ge(sem("wt_lo"), 8 + kp + 1)
                pe.wait_ge(lo_done, u + 1)
                unit_pair(u, sT_hi, sT_lo, 2 * kp, (0, 1), kp == 0, kp == 3)
                if kp == 1:
                    pe.wait_ge(sem("h_done"), 4)
                    transposes((4, 5), half_rows(h, 1), "wt_done")
            pe.wait_ge(sem("squared"), 2)
            hidden_T()
            acc = ((4, 5), (6, 7))
            for b in (4, 5, 6, 7):
                nc.tensor.matmul(B[:, b, :], zero_r[:, :], sT_hi[:, 0:2, :].rearrange("p k n -> p (k n)"), start=True, stop=False)
            with pe.Fori(1, FF_CHUNKS) as j:
                for r in range(4):
                    pe.wait_ge(lo_done, j * 8 + (U_FFL + r - 7))
                    unit_pair(U_FFL + r, sT_hi, sT_lo, 2 * r, (0, 1), r == 0, r == 3, 512)
                for r in range(4):
                    if r == 0:
                        pe.wait_ge(sem("hid_lo"), j * 2)
                    pe.wait_ge(lo_done, j * 8 + (U_FFL + r - 3))
                    unit_wide(U_FFL + 4 + r, xT_hi, xT_lo, r, acc, False, False)
                pe.wait_ge(sem("squared"), j * 2 + 2)
                hidden_T()
            pe.wait_ge(sem("p_in"), 16)
            transposes((0,), lambda t, k: p_sb[:, t, k * P:(k + 1) * P], "pT_done")
            for r in range(4):
                if r == 0:
                    pe.wait_ge(sem("hid_lo"), 2 * FF_CHUNKS)
                pe.wait_ge(lo_done, U_FFE + r + 1)
                unit_wide(U_FFE + r, xT_hi, xT_lo, r, acc, False, r == 3)
            pe.wait_ge(sem("pT_lo"), 1)
            for r in range(2):
                pe.wait_ge(lo_done, U_PP + r + 1)
                unit_wide(U_PP + r, xT_hi, xT_lo, 4 + r, ((0, 1), (2, 3)), r == 0, r == 1)
            pe.wait_ge(sem("h_done"), 7)
            transposes((4, 5), half_rows(h, 0), "wt_done")
            pe.wait_ge(sem("h_done"), 8)
            transposes((6, 7), half_rows(h, 1), "wt_done")
            for half in range(2):
                for kp in range(4):
                    u = U_PG + 4 * half + kp
                    if half == 0:
                        pe.wait_ge(sem("wt_lo"), 12 + max(kp + 1, 2))
                    pe.wait_ge(lo_done, u + 1)
                    unit_pair(u, sT_hi, sT_lo, 2 * kp, (4 + 2 * half, 5 + 2 * half), kp == 0, kp == 3)

            pe.wait_ge(sem("ada_used"), 4 * KT)
            pe.wait_ge(sem("pg_exp"), 4)
            for i, v in enumerate((0, 1, 3, 4)):
                for kt in range(KT):
                    m = nc.tensor.matmul(B[:, 4, 8 * i + kt:8 * i + kt + 1], ada_acc[:, v * D + kt * P:v * D + (kt + 1) * P], ones[:, 0:1],
                                         start=True, stop=True)
            m.then_inc(sem("ada_cols"), 1)
            pe.wait_ge(sem("gate_bias_in"), 32)
            for i in range(4):
                if i == 3:
                    pe.wait_ge(sem("h_done"), 12)
                g, c0 = i // 2, 512 * (i % 2)
                bank = B[:, (5, 6, 7, 0)[i], :]
                nc.tensor.matmul(bank, ones[:, :], ada_acc[:, (2, 5)[g] * D + c0:(2, 5)[g] * D + c0 + 512], start=True, stop=False)
                nc.tensor.matmul(bank, ones[0:1, :], gate_bias[0:1, g * D + c0:g * D + c0 + 512], start=False, stop=True)\
                    .then_inc(sem("gate_sum"), 1)
            pe.wait_ge(sem("normed"), 2)
            transposes((2, 3), lambda t, k: nat[:, 0, t, k * P:(k + 1) * P], "wt_done")
            pe.wait_ge(sem("mod_1"), 1)
            pe.wait_ge(sem("gate_b"), 4)
            pe.wait_ge(sem("normed"), 4)
            transposes((4, 5), lambda t, k: nat[:, 1, t, k * P:(k + 1) * P], "wt_done")
            NAT_T = {7: (4, (6, 7), 2), 11: (5, (6,), 1), 15: (6, (6, 7), 2), 19: (7, (6, 7), 2), 27: (8, (6, 7), 2), 31: (9, (6, 7), 2)}
            for q in range(60):
                u = U_IN2 + q
                c, kp = q // 4, q % 4
                if c == 0:
                    pe.wait_ge(sem("wt_lo"), 16 + kp + 1)
                elif kp == 0 and c >= 2:
                    pe.wait_ge(sem("evac"), 9 + c - 1)
                    if c in (11, 12):
                        pe.wait_ge(sem("gr_done"), 2 * (c - 10))
                pe.wait_ge(lo_done, u + 1)
                unit_pair(u, xT_hi, xT_lo, 2 * kp, (2 * (c % 2), 2 * (c % 2) + 1), kp == 0, kp == 3)
                if q in NAT_T:
                    k, banks, nk = NAT_T[q]
                    pe.wait_ge(sem("roped"), k - 3)
                    pe.wait_ge(sem("natT_copied"), k)
                    transposes(banks, lambda t, kk: nat[:, k % 2, t, kk * P:(kk + 1) * P], "natT_bank", nk)
                if 13 <= q < 21:
                    i = q - 13
                    if i == 0:
                        pe.wait_ge(sem("natT_copied"), 6)
                    if i >= 2:
                        pe.wait_ge(sem("index_relu"), i - 1)
                    p0 = 64 * (i % 2)
                    for t, (k0, k1) in enumerate(TILE_KEYS):
                        m = nc.tensor.matmul(B[:, 4 + i % 2, k0:k1], iqT[p0:p0 + 64, i // 2, t * P:(t + 1) * P],
                                             ikT[p0:p0 + 64, 0, 0:k1 - k0], start=True, stop=True)
                    m.then_inc(sem("index_done"), 1)
                if 33 <= q < 41:
                    n = q - 17
                    if n == 16:
                        pe.wait_ge(sem("selected"), 1)
                        pe.wait_ge(sem("index_relu"), HEADS)
                        pe.wait_ge(sem("natT_copied"), 8)
                    else:
                        pe.wait_ge(sem("exp_done"), n - 1)
                    p0, p1, kq = head_slices(n)
                    for t, (k0, k1) in enumerate(TILE_KEYS):
                        s = B[:, 4 + n % 2, k0:k1]
                        nc.tensor.matmul(s, qsT[p0:p1, kq, t * P:(t + 1) * P], ksT[p0:p1, kq, 0:k1 - k0], start=True, stop=False)
                        m = nc.tensor.matmul(s, identr[:, :], selected[:, k0:k1], start=False, stop=True)
                    m.then_inc(sem("scores_done"), 1)
                if 35 <= q < 43:
                    if q == 35:
                        pe.wait_ge(sem("natT_copied"), 10)
                    head_pt(q - 19)
                if 36 <= q < 44:
                    head_pv(q - 20, vs, HD * (q - 36))
                if q >= 44 and (q - 44) % 3 == 0 and (q - 44) // 3 < R_HEADS:
                    i = (q - 44) // 3
                    pe.wait_ge(sem("exp_done"), 24)
                    if i >= 2:
                        pe.wait_ge(sem("decayed"), i - 1)
                    nc.tensor.matmul(B[:, 4 + i % 2, 0:SEQ], krT[:, i, 0:P], qrT[:, i, :], start=True, stop=True)
                    nc.tensor.matmul(B[:, 4 + i % 2, SEQ:KEYS], krT[:, i, P:SEQ], qrT[:, i, P:SEQ], start=True, stop=True)\
                        .then_inc(sem("kq_done"), 1)
                if q >= 46 and (q - 46) % 3 == 0 and (q - 46) // 3 < R_HEADS:
                    i = (q - 46) // 3
                    pe.wait_ge(sem("decayed"), i + 1)
                    if i == 0:
                        pe.wait_ge(sem("aT_lo"), 12)
                    if i >= 2:
                        pe.wait_ge(sem("og_done"), i - 1)
                    o = B[:, 6 + i % 2, :]
                    v0, v1 = vr[:, 0, i * R_DV:(i + 1) * R_DV], vr[:, 1, i * R_DV:(i + 1) * R_DV]
                    w = prob[:, i % 2, :]
                    nc.tensor.matmul(o[:, 0:R_DV], w[:, 0:P], v0, start=True, stop=True)
                    nc.tensor.matmul(o[:, R_DV:2 * R_DV], w[:, P:SEQ], v0, start=True, stop=False)
                    nc.tensor.matmul(o[:, R_DV:2 * R_DV], w[:, SEQ:KEYS], v1, start=False, stop=True).then_inc(sem("av_done"), 1)
            pe.wait_ge(sem("decayed"), R_HEADS)
            pe.wait_ge(sem("y_gated"), 2 * R_HEADS)
            transposes((4, 5), half_rows(gr, 0), "wt_done")
            pe.wait_ge(sem("gn_half"), 1)
            transposes((6, 7), half_rows(gr, 1), "wt_done")
            for i in range(4):
                u = U_BR2 + i
                if i % 2 == 0:
                    pe.wait_ge(sem("evac"), 23 + i // 2)
                pe.wait_ge(lo_done, u + 1)
                unit_pair(u, sT_hi, sT_lo, 2 * (i % 2), ((2, 3), (0, 1))[i // 2], i % 2 == 0, i % 2 == 1)
            for i in range(8):
                u = U_RP + i
                kp = i % 4
                pe.wait_ge(sem("wt_lo"), 24 if i == 4 else 20 + max(kp + 1, 2))
                pe.wait_ge(lo_done, u + 1)
                unit_pair(u, xT_hi, xT_lo, 2 * kp, ((4, 5), (6, 7))[i // 4], kp == 0, kp == 3)
            pe.wait_ge(sem("mixed_done"), 6)
            transposes((2, 3), lambda t, k: nat[:, 0, t, k * P:(k + 1) * P], "wt_done")
            for half in range(2):
                for kp in range(4):
                    u = U_WO + 4 * half + kp
                    if half == 0:
                        pe.wait_ge(sem("wt_lo"), 24 + kp + 1)
                    pe.wait_ge(lo_done, u + 1)
                    unit_pair(u, sT_hi, sT_lo, 2 * kp, (4 + 2 * half, 5 + 2 * half), kp == 0, kp == 3)
                    if half == 0 and kp == 1:
                        pe.wait_ge(sem("mixed_done"), 8)
                        transposes((0, 1), lambda t, k: nat[:, 1, t, k * P:(k + 1) * P], "wt_done")
            pe.wait_ge(sem("normed"), 6)
            transposes((2, 3), lambda t, k: nat[:, 0, t, k * P:(k + 1) * P], "wt_done")
            pe.wait_ge(sem("normed"), 8)
            transposes((4, 5), lambda t, k: nat[:, 1, t, k * P:(k + 1) * P], "wt_done")

            def ffn_T(par):
                for kk in range(2):
                    for t in range(TILES):
                        m = nc.tensor.transpose(B[:, 2 + par, kk * SEQ + t * P:kk * SEQ + (t + 1) * P],
                                                ffn_hid[:, par, t * 256 + kk * P:t * 256 + (kk + 1) * P], ident)
                m.then_inc(sem("ffn_T"), 1)

            for kp in range(4):
                pe.wait_ge(sem("wt_lo"), 28 + kp + 1)
                pe.wait_ge(lo_done, U_FN + kp + 1)
                unit_pair(U_FN + kp, xT_hi, xT_lo, 2 * kp, (0, 1), kp == 0, kp == 3)
            for b in (4, 5, 6, 7):
                nc.tensor.matmul(B[:, b, :], zero_r[:, :], xT_hi[:, 0:2, :].rearrange("p k n -> p (k n)"), start=True, stop=False)
            pe.wait_ge(sem("ffn_hid"), 1)
            ffn_T(0)
            with pe.Fori(0, (FN_CHUNKS - 1) // 2) as i:
                for half in range(2):
                    for e in range(6):
                        u = U_FNL + 6 * half + e
                        if e == 4:
                            pe.wait_ge(sem("ffn_lo"), i * 2 + (half + 1))
                        pe.wait_ge(lo_done, i * 12 + (u + 1))
                        if e < 4:
                            unit_pair(u, xT_hi, xT_lo, 2 * e, (0, 1), e == 0, e == 3, 512)
                        else:
                            unit_wide(u, sT_hi, sT_lo, 2 * half + e - 4, acc, False, False)
                    pe.wait_ge(sem("ffn_hid"), i * 2 + (half + 2))
                    ffn_T(1 - half)
            pe.wait_ge(sem("ffn_lo"), FN_CHUNKS)
            for e in range(2):
                pe.wait_ge(lo_done, U_FNE + e + 1)
                unit_wide(U_FNE + e, sT_hi, sT_lo, e, acc, False, e == 1)


_INS = ["x", "p", "g_mix", "w_in", "b_forget", "swa_sinks", "w_br_swa", "w_br_fox", "w_mix_out", "g_mlp", "w_ff1", "w_ff2",
        "g_ple", "w_ple_gate", "w_ple_proj", "g_final", "c_2", "w_ada_2", "b_ada_2", "norm1_w_2", "w_in_2", "w_attn_proj_2",
        "w_ret_proj_2", "gn_w_2", "w_out_2", "norm2_w_2", "w_ffn_gate_2", "w_ffn_up_2", "w_ffn_down_2", "final_norm_w_2"]


def kernel(**inputs):
    import concourse.bacc as bacc
    from concourse.bass_utils import run_bass_kernel_spmd

    nc = bacc.Bacc("TRN2", target_bir_lowering=False, num_devices=1)
    arrays, args = {}, []

    def give(name, a):
        arrays[f"in_{name}_dram"] = a
        args.append(nc.dram_tensor(f"in_{name}_dram", a.shape, F32, kind="ExternalInput").ap())

    for name in _INS:
        give(name, np.ascontiguousarray(inputs[name]))
    tables, decay = constants()
    give("tables", tables)
    give("decay", decay)
    args.append(nc.dram_tensor("out_0_dram", (1, SEQ, D), F32, kind="ExternalOutput").ap())
    build(nc, *args)
    return run_bass_kernel_spmd(nc, [arrays], core_ids=[0]).results[0]["out_0_dram"]
```

```python
from contextlib import ExitStack

import numpy as np

import concourse.bass as bass
from concourse import mybir

P = 128
F32 = mybir.dt.float32
F32R = mybir.dt.float32r
BF16 = mybir.dt.bfloat16
ALU = mybir.AluOpType
ACT = mybir.ActivationFunctionType
AX = mybir.AxisListType

SEQ = 256
TILES = SEQ // P
D = 1024
KT = D // P
HD = 64
HEADS = 8
EPS = 1e-6
BIG = 1e30
LO_ROW = 64
TAKEN = -3e38
FAR = float(2.0 ** 100)
D_FF = 4096
D_FF_2 = 2816
R_HEADS = 4
R_DK = 128
R_DV = 256
TOPK = 64
KEYS = P + SEQ
TILE_KEYS = [(0, P), (P, KEYS)]

RAW = 8
SPLIT = 4
AHEAD = 3
FFN_RAW = 6
FFN_AHEAD = 2
SQUARE = [(half, kp) for k0 in (0, 2) for half in (0, 1) for kp in (k0, k0 + 1)]

V_GMIX, V_GMLP, V_GPLE, V_NORM1, V_NORM2, V_GN, V_BADA, V_C = 0, 8, 16, 24, 32, 40, 48, 96
V_ROWS = 104

C_IDENT = 0
C_SWA = 128
C_CAUSAL = C_SWA + KEYS
C_UPPER = C_CAUSAL + KEYS
C_COS_A = C_UPPER + P
C_SIN_A = C_COS_A + 16
C_COS_R = C_SIN_A + 16
C_SIN_R = C_COS_R + P
C_COLS = C_SIN_R + P


def constants():
    q = np.arange(P)[:, None]
    c = np.zeros((P, C_COLS), np.float32)
    c[:, C_IDENT:C_IDENT + P] = np.eye(P)
    for t, (k0, k1) in enumerate(TILE_KEYS):
        k = np.arange(k1 - k0)[None, :]
        a = q + t * P
        chunk = a // 64 - k // 64
        c[:, C_SWA + k0:C_SWA + k1] = np.where((chunk >= 0) & (chunk <= 2), np.abs(a - k), FAR)
        c[:, C_CAUSAL + k0:C_CAUSAL + k1] = np.where(k <= a, 0.0, BIG)
    c[:, C_UPPER:C_UPPER + P] = q <= np.arange(P)[None, :]
    for dim, theta, c0, s0 in ((16, 500000.0, C_COS_A, C_SIN_A), (R_DK, 10000.0, C_COS_R, C_SIN_R)):
        inv = (np.float32(1.0) / (np.float32(theta) ** (np.arange(0, dim, 2, dtype=np.float32) / np.float32(dim)))).astype(np.float32)
        ang = np.arange(SEQ, dtype=np.float32)[:, None] * inv[None, :]
        h = dim // 2
        for t in range(TILES):
            c[:, c0 + t * h:c0 + (t + 1) * h] = np.cos(ang[t * P:(t + 1) * P])
            c[:, s0 + t * h:s0 + (t + 1) * h] = np.sin(ang[t * P:(t + 1) * P])
    decay = np.zeros((P, R_HEADS, KEYS), np.float64)
    for h in range(R_HEADS):
        log_g = np.log(1.0 - 2.0 ** (-5.0 - h))
        i0 = np.arange(SEQ)[None, :] - q
        decay[:, h, :SEQ] = np.where(i0 >= 0, np.exp(log_g * np.maximum(i0, 0)), 0.0)
        i1 = np.arange(P)[None, :] - q
        decay[:, h, SEQ:] = np.where(i1 >= 0, np.exp(log_g * np.maximum(i1, 0)), 0.0)
    decay = (decay * R_DK ** -0.5).astype(np.float32).reshape(P, R_HEADS * KEYS)
    return c, decay


SIGNALS = {
    "ident_in": "identity", "consts_in": "the other constants", "x_in0": "x, first half of the columns", "x_in1": "x, second half",
    "g_mix_in": "g_mix's rows", "vectors_in": "the other vectors' rows", "sinks_in": "sinks", "forget_in": "forget gates' bias",
    "g_row_in": "g_final", "grow2_in": "final_norm_w_2", "p_in": "p", "decay_in": "decay tables", "gate_bias_in": "gates' part of b_ada",
    "ada_in0": "w_ada piece 0", "ada_in1": "w_ada piece 1", "ada_in2": "w_ada piece 2", "ada_in3": "w_ada piece 3",
    "ada_rows_in": "the modulation's rows, 128 columns a partition", "stored": "parts of the output written",
    "hi_done": "ACT: units' upper halves", "lo_done": "DVE: units' lower halves, the raw slot is free",
    "units_used": "PE: units' products done, the split slot is free", "last_first_tile": "PE: first tile of rows of a stage's last unit",
    "vec_T": "PE: vectors as columns", "vec_done": "ACT: their copies", "ones": "DVE: ones", "zeros": "DVE: zeros under the one-row table",
    "lf_zero": "DVE: zeros under the forget logs", "tables": "DVE: float32r tables", "nsink": "DVE: minus the sinks",
    "neg_half": "Pool: exponent -1/2", "dve_chain": "DVE: results that its next instruction reads",
    "wt_done": "PE: banks transposed", "wt_hi": "ACT: their upper halves", "wt_lo": "DVE: their lower halves, the bank is free",
    "affine": "DVE: modulated contraction tiles", "affine_lo": "DVE: lower halves of modulated pairs",
    "squares": "ACT: sums of squares", "ms_done": "DVE: mean squares", "rstd_done": "Pool: rstd", "rstd_id": "DVE: diag(rstd), a tile of rows each",
    "half_done": "DVE: rstd / 2", "nr8_done": "DVE: -rstd / 8", "h_done": "DVE: quarters of the residual",
    "hg_done": "DVE: quarters of residual * g_final", "y_ready": "DVE: the blocks' outputs (2, then 4)",
    "evac": "ACT: chunks out of their banks", "roped": "DVE: chunks rotated", "natT_bank": "PE: banks of transposed q, k",
    "natT_copied": "DVE: chunks of transposed q, k copied",
    "f_logit": "DVE: logits", "f_act": "ACT: steps of ln(1 + exp(-|f|))", "log_f": "DVE: log of the gates",
    "cum_done": "PE: cumulative sums", "cum_hi": "ACT: their upper halves", "cum_lo": "DVE: their lower halves",
    "scores_done": "PE: minus scores", "rmin_done": "DVE: row minima", "exp_done": "ACT: exponentials", "probs_done": "DVE: probabilities",
    "pt_done": "PE: probabilities transposed", "pt_copied": "ACT: their copy", "pv_done": "PE: heads' outputs",
    "aT_hi": "ACT: pairs of heads, upper halves", "aT_lo": "DVE: pairs of heads, lower halves",
    "index_done": "PE: index heads' products", "index_relu": "ACT: their relu", "index_sum": "DVE: heads added", "selected": "DVE: mask of the selected keys",
    "kq_done": "PE: keys by queries", "decayed": "DVE: times the decay", "av_done": "PE: heads' outputs", "gvar": "DVE: variance + eps",
    "grstd": "Pool: rstd of the group norm", "gshift": "DVE: -mean * rstd", "og_done": "ACT: normed heads", "y_gated": "DVE: gated heads' tiles",
    "gr_done": "DVE: silu gates' tiles", "gn_half": "DVE: group norm's weight / 2",
    "gated": "DVE: branches times their gates", "mixed_done": "DVE: merged halves' tiles",
    "relu": "ACT: relu tiles", "squared": "ACT: squared tiles", "hid_T": "PE: banks of transposed hidden units", "hid_hi": "ACT: upper halves",
    "hid_lo": "DVE: lower halves", "pT_done": "PE: p transposed", "pT_hi": "ACT: upper half", "pT_lo": "DVE: lower half",
    "pp0_done": "ACT: bank 0 of p's projection copied", "pg_exp": "ACT: tanh of the embedding's gate",
    "c_tanh": "ACT: tanh(c / 2)", "silu_now": "DVE: this tile's silu(c)", "ada_used": "DVE: pieces of w_ada summed",
    "gate_bias_added": "Pool: gates' bias", "ada_hi": "ACT: sums' upper halves", "ada_lo": "DVE: sums' lower halves",
    "ada_rows": "PE: a norm's shift and scale summed over the partitions", "ada_rows_out": "ACT: their copy", "ada_cols": "PE: as columns",
    "mod_1": "DVE: columns of the first norm", "mod_2": "DVE: columns of the second norm", "gate_sum": "PE: gates' rows", "gate_b": "ACT: their copies",
    "ffn_tanh": "ACT: tanh(gate / 2)", "ffn_silu": "DVE: twice silu", "ffn_hid": "DVE: twice the hidden units", "ffn_T": "PE: transposed",
    "ffn_hi": "ACT: upper halves", "ffn_lo": "DVE: lower halves", "ffn_out": "PE: the output's banks",
}


class Stream:

    def __init__(self):
        self.slot, self.landed, self.loads = [], [], []
        self.count = [0] * RAW

    def add(self, loads, slot=None):
        u = len(self.slot)
        s = u % RAW if slot is None else slot
        self.count[s] += 16 * len(loads)
        self.slot.append(s)
        self.landed.append(self.count[s])
        self.loads.append(loads)
        return u

    def previous(self, u):
        for v in range(u - 1, -1, -1):
            if self.slot[v] == self.slot[u]:
                return v
        return None


def build(nc, x, p, g_mix, w_in, b_forget, swa_sinks, w_br_swa, w_br_fox, w_mix_out, g_mlp, w_ff1, w_ff2,
          g_ple, w_ple_gate, w_ple_proj, g_final, c_2, w_ada_2, b_ada_2, norm1_w_2, w_in_2, w_attn_proj_2,
          w_ret_proj_2, gn_w_2, w_out_2, norm2_w_2, w_ffn_gate_2, w_ffn_up_2, w_ffn_down_2, final_norm_w_2,
          consts, decay_dram, out):

    def pair(w, kp, c0, n):
        return w.rearrange("(k p) n -> p k n", p=P)[:, 2 * kp:2 * kp + 2, c0:c0 + n]

    def wide(w, kt):
        return w.rearrange("(k p) (h n) -> p k h n", p=P, n=512)[:, kt, :, :]

    w_in1, ff1, ff2 = w_in[0], w_ff1[0], w_ff2[0]
    st = Stream()
    CH1 = [(264, [(0, 512, 256), (256, 2304, 8)]), (512, [(0, 0, 512)]), (512, [(0, 768, 512)]),
           (512, [(0, 1280, 512)]), (512, [(0, 1792, 512)])] + [(512, [(0, 2312 + 512 * i, 512)]) for i in range(4)]
    for _, parts in CH1:
        for kp in range(4):
            st.add([(d, n, pair(w_in1, kp, c, n)) for d, c, n in parts])
    U_BR = len(st.slot)
    for w in (w_br_swa[0], w_br_fox[0]):
        for half in range(2):
            for kp in range(2):
                st.add([(0, 512, pair(w, kp, 512 * half, 512))])
    U_MO = len(st.slot)
    for half, kp in SQUARE:
        st.add([(0, 512, pair(w_mix_out[0], kp, 512 * half, 512))])
    U_FF = len(st.slot)
    for kp in range(4):
        st.add([(0, 512, pair(ff1, kp, 0, 512))])
    U_FFL = len(st.slot)
    FF_CHUNKS = D_FF // 512
    for j in range(1, FF_CHUNKS):
        for kp in range(4):
            st.add([(0, 512, pair(ff1, kp, 512 * j, 512))])
        for kk in range(4):
            st.add([(0, 512, wide(ff2, 4 * (j - 1) + kk))])
    U_FFE = len(st.slot)
    for kk in range(4):
        st.add([(0, 512, wide(ff2, 4 * (FF_CHUNKS - 1) + kk))])
    U_PP = len(st.slot)
    for kk in range(2):
        st.add([(0, 512, wide(w_ple_proj[0], kk))])
    U_PG = len(st.slot)
    for half in range(2):
        for kp in range(4):
            st.add([(0, 512, pair(w_ple_gate[0], kp, 512 * half, 512))])
    U_IN2 = len(st.slot)
    CH2 = [(512, 1536), (72, 2048), (512, 0), (512, 512), (512, 1024)] + [(512, 2120 + 512 * i) for i in range(10)]
    for n, c in CH2:
        for kp in range(4):
            st.add([(0, n, pair(w_in_2, kp, c, n))])
    U_BR2 = len(st.slot)
    for half in range(2):
        for kp in range(2):
            st.add([(0, 512, pair(w_attn_proj_2, kp, 512 * half, 512))])
    U_RP = len(st.slot)
    for half in range(2):
        for kp in range(4):
            st.add([(0, 512, pair(w_ret_proj_2, kp, 512 * half, 512))])
    U_WO = len(st.slot)
    for half, kp in SQUARE:
        st.add([(0, 512, pair(w_out_2, kp, 512 * half, 512))])
    U_FN = len(st.slot)
    FN_CHUNKS = D_FF_2 // 256

    def fn_slot():
        return (len(st.slot) - U_FN) % FFN_RAW

    for j in range(FN_CHUNKS + 1):
        if j < FN_CHUNKS:
            for kp in range(4):
                st.add([(0, 256, pair(w_ffn_gate_2, kp, 256 * j, 256)), (256, 256, pair(w_ffn_up_2, kp, 256 * j, 256))],
                       fn_slot())
        if j:
            for kk in range(2):
                src = wide(w_ffn_down_2, 2 * (j - 1) + kk)
                st.add([(0, 512, src)] if j < FN_CHUNKS else [(d, 256, src[:, :, d:d + 256]) for d in (0, 256)], fn_slot())
    U_END = len(st.slot)
    U_FNL = U_FN + 4
    U_FNE = U_END - 2
    for u in range(U_FN, U_FN + FFN_RAW):
        assert st.previous(u) <= u - FFN_RAW
    assert U_FFL % RAW == 0 and 12 % SPLIT == 0

    with ExitStack() as ctx:
        def sb(name, shape, dt=F32):
            return ctx.enter_context(nc.sbuf_tensor(name, shape, dt))

        sems = {name: ctx.enter_context(nc.semaphore(name)) for name in SIGNALS}

        def sem(name):
            return sems[name]

        raw = sb("raw", [P, RAW, 2, 512])
        w_hi = sb("w_hi", [P, SPLIT, 2, 512], F32R)
        w_lo = sb("w_lo", [P, SPLIT, 2, 512], F32R)
        xT_hi = sb("xT_hi", [P, KT, SEQ], F32R)
        xT_lo = sb("xT_lo", [P, KT, SEQ], F32R)
        sT_hi = sb("sT_hi", [P, KT, SEQ], F32R)
        sT_lo = sb("sT_lo", [P, KT, SEQ], F32R)
        h = sb("h", [P, TILES, D])
        nat = sb("nat", [P, 2, TILES, 512])
        junk = sb("junk", [P, 512], BF16)
        cst = sb("cst", [P, C_COLS])
        zero_r = sb("zero_r", [P, P], F32R)
        identr = sb("identr", [P, P], F32R)
        slope_id = sb("slope_id", [P, HEADS, P], F32R)
        rstd_id = sb("rstd_id", [P, TILES, P])
        swa_dist = sb("swa_dist", [P, KEYS], F32R)
        causal_r = sb("causal_r", [P, KEYS], F32R)
        one_row = sb("one_row", [P, 16], F32R)
        pick = sb("pick", [LO_ROW + HEADS, HEADS, P], F32R)
        cum = sb("cum", [LO_ROW + HEADS, 2, SEQ], F32R)
        ones_r = sb("ones_r", [P, P], F32R)
        vrows = sb("vrows", [P, P])
        vec = sb("vec", [P, V_ROWS])
        small = sb("small", [P, 768])
        gate_b = sb("gate_b", [P, 2, D])
        Z = sb("Z", [P, 15360])

        ones = ones_r[:, :].bitcast(F32)
        ident = cst[:, C_IDENT:C_IDENT + P]
        causal = cst[:, C_CAUSAL:C_CAUSAL + KEYS]
        upper = cst[:, C_UPPER:C_UPPER + P]

        at = [0]

        def sm(n):
            at[0] += n
            assert at[0] <= 768
            return small[:, at[0] - n:at[0]]

        rstd = sm(14).rearrange("p (k t) -> p k t", t=2)
        ms = sm(14).rearrange("p (k t) -> p k t", t=2)
        sq = sm(28).rearrange("p (k i t) -> p k i t", i=2, t=2)
        nr8 = sm(2)
        neg_half = sm(8).rearrange("p (k t) -> p k t", t=2)
        half_rstd = sm(4).rearrange("p (k t) -> p k t", t=2)
        sink = sm(8)
        nsink = sm(8)
        bf = sm(8)
        rmin = sm(48).rearrange("p (n t) -> p n t", t=2)
        psum_e = sm(48).rearrange("p (n t) -> p n t", t=2)
        rden = sm(48).rearrange("p (n t) -> p n t", t=2)
        esink = sm(16).rearrange("p (n t) -> p n t", t=2)
        fz = sm(16).rearrange("p (t n) -> p t n", t=2)
        fa = sm(16).rearrange("p (t n) -> p t n", t=2)
        lf = sm(2 * (LO_ROW + HEADS)).rearrange("p (t n) -> p t n", t=2)
        silu_c = sm(8)
        silu_now = sm(1)
        ctmp = sm(8)
        ada_col = sm(32)
        iw = sm(16).rearrange("p (t n) -> p t n", t=2)
        top8 = sm(16).rearrange("p (t n) -> p t n", t=2)
        gate_a1 = sm(8)
        gate_a2 = sm(8)
        bns = sm(48).rearrange("p (r t s) -> p r t s", r=4, t=2)
        mv = sm(16).rearrange("p (r t s) -> p r t s", r=4, t=2)
        gvar = sm(8).rearrange("p (r t) -> p r t", r=4)
        grstd = sm(8).rearrange("p (r t) -> p r t", r=4)
        gshift = sm(8).rearrange("p (r t) -> p r t", r=4)

        def z(c0, *dims):
            n = int(np.prod(dims))
            assert c0 + n <= Z.shape[1]
            v = Z[:, c0:c0 + n]
            if len(dims) == 2:
                v = v.rearrange("p (a b) -> p a b", a=dims[0])
            if len(dims) == 3:
                v = v.rearrange("p (a b c) -> p a b c", a=dims[0], b=dims[1])
            return v

        prob = z(0, 2, KEYS)
        probT = z(768, 2, KEYS)
        qaT = z(1536, 4, SEQ)
        kaT = z(2560, 2, SEQ)
        va = z(3072, TILES, P)
        qbT = z(3328, 4, SEQ)
        kbT = z(4352, 4, SEQ)
        vb = z(5376, TILES, 512)
        gates = z(6400, TILES, 2, D)
        ada_acc = z(0, 6 * D)
        ada_raw = z(6 * D, 4, 1536)
        p_sb = z(6 * D + 6144, TILES, SEQ)
        pg = z(8 * D, TILES, D)
        g_row = z(12800, D)

        pp0 = z(6 * D, 512)
        ada_rows = z(6 * D + 512, 512)[0:8, :]
        ada_hi, ada_lo = (v[:, :, :].rearrange("p k n -> p (k n)") for v in (xT_hi, xT_lo))
        ADA_PARTS = [((0, 0, 2 * D),), ((0, 3 * D, 2 * D),), ((0, 2 * D, D), (D, 5 * D, D))]
        iqT = z(1536, 4, SEQ)
        ikT = z(2560, 1, SEQ)
        score = z(2816, KEYS)
        work = z(3200, KEYS)
        decay = z(1536, R_HEADS, KEYS)
        qsT = z(3584, 4, SEQ)
        ksT = z(4608, 4, SEQ)
        vs = z(5632, TILES, 512)
        qrT = z(6656, 4, SEQ)
        krT = z(7680, 4, SEQ)
        vr = z(8704, TILES, D)
        gr = z(10752, TILES, D)
        gates2 = {(0, 0): z(3584, TILES, 512), (0, 1): z(4608, TILES, 512), (1, 0): z(5632, TILES, 512), (1, 1): z(12800, TILES, 512)}
        temp = z(13824, 3, 512)
        grow2 = z(10752, D)
        ffn_gate = z(0, 2, 2 * 256)
        ffn_hid = z(1024, 2, 2 * 256)
        selected = swa_dist

        B = ctx.enter_context(nc.psum_tensor("B", [P, 8, 512], F32))

        landed = [ctx.enter_context(nc.semaphore(f"landed{i}")) for i in range(RAW)]
        hi_done, lo_done, units_used = sem("hi_done"), sem("lo_done"), sem("units_used")
        block = ctx.enter_context(nc.Block())

        def spans(u):
            return max(d + n for d, n, _ in st.loads[u])

        @block.sync
        def _(sp):
            def load(u):
                prev = st.previous(u)
                if prev is not None:
                    sp.wait_ge(lo_done, prev + 1)
                for d, n, src in st.loads[u]:
                    sp.dma_start(raw[:, st.slot[u], :, d:d + n], src).then_inc(landed[st.slot[u]], 16)

            sp.dma_start(cst[:, C_IDENT:C_IDENT + P], consts[:, C_IDENT:C_IDENT + P]).then_inc(sem("ident_in"), 16)
            for half in range(2):
                for t in range(TILES):
                    sp.dma_start(h[:, t, 512 * half:512 * half + 512], x[0, t * P:(t + 1) * P, 512 * half:512 * half + 512]).then_inc(sem(f"x_in{half}"), 16)
            for u in range(4):
                load(u)
            sp.dma_start(cst[:, P:], consts[:, P:]).then_inc(sem("consts_in"), 16)
            for i, v in enumerate((g_mlp[0], g_ple[0], norm1_w_2, norm2_w_2, gn_w_2)):
                sp.dma_start(vrows[8 * i + 8:8 * i + 16, :], v.rearrange("(k p) -> k p", p=P)).then_inc(sem("vectors_in"), 16)
            sp.dma_start(vrows[V_BADA:V_BADA + 48, :], b_ada_2.rearrange("(k p) -> k p", p=P)).then_inc(sem("vectors_in"), 16)
            sp.dma_start(vrows[V_C:V_C + 8, :], c_2[0].rearrange("(k p) -> k p", p=P)).then_inc(sem("vectors_in"), 16)
            for u in range(4, U_FFL):
                load(u)
            with sp.Fori(1, FF_CHUNKS) as j:
                for r in range(8):
                    sp.wait_ge(lo_done, j * 8 + (U_FFL + r - RAW - 7))
                    if r < 4:
                        src = ff1.rearrange("(k p) n -> p k n", p=P)[:, 2 * r:2 * r + 2, bass.ds(j * 512, 512)]
                    else:
                        src = ff2.rearrange("(k p) (h n) -> p k h n", p=P, n=512)[:, bass.ds(j * 4 + (r - 8), 1), :, :].rearrange("p k h n -> p (k h) n")
                    sp.dma_start(raw[:, st.slot[U_FFL + r], :, :], src).then_inc(landed[st.slot[U_FFL + r]], 16)
            for u in range(U_FFE, U_FNL):
                load(u)
            with sp.Fori(0, (FN_CHUNKS - 1) // 2) as i:
                for q in range(12):
                    u = U_FNL + q
                    j0, e = 1 + q // 6, q % 6
                    sp.wait_ge(lo_done, i * 12 + (u - FFN_RAW + 1))
                    if e < 4:
                        for d, w in ((0, w_ffn_gate_2), (256, w_ffn_up_2)):
                            src = w.rearrange("(k p) n -> p k n", p=P)[:, 2 * e:2 * e + 2, bass.ds(i * 512 + 256 * j0, 256)]
                            sp.dma_start(raw[:, st.slot[u], :, d:d + 256], src).then_inc(landed[st.slot[u]], 16)
                    else:
                        src = w_ffn_down_2.rearrange("(k p) (h n) -> p k h n", p=P, n=512)[
                            :, bass.ds(i * 4 + (2 * (j0 - 1) + e - 4), 1), :, :].rearrange("p k h n -> p (k h) n")
                        sp.dma_start(raw[:, st.slot[u], :, :], src).then_inc(landed[st.slot[u]], 16)
            for u in range(U_FNE, U_END):
                load(u)
            for t in range(TILES):
                for half in range(2):
                    sp.wait_ge(sem("y_ready"), TILES + 2 * t + half + 1)
                    sp.dma_start(out[0, t * P:(t + 1) * P, 512 * half:512 * half + 512],
                                 h[:, t, 512 * half:512 * half + 512]).then_inc(sem("stored"), 16)
            sp.wait_ge(sem("stored"), 64)

        @block.gpsimd
        def _(pool):
            pool.dma_start(vrows[0:8, :], g_mix[0].rearrange("(k p) -> k p", p=P)).then_inc(sem("g_mix_in"), 16)
            pool.dma_start(sink, swa_sinks.partition_broadcast(P).rearrange("p a n -> p (a n)")).then_inc(sem("sinks_in"), 16)
            pool.dma_start(bf, b_forget.partition_broadcast(P).rearrange("p a n -> p (a n)")).then_inc(sem("forget_in"), 16)

            roots = [0]

            def root(k, n=1, t0=0, t1=TILES):
                roots[0] += 1
                pool.wait_ge(sem("ms_done"), roots[0])
                nc.gpsimd.tensor_tensor(rstd[:, k:k + n, t0:t1], ms[:, k:k + n, t0:t1], neg_half[:, :, t0:t1][:, 0:n], ALU.pow)\
                    .then_inc(sem("rstd_done"), 1)

            nc.gpsimd.memset(neg_half, -0.5).then_inc(sem("neg_half"), 1)
            pool.wait_ge(sem("neg_half"), 1)
            root(0)
            pool.dma_start(g_row, g_final[None, :].partition_broadcast(P).rearrange("p a n -> p (a n)")).then_inc(sem("g_row_in"), 16)
            for i, v in enumerate((2, 5)):
                pool.dma_start(gate_b[0:1, i, :], b_ada_2[None, v * D:(v + 1) * D]).then_inc(sem("gate_bias_in"), 16)
            pool.wait_ge(sem("mixed_done"), 4)
            pool.dma_start(p_sb, p[0, 0].rearrange("(t p) n -> p t n", p=P)).then_inc(sem("p_in"), 16)
            wa = w_ada_2.rearrange("(k p) n -> p k n", p=P)
            for q in range(4):
                pool.dma_start(ada_raw[:, q, :], wa[:, 0, 1536 * q:1536 * (q + 1)]).then_inc(sem(f"ada_in{q}"), 16)
            root(1)
            with pool.Fori(1, KT) as kt:
                for q in range(4):
                    pool.wait_ge(sem("ada_used"), kt * 4 + (q - 3))
                    pool.dma_start(ada_raw[:, q, :], wa[:, bass.ds(kt, 1), 1536 * q:1536 * (q + 1)].rearrange("p k n -> p (k n)")).then_inc(sem(f"ada_in{q}"), 16)
            pool.wait_ge(sem("ada_used"), 4 * KT)
            pool.wait_ge(sem("gate_bias_in"), 32)
            for i, v in enumerate((2, 5)):
                part = ada_acc[0:1, v * D:(v + 1) * D]
                nc.gpsimd.tensor_tensor(part, part, gate_b[0:1, i, :], ALU.add).then_inc(sem("gate_bias_added"), 1)
            root(2)
            pool.wait_ge(sem("ada_rows_out"), 1)
            pool.dma_start(vrows[0:32, :], ada_rows.rearrange("r (k n) -> r k n", n=P)).then_inc(sem("ada_rows_in"), 16)
            root(3, 2)
            pool.wait_ge(sem("selected"), 1)
            pool.dma_start(decay.rearrange("p r n -> p (r n)"), decay_dram).then_inc(sem("decay_in"), 16)
            for i in range(R_HEADS):
                pool.wait_ge(sem("gvar"), i + 1)
                nc.gpsimd.tensor_tensor(grstd[:, i, :], gvar[:, i, :], neg_half[:, 0, :], ALU.pow).then_inc(sem("grstd"), 1)
            pool.wait_ge(sem("mixed_done"), 8)
            pool.dma_start(grow2, final_norm_w_2[None, :].partition_broadcast(P).rearrange("p a n -> p (a n)")).then_inc(sem("grow2_in"), 16)
            root(5)
            for t in range(TILES):
                root(6, 1, t, t + 1)

        @block.scalar
        def _(act):
            done = [0]

            def split_hi(u, n, landed_at, used_at):
                act.wait_ge(landed[st.slot[u]], landed_at)
                if used_at is not None:
                    act.wait_ge(units_used, used_at)
                nc.scalar.activation(w_hi[:, u % SPLIT, :, 0:n], raw[:, st.slot[u], :, 0:n], ACT.Copy).then_inc(hi_done, 1)

            def split_to(u_last):
                for u in range(done[0], u_last + 1):
                    split_hi(u, spans(u), st.landed[u], u - SPLIT + 1 if u >= SPLIT else None)
                done[0] = max(done[0], u_last + 1)

            wt = [0]

            def wide_hi(banks, dst, kt0, scale=None, bias=None):
                for i, b in enumerate(banks):
                    act.wait_ge(sem("wt_done"), wt[0] + 1)
                    for kk in range(2):
                        kt = kt0 + 2 * i + kk
                        src = B[:, b, kk * SEQ:(kk + 1) * SEQ]
                        if scale is None:
                            if kk == 0:
                                last = nc.scalar.activation(dst[:, kt:kt + 2, :], B[:, b, :].rearrange("p (k n) -> p k n", k=2), ACT.Copy)
                        elif bias is None:
                            last = nc.scalar.activation(dst[:, kt, :], src, ACT.Copy, scale=vec[:, scale + kt:scale + kt + 1])
                        else:
                            last = nc.scalar.activation(dst[:, kt, :], src, ACT.Identity, scale=scale[:, kt:kt + 1], bias=bias[:, kt:kt + 1])
                    last.then_inc(sem("wt_hi"), 1)
                    wt[0] += 1

            squared_so_far = [0]

            def squares(k, half, ready, count, src=None, tiles=range(TILES)):
                src = h if src is None else src
                for t in tiles:
                    if ready is not None:
                        act.wait_ge(ready, count + t)
                    if squared_so_far[0]:
                        act.wait_ge(sem("squares"), squared_so_far[0])
                    nc.scalar.activation(junk[:, :], src[:, t, 512 * half:512 * half + 512], ACT.Square, scale=D ** -0.5,
                                         accum_out=sq[:, k, half, t:t + 1]).then_inc(sem("squares"), 1)
                    squared_so_far[0] += 1

            def head_exp(n, swa):
                act.wait_ge(sem("rmin_done"), n + 1)
                if n >= 2:
                    act.wait_ge(sem("pt_done"), n - 1)
                for t, (k0, k1) in enumerate(TILE_KEYS):
                    last = nc.scalar.activation(prob[:, n % 2, k0:k1], B[:, 4 + n % 2, k0:k1], ACT.Exp, scale=-1.0,
                                                bias=rmin[:, n, t:t + 1], accum_out=psum_e[:, n, t:t + 1])
                if swa:
                    last = nc.scalar.activation(esink[:, n, :], rmin[:, n, :], ACT.Exp, bias=sink[:, n:n + 1])
                last.then_inc(sem("exp_done"), 1)

            def head_pt(n):
                act.wait_ge(sem("pt_done"), n + 1)
                if n >= 2:
                    act.wait_ge(sem("pv_done"), n - 1)
                nc.scalar.activation(probT[:, n % 2, :], B[:, 6, 0:KEYS], ACT.Copy).then_inc(sem("pt_copied"), 1)

            def head_out_hi(m, kt):
                act.wait_ge(sem("pv_done"), 2 * m + 2)
                nc.scalar.activation(sT_hi[:, kt, :], B[:, 7, (m % 2) * SEQ:(m % 2 + 1) * SEQ], ACT.Copy).then_inc(sem("aT_hi"), 1)

            def to_nat(k, t, src, scale, dst=None):
                return nc.scalar.activation(nat[:, k % 2, t, 0:512] if dst is None else dst, src, ACT.Copy, scale=scale)

            act.wait_ge(sem("vec_T"), 1)
            nc.scalar.activation(vec[:, 0:8], B[:, 7, 0:8], ACT.Copy).then_inc(sem("vec_done"), 1)
            act.wait_ge(sem("vec_done"), 1)
            wide_hi((0, 1), xT_hi, 0, V_GMIX)
            split_to(0)
            wide_hi((2, 3), xT_hi, 4, V_GMIX)
            split_to(3)
            for half in range(2):
                squares(0, half, None, 0)
            act.wait_ge(sem("nr8_done"), 1)
            split_to(AHEAD + 3)
            act.wait_ge(sem("vec_T"), 2)
            nc.scalar.activation(vec[:, 8:], B[:, 7, 8:V_ROWS], ACT.Copy).then_inc(sem("vec_done"), 1)
            act.wait_ge(units_used, 4)
            for t in range(TILES):
                r = rstd[:, 0, t:t + 1]
                for dup in range(2):
                    to_nat(0, t, B[:, t, 0:P].rearrange("p (g d) -> p g d", g=2), r,
                           nat[:, 0, t, 0:2 * P].rearrange("p (g u d) -> p g u d", g=2, u=2)[:, :, dup, :])
                to_nat(0, t, B[:, t, P:2 * P], r, va[:, t, :])
                last = to_nat(0, t, B[:, t, 2 * P:2 * P + 8], r, fz[:, t, :])
            last.then_inc(sem("evac"), 1)
            for c in range(1, 5):
                split_to(4 * c + 3 + AHEAD)
                act.wait_ge(units_used, 4 * c + 4)
                if 2 <= c < 4:
                    act.wait_ge(sem("natT_bank"), 2 * c - 3)
                for t in range(TILES):
                    bank = B[:, 2 * (c % 2) + t, :]
                    r = rstd[:, 0, t:t + 1]
                    if c == 4:
                        last = to_nat(c, t, bank, r, vb[:, t, :])
                    else:
                        last = to_nat(c, t, bank, nr8[:, t:t + 1] if c < 3 else r)
                last.then_inc(sem("evac"), 1)
                if c == 1:
                    act.wait_ge(sem("f_logit"), 1)
                    nc.scalar.activation(fa, fz, ACT.Abs).then_inc(sem("f_act"), 1)
                    act.wait_ge(sem("f_act"), 1)
                    nc.scalar.activation(fa, fa, ACT.Exp, scale=-1.0).then_inc(sem("f_act"), 1)
                    act.wait_ge(sem("f_act"), 2)
                    nc.scalar.activation(fa, fa, ACT.Ln, bias=1.0).then_inc(sem("f_act"), 1)
                if c == 3:
                    act.wait_ge(sem("cum_done"), 1)
                    nc.scalar.activation(cum[:, 0, :], B[0:LO_ROW + HEADS, 7, 0:SEQ], ACT.Copy)
                    nc.scalar.activation(cum[:, 1, :], B[0:LO_ROW + HEADS, 7, 0:SEQ], ACT.Copy, scale=-1.0).then_inc(sem("cum_hi"), 1)
            for n in range(2 * HEADS + 4):
                u = 20 + n
                split_to(u + AHEAD)
                if n < 16 and n % 4 == 3:
                    c = 5 + n // 4
                    act.wait_ge(units_used, u + 1)
                    for t in range(TILES):
                        g = n // 4
                        last = nc.scalar.activation(gates[:, t, g // 2, 512 * (g % 2):512 * (g % 2) + 512], B[:, 2 * (c % 2) + t, :],
                                                    ACT.Tanh, scale=half_rstd[:, 0, t:t + 1])
                    last.then_inc(sem("evac"), 1)
                if n < 16:
                    head_exp(n, n < HEADS)
                if 0 <= n - 2 < 16:
                    head_pt(n - 2)
                if 4 <= n < 20 and n % 2 == 0:
                    head_out_hi(n // 2 - 2, n // 2 - 2)
            split_to(U_MO + 1)
            wide_hi((2, 3), xT_hi, 0)
            split_to(U_MO + 1 + AHEAD)
            wide_hi((0, 1), xT_hi, 4)
            split_to(U_MO + 6 + AHEAD)
            wide_hi((2, 3), sT_hi, 0, V_GMLP)
            split_to(U_MO + 7 + AHEAD)
            nc.scalar.activation(ctmp, vec[:, V_C:V_C + 8], ACT.Tanh, scale=0.5).then_inc(sem("c_tanh"), 1)
            split_to(U_FF + AHEAD)
            wide_hi((4, 5), sT_hi, 4, V_GMLP)
            for half in range(2):
                squares(1, half, sem("h_done"), 2 * half + 1)
            split_to(U_FF + 1 + AHEAD)

            def relu2(j_done):
                for t in range(TILES):
                    nc.scalar.activation(nat[:, 0, t, :], B[:, t, :], ACT.Relu, scale=rstd[:, 1, t:t + 1]).then_inc(sem("relu"), 1)
                act.wait_ge(sem("relu"), j_done)
                for t in range(TILES):
                    nc.scalar.activation(nat[:, 1, t, :], nat[:, 0, t, :], ACT.Square).then_inc(sem("squared"), 1)

            def hidden_hi(banks=(0, 1)):
                for i in banks:
                    b = 2 + i
                    nc.scalar.activation(xT_hi[:, 2 * i:2 * i + 2, :], B[:, b, :].rearrange("p (k n) -> p k n", k=2),
                                         ACT.Copy).then_inc(sem("hid_hi"), 1)

            split_to(U_FF + 3 + AHEAD)
            act.wait_ge(sem("rstd_done"), 2)
            act.wait_ge(units_used, U_FF + 4)
            relu2(2)
            act.wait_ge(sem("hid_T"), 2)
            hidden_hi()
            with act.Fori(1, FF_CHUNKS) as j:
                def loop_split(r):
                    u = U_FFL + r
                    act.wait_ge(landed[st.slot[u]], j * 16 + (st.landed[u] - 16))
                    act.wait_ge(units_used, j * 8 + (u - SPLIT - 7))
                    nc.scalar.activation(w_hi[:, u % SPLIT, :, :], raw[:, st.slot[u], :, :], ACT.Copy).then_inc(hi_done, 1)

                for r in range(AHEAD, 7):
                    loop_split(r)
                act.wait_ge(units_used, j * 8 + (U_FFL - 4))
                relu2(j * 2 + 2)
                for r in range(7, 7 + AHEAD):
                    loop_split(r)
                act.wait_ge(sem("hid_T"), j * 2 + 1)
                hidden_hi((0,))
                loop_split(7 + AHEAD)
                act.wait_ge(sem("hid_T"), j * 2 + 2)
                act.wait_ge(units_used, j * 8 + U_FFL)
                hidden_hi((1,))
            done[0] = U_FFE + AHEAD
            split_to(U_FFE + AHEAD)
            act.wait_ge(sem("pT_done"), 1)
            nc.scalar.activation(xT_hi[:, 4:6, :], B[:, 0, :].rearrange("p (k n) -> p k n", k=2), ACT.Copy).then_inc(sem("pT_hi"), 1)
            split_to(U_FFE + 3 + AHEAD)
            wide_hi((4, 5), sT_hi, 0, V_GPLE)
            split_to(U_PG + 2)
            wide_hi((6, 7), sT_hi, 4, V_GPLE)
            act.wait_ge(units_used, U_PP + 2)
            nc.scalar.activation(pp0, B[:, 0, :], ACT.Copy).then_inc(sem("pp0_done"), 1)
            act.wait_ge(sem("ada_used"), 4 * KT)

            def ada_upper(i):
                for c, v, n in ADA_PARTS[i]:
                    nc.scalar.activation(ada_hi[:, c:c + n], ada_acc[:, v:v + n], ACT.Copy).then_inc(sem("ada_hi"), 1)

            def ple_gate(half):
                if half == 0:
                    act.wait_ge(units_used, U_PG + 4)
                for t in range(TILES):
                    if half and t == 0:
                        act.wait_ge(sem("last_first_tile"), 2)
                    elif half:
                        act.wait_ge(units_used, U_PG + 8)
                    nc.scalar.activation(pg[:, t, 512 * half:512 * half + 512], B[:, 4 + 2 * half + t, :], ACT.Tanh,
                                         scale=half_rstd[:, 1, t:t + 1]).then_inc(sem("pg_exp"), 1)

            ada_upper(0)
            split_to(U_PG + 3)
            for half in range(2):
                squares(2, half, sem("h_done"), 2 * half + 5)
            split_to(U_PG + 5)
            act.wait_ge(sem("ada_rows"), 1)
            ada_upper(1)
            act.wait_ge(sem("half_done"), 2)
            ple_gate(0)
            split_to(U_PG + 7)
            act.wait_ge(sem("ada_rows"), 2)
            nc.scalar.activation(ada_rows, B[0:8, 0, :], ACT.Copy).then_inc(sem("ada_rows_out"), 1)
            act.wait_ge(sem("gate_bias_added"), 2)
            ada_upper(2)
            squares(3, 0, sem("h_done"), 9)
            squares(4, 0, sem("hg_done"), 1, pg)
            ple_gate(1)
            split_to(U_IN2)
            for t in range(TILES):
                squares(3, 1, sem("h_done"), 11, tiles=(t,))
                squares(4, 1, sem("hg_done"), 3, pg, tiles=(t,))
            split_to(U_IN2 + 1)
            def gate_rows(i):
                act.wait_ge(sem("gate_sum"), i + 1)
                nc.scalar.activation(gate_b[:, i // 2, 512 * (i % 2):512 * (i % 2) + 512], B[:, 4 + i, :], ACT.Copy,
                                     scale=0.5).then_inc(sem("gate_b"), 1)

            gate_rows(0)
            gate_rows(1)
            act.wait_ge(sem("mod_1"), 1)
            wide_hi((2, 3), xT_hi, 0, gate_a1, ada_col[:, 0:8])
            split_to(U_IN2 + 2)
            wide_hi((4, 5), xT_hi, 4, gate_a1, ada_col[:, 0:8])
            split_to(U_IN2 + AHEAD)
            gate_rows(2)
            gate_rows(3)
            act.wait_ge(sem("y_ready"), TILES)

            for q in range(60):
                u = U_IN2 + q
                split_to(u + AHEAD)
                c = q // 4
                if q % 4 == 3:
                    act.wait_ge(units_used, u + 1)
                    if c in (2, 3, 5, 6):
                        act.wait_ge(sem("natT_bank"), {2: 9, 3: 10, 5: 12, 6: 14}[c])
                    for t in range(TILES):
                        bank = B[:, 2 * (c % 2) + t, :]
                        if c == 1:
                            for dup in range(2):
                                to_nat(1, t, bank[:, 0:HD], 1.0, nat[:, 1, t, dup * HD:(dup + 1) * HD])
                            last = to_nat(1, t, bank[:, HD:HD + 8], HEADS ** -0.5, iw[:, t, :])
                        elif c in (0, 2, 3, 5, 6):
                            last = to_nat((0, 1, 0, 1, 0, 0, 1)[c], t, bank, {0: HD ** -0.5, 2: -HD ** -0.5}.get(c, 1.0))
                        elif c == 4:
                            last = to_nat(0, t, bank, 1.0, vs[:, t, :])
                        elif c in (7, 8):
                            last = to_nat(0, t, bank, 1.0, vr[:, t, 512 * (c - 7):512 * (c - 6)])
                        elif c in (9, 10):
                            last = nc.scalar.activation(gr[:, t, 512 * (c - 9):512 * (c - 8)], bank, ACT.Tanh, scale=0.5)
                        else:
                            if c == 11 and t == 0:
                                act.wait_ge(sem("aT_lo"), 12)
                            last = nc.scalar.activation(gates2[(c - 11) // 2, (c - 11) % 2][:, t, :], bank, ACT.Tanh, scale=0.5)
                    last.then_inc(sem("evac"), 1)
                if 13 <= q < 21:
                    i = q - 13
                    act.wait_ge(sem("index_done"), i + 1)
                    if i >= 2:
                        act.wait_ge(sem("index_sum"), i - 1)
                    nc.scalar.activation(prob[:, i % 2, :], B[:, 4 + i % 2, 0:KEYS], ACT.Relu).then_inc(sem("index_relu"), 1)
                if 33 <= q < 41:
                    head_exp(q - 17, False)
                if 35 <= q < 43:
                    head_pt(q - 19)
                if q in (37, 39, 41, 43):
                    head_out_hi((q - 37) // 2 + 8, (q - 37) // 2)
                if q >= 47 and (q - 47) % 3 == 0 and (q - 47) // 3 < R_HEADS:
                    i = (q - 47) // 3
                    act.wait_ge(sem("gshift"), i + 1)
                    if i >= 2:
                        act.wait_ge(sem("y_gated"), 2 * i - 2)
                    for t in range(TILES):
                        last = nc.scalar.activation(nat[:, i % 2, t, 0:R_DV], B[:, 6 + i % 2, t * R_DV:(t + 1) * R_DV], ACT.Identity,
                                                    scale=grstd[:, i, t:t + 1], bias=gshift[:, i, t:t + 1])
                    last.then_inc(sem("og_done"), 1)
            wide_hi((4, 5), xT_hi, 0, V_GN)
            wide_hi((6, 7), xT_hi, 4, V_GN)
            split_to(U_WO)
            wide_hi((2, 3), sT_hi, 0)
            split_to(U_WO + 1 + AHEAD)
            wide_hi((0, 1), sT_hi, 4)
            split_to(U_WO + 5 + AHEAD)
            squares(5, 0, sem("h_done"), 13)
            split_to(U_WO + 7)
            squares(5, 1, sem("h_done"), 15)
            split_to(U_FN + 1)
            act.wait_ge(sem("mod_2"), 1)
            wide_hi((2, 3), xT_hi, 0, gate_a2, ada_col[:, 16:24])
            wide_hi((4, 5), xT_hi, 4, gate_a2, ada_col[:, 16:24])

            def ffn_hi(par, count):
                act.wait_ge(sem("ffn_T"), count)
                nc.scalar.activation(sT_hi[:, 2 * par:2 * par + 2, :], B[:, 2 + par, :].rearrange("p (k n) -> p k n", k=2),
                                     ACT.Copy).then_inc(sem("ffn_hi"), 1)

            def ffn_tanh(par):
                nc.scalar.activation(ffn_gate[:, par, :].rearrange("p (t n) -> p t n", t=2), B[:, 0:2, 0:256], ACT.Tanh,
                                     scale=0.5).then_inc(sem("ffn_tanh"), 1)

            split_to(U_FN + 3 + FFN_AHEAD)
            act.wait_ge(units_used, U_FN + 4)
            ffn_tanh(0)
            ffn_hi(0, 1)
            with act.Fori(0, (FN_CHUNKS - 1) // 2) as i:
                def ffn_split(q):
                    u = U_FNL + q
                    per = 64 if len(st.loads[u]) == 2 else 32
                    act.wait_ge(landed[st.slot[u]], i * per + st.landed[u])
                    act.wait_ge(units_used, i * 12 + (u - SPLIT + 1))
                    nc.scalar.activation(w_hi[:, u % SPLIT, :, :], raw[:, st.slot[u], :, :], ACT.Copy).then_inc(hi_done, 1)

                for half in range(2):
                    for q in range(FFN_AHEAD, 4 + FFN_AHEAD):
                        ffn_split(6 * half + q)
                    act.wait_ge(units_used, i * 12 + (U_FNL + 6 * half + 4))
                    ffn_tanh(1 - half)
                    for q in range(4 + FFN_AHEAD, 6 + FFN_AHEAD):
                        ffn_split(6 * half + q)
                    ffn_hi(1 - half, i * 2 + (half + 2))
            done[0] = U_FNE + FFN_AHEAD
            split_to(U_END - 1)
            for t in range(TILES):
                for half in range(2):
                    squares(6, half, sem("h_done"), 17 + t + half, tiles=(t,))

        @block.vector
        def _(dve):
            done = [0]
            chain = [0]

            def link(ins):
                chain[0] += 1
                ins.then_inc(sem("dve_chain"), 1)
                dve.wait_ge(sem("dve_chain"), chain[0])

            def split_to(u_last):
                for u in range(done[0], u_last + 1):
                    dve.wait_ge(hi_done, u + 1)
                    n = spans(u)
                    nc.vector.tensor_tensor(w_lo[:, u % SPLIT, :, 0:n], raw[:, st.slot[u], :, 0:n],
                                            w_hi[:, u % SPLIT, :, 0:n].bitcast(F32), ALU.subtract).then_inc(lo_done, 1)
                done[0] = max(done[0], u_last + 1)

            wt = [0]

            def wide_lo(banks, hi, lo, kt0, scale=None):
                for i, b in enumerate(banks):
                    dve.wait_ge(sem("wt_hi"), wt[0] + 1)
                    k = kt0 + 2 * i
                    if scale is None:
                        last = nc.vector.tensor_tensor(lo[:, k:k + 2, :], B[:, b, :].rearrange("p (k n) -> p k n", k=2),
                                                       hi[:, k:k + 2, :].bitcast(F32), ALU.subtract)
                    else:
                        for kt in (k, k + 1):
                            last = nc.vector.scalar_tensor_tensor(lo[:, kt, :], B[:, b, (kt - k) * SEQ:(kt - k + 1) * SEQ],
                                                                  vec[:, scale + kt:scale + kt + 1], hi[:, kt, :].bitcast(F32),
                                                                  ALU.mult, ALU.subtract)
                    last.then_inc(sem("wt_lo"), 1)
                    wt[0] += 1

            def mean_square(k, count):
                dve.wait_ge(sem("squares"), count)
                return nc.vector.scalar_tensor_tensor(ms[:, k, :], sq[:, k, 0, :], EPS, sq[:, k, 1, :], ALU.add, ALU.add)

            def copy_T(k, dst, banks, n):
                for i, b in enumerate(banks):
                    dve.wait_ge(sem("natT_bank"), natb[0] + 1)
                    last = nc.vector.tensor_copy(dst[:, 2 * i:2 * i + n, :], B[:, b, 0:n * SEQ].rearrange("p (k n) -> p k n", k=n))
                    natb[0] += 1
                last.then_inc(sem("natT_copied"), 1)

            natb = [0]

            def head_min(n, swa):
                dve.wait_ge(sem("scores_done"), n + 1)
                for t, (k0, k1) in enumerate(TILE_KEYS):
                    last = nc.vector.tensor_reduce(rmin[:, n, t:t + 1], B[:, 4 + n % 2, k0:k1], AX.X, ALU.min)
                if swa:
                    link(last)
                    last = nc.vector.tensor_scalar(rmin[:, n, :], rmin[:, n, :], nsink[:, n:n + 1], None, ALU.min)
                last.then_inc(sem("rmin_done"), 1)

            def head_norm(n, swa):
                dve.wait_ge(sem("exp_done"), n + 1)
                if swa:
                    link(nc.vector.tensor_tensor(psum_e[:, n, :], psum_e[:, n, :], esink[:, n, :], ALU.add))
                link(nc.vector.reciprocal(rden[:, n, :], psum_e[:, n, :]))
                for t, (k0, k1) in enumerate(TILE_KEYS):
                    last = nc.vector.tensor_scalar(prob[:, n % 2, k0:k1], prob[:, n % 2, k0:k1], rden[:, n, t:t + 1], None, ALU.mult)
                last.then_inc(sem("probs_done"), 1)

            def head_out_lo(m, kt):
                dve.wait_ge(sem("aT_hi"), m + 1)
                nc.vector.tensor_tensor(sT_lo[:, kt, :], B[:, 7, (m % 2) * SEQ:(m % 2 + 1) * SEQ],
                                        sT_hi[:, kt, :].bitcast(F32), ALU.subtract).then_inc(sem("aT_lo"), 1)

            nc.vector.memset(zero_r[:, :].bitcast(F32), 0.0)
            nc.vector.memset(one_row[:, :].bitcast(F32), 0.0).then_inc(sem("zeros"), 1)
            dve.wait_ge(sem("zeros"), 1)
            nc.vector.memset(one_row[:, 7:8].bitcast(F32), 1.0)
            nc.vector.memset(lf, 0.0).then_inc(sem("lf_zero"), 1)
            nc.vector.memset(ones, 1.0).then_inc(sem("ones"), 1)
            dve.wait_ge(sem("vec_done"), 1)
            wide_lo((0, 1), xT_hi, xT_lo, 0, V_GMIX)
            split_to(0)
            wide_lo((2, 3), xT_hi, xT_lo, 4, V_GMIX)
            split_to(3)
            mean_square(0, 4).then_inc(sem("ms_done"), 1)
            dve.wait_ge(sem("rstd_done"), 1)
            nc.vector.tensor_scalar(half_rstd[:, 0, :], rstd[:, 0, :], 0.5, None, ALU.mult).then_inc(sem("half_done"), 1)
            nc.vector.tensor_scalar(nr8, rstd[:, 0, :], -HD ** -0.5, None, ALU.mult).then_inc(sem("nr8_done"), 1)
            split_to(AHEAD + 2)
            dve.wait_ge(sem("consts_in"), 16)
            nc.vector.tensor_copy(identr[:, :], ident)
            nc.vector.tensor_copy(swa_dist[:, :], cst[:, C_SWA:C_SWA + KEYS])
            nc.vector.tensor_copy(causal_r[:, :], causal)
            split_to(AHEAD + 3)
            for i in range(HEADS):
                nc.vector.tensor_scalar(slope_id[:, i, :], ident, 2.0 ** -(i + 1), None, ALU.mult)
                nc.vector.tensor_copy(pick[0:LO_ROW, i, :], cst[0:LO_ROW, C_IDENT + i:C_IDENT + i + 1].to_broadcast([LO_ROW, P]))
                low = C_IDENT + LO_ROW + i
                last = nc.vector.tensor_copy(pick[LO_ROW:LO_ROW + HEADS, i, :], cst[LO_ROW:LO_ROW + HEADS, low:low + 1].to_broadcast([HEADS, P]))
            last.then_inc(sem("tables"), 1)
            dve.wait_ge(sem("sinks_in"), 16)
            nc.vector.tensor_scalar(nsink, sink, -1.0, None, ALU.mult).then_inc(sem("nsink"), 1)
            dve.wait_ge(sem("nsink"), 1)
            dve.wait_ge(sem("forget_in"), 16)
            dve.wait_ge(sem("evac"), 1)
            for t in range(TILES):
                last = nc.vector.tensor_tensor(fz[:, t, :], fz[:, t, :], bf, ALU.add)
            last.then_inc(sem("f_logit"), 1)
            split_to(7 + AHEAD)
            copy_T(0, kaT, (4,), 2)
            dve.wait_ge(sem("f_act"), 3)
            dve.wait_ge(sem("lf_zero"), 1)
            for row in (0, LO_ROW):
                nc.vector.scalar_tensor_tensor(lf[:, :, row:row + HEADS], fz, 0.0, fa, ALU.min, ALU.subtract).then_inc(sem("log_f"), 1)
            for k, dst in ((1, qaT), (2, qbT), (3, kbT)):
                split_to(4 * k + 7 + AHEAD)
                copy_T(k, dst, (4, 5), 2)
                if k == 2:
                    dve.wait_ge(sem("cum_hi"), 1)
                    low = slice(LO_ROW, LO_ROW + HEADS)
                    link(nc.vector.tensor_tensor(cum[low, 0, :], B[low, 7, 0:SEQ], cum[low, 0, :].bitcast(F32), ALU.subtract))
                    nc.vector.tensor_scalar(cum[low, 1, :], cum[low, 0, :].bitcast(F32), -1.0, None, ALU.mult).then_inc(sem("cum_lo"), 1)
            for n in range(2 * HEADS + 4):
                split_to(20 + n + AHEAD)
                if n < 16:
                    head_min(n, n < HEADS)
                if 0 <= n - 1 < 16:
                    head_norm(n - 1, n - 1 < HEADS)
                if n >= 4 and n % 2 == 0 and n < 20:
                    head_out_lo(n // 2 - 2, n // 2 - 2)

            def gate_branch(g, half, bank):
                for t in range(TILES):
                    v = gates[:, t, g, 512 * half:512 * half + 512]
                    nc.vector.scalar_tensor_tensor(v, v, 1.0, B[:, bank + t, :], ALU.add, ALU.mult).then_inc(sem("gated"), 1)

            def merge(half, count):
                for t in range(TILES):
                    dve.wait_ge(sem("gated"), count + t + 1)
                    nc.vector.tensor_tensor(nat[:, half, t, :], gates[:, t, 0, 512 * half:512 * half + 512],
                                            gates[:, t, 1, 512 * half:512 * half + 512], ALU.add).then_inc(sem("mixed_done"), 1)

            def add_h(t, half, bank, factor=1.0):
                v = h[:, t, 512 * half:512 * half + 512]
                nc.vector.scalar_tensor_tensor(v, B[:, bank, :], factor, v, ALU.mult, ALU.add).then_inc(sem("h_done"), 1)

            dve.wait_ge(sem("evac"), 9)
            dve.wait_ge(units_used, U_BR + 2)
            gate_branch(0, 0, 2)
            dve.wait_ge(units_used, U_BR + 4)
            gate_branch(0, 1, 0)
            split_to(U_MO)
            dve.wait_ge(units_used, U_BR + 6)
            gate_branch(1, 0, 4)
            merge(0, 4)
            split_to(U_MO + 1)
            wide_lo((2, 3), xT_hi, xT_lo, 0)
            dve.wait_ge(units_used, U_BR + 8)
            gate_branch(1, 1, 6)
            split_to(U_MO + 2)
            merge(1, 6)
            split_to(U_MO + 1 + AHEAD)
            wide_lo((0, 1), xT_hi, xT_lo, 4)
            split_to(U_MO + 5 + AHEAD)
            dve.wait_ge(units_used, U_MO + 6)
            for t in range(TILES):
                add_h(t, 0, 4 + t, 0.5)
            split_to(U_MO + 6 + AHEAD)
            wide_lo((2, 3), sT_hi, sT_lo, 0, V_GMLP)
            split_to(U_MO + 7 + AHEAD)
            dve.wait_ge(sem("last_first_tile"), 1)
            add_h(0, 1, 6, 0.5)
            dve.wait_ge(units_used, U_MO + 8)
            add_h(1, 1, 7, 0.5)
            dve.wait_ge(sem("c_tanh"), 1)
            link(nc.vector.tensor_scalar(ctmp, ctmp, 0.5, 0.5, ALU.mult, ALU.add))
            link(nc.vector.tensor_tensor(silu_c, ctmp, vec[:, V_C:V_C + 8], ALU.mult))
            split_to(U_FF + AHEAD)
            wide_lo((4, 5), sT_hi, sT_lo, 4, V_GMLP)
            mean_square(1, 8).then_inc(sem("ms_done"), 1)
            split_to(U_FF + 1 + AHEAD)
            split_to(U_FF + 3 + AHEAD)
            for q in range(4):
                dve.wait_ge(sem(f"ada_in{q}"), 16)
                nc.vector.tensor_scalar(ada_acc[:, 1536 * q:1536 * (q + 1)], ada_raw[:, q, :], silu_c[:, 0:1], None,
                                        ALU.mult).then_inc(sem("ada_used"), 1)

            def hidden_lo(i, count):
                    b = 2 + i
                    dve.wait_ge(sem("hid_hi"), count)
                    nc.vector.tensor_tensor(xT_lo[:, 2 * i:2 * i + 2, :], B[:, b, :].rearrange("p (k n) -> p k n", k=2),
                                            xT_hi[:, 2 * i:2 * i + 2, :].bitcast(F32), ALU.subtract).then_inc(sem("hid_lo"), 1)

            hidden_lo(0, 1)
            hidden_lo(1, 2)
            with dve.Fori(1, FF_CHUNKS) as j:
                dve.wait_ge(sem("ada_used"), j * 4)
                nc.vector.tensor_copy(silu_now, silu_c[:, bass.ds(j, 1)]).then_inc(sem("silu_now"), 1)
                dve.wait_ge(sem("silu_now"), j)
                for r in range(AHEAD, 8 + AHEAD):
                    u = U_FFL + r
                    dve.wait_ge(hi_done, j * 8 + (u - 7))
                    nc.vector.tensor_tensor(w_lo[:, u % SPLIT, :, :], raw[:, st.slot[u], :, :],
                                            w_hi[:, u % SPLIT, :, :].bitcast(F32), ALU.subtract).then_inc(lo_done, 1)
                    if r >= 7 + AHEAD - 1:
                        hidden_lo(r - 9, j * 2 + (r - 8))
                    if r % 2 == 0:
                        q = r // 2 - 2
                        dve.wait_ge(sem(f"ada_in{q}"), j * 16 + 16)
                        dve.wait_ge(sem("ada_used"), j * 4 + (q - 3))
                        nc.vector.scalar_tensor_tensor(ada_acc[:, 1536 * q:1536 * (q + 1)], ada_raw[:, q, :], silu_now,
                                                       ada_acc[:, 1536 * q:1536 * (q + 1)], ALU.mult, ALU.add).then_inc(sem("ada_used"), 1)
            done[0] = U_FFE + AHEAD
            split_to(U_FFE + AHEAD)
            dve.wait_ge(sem("pT_hi"), 1)
            nc.vector.tensor_tensor(xT_lo[:, 4:6, :], B[:, 0, :].rearrange("p (k n) -> p k n", k=2), xT_hi[:, 4:6, :].bitcast(F32),
                                    ALU.subtract).then_inc(sem("pT_lo"), 1)
            split_to(U_FFE + 3 + AHEAD)
            dve.wait_ge(units_used, U_FFE + 4)
            for t in range(TILES):
                add_h(t, 0, 4 + t)
            for t in range(TILES):
                add_h(t, 1, 6 + t)
            wide_lo((4, 5), sT_hi, sT_lo, 0, V_GPLE)
            split_to(U_PG + 2)
            wide_lo((6, 7), sT_hi, sT_lo, 4, V_GPLE)
            dve.wait_ge(sem("g_row_in"), 16)
            ada_parts = [0]

            def ada_lower(i):
                for c, v, n in ADA_PARTS[i]:
                    ada_parts[0] += 1
                    dve.wait_ge(sem("ada_hi"), ada_parts[0])
                    nc.vector.tensor_tensor(ada_lo[:, c:c + n], ada_acc[:, v:v + n], ada_hi[:, c:c + n].bitcast(F32),
                                            ALU.subtract).then_inc(sem("ada_lo"), 1)

            def add_ple(half, tiles):
                for t in tiles:
                    v = pg[:, t, 512 * half:512 * half + 512]
                    dve.wait_ge(sem("pg_exp"), 2 * half + t + 1)
                    link(nc.vector.scalar_tensor_tensor(v, v, 1.0, B[:, 2 * t + half, :] if t or half else pp0, ALU.add, ALU.mult))
                    hv = h[:, t, 512 * half:512 * half + 512]
                    nc.vector.scalar_tensor_tensor(hv, v, 0.5, hv, ALU.mult, ALU.add).then_inc(sem("h_done"), 1)
                    dve.wait_ge(sem("h_done"), 9 + 2 * half + t)
                    nc.vector.tensor_tensor(v, hv, g_row[:, 512 * half:512 * half + 512], ALU.mult).then_inc(sem("hg_done"), 1)

            ada_lower(0)
            split_to(U_PG + 3)
            mean_square(2, 12).then_inc(sem("ms_done"), 1)
            split_to(U_PG + 4)
            dve.wait_ge(sem("rstd_done"), 3)
            nc.vector.tensor_scalar(half_rstd[:, 1, :], rstd[:, 2, :], 0.5, None, ALU.mult).then_inc(sem("half_done"), 1)
            split_to(U_PG + 5)
            ada_lower(1)
            add_ple(0, (0,))
            split_to(U_PG + 6)
            add_ple(0, (1,))
            split_to(U_PG + 7)
            ada_lower(2)
            add_ple(1, (0, 1))
            link(mean_square(3, 20))
            link(nc.vector.tensor_tensor(ms[:, 4, :], sq[:, 4, 0, :], sq[:, 4, 1, :], ALU.add))
            nc.vector.scalar_tensor_tensor(ms[:, 4, :], ms[:, 3, :], EPS, ms[:, 4, :], ALU.mult, ALU.add).then_inc(sem("ms_done"), 1)

            def scaled_identity(k, roots):
                dve.wait_ge(sem("rstd_done"), roots)
                for t in range(TILES):
                    nc.vector.tensor_scalar(rstd_id[:, t, :], ident, rstd[:, k, t:t + 1], None, ALU.mult).then_inc(sem("rstd_id"), 1)

            def wide_lo_affine(banks, hi, lo, kt0, a, b, count):
                for i, bk in enumerate(banks):
                    dve.wait_ge(sem("wt_hi"), wt[0] + 1)
                    wt[0] += 1
                    k = kt0 + 2 * i
                    v = temp[:, (k // 2) % 2, :].rearrange("p (k n) -> p k n", k=2)
                    if count + k >= 4:
                        dve.wait_ge(sem("affine_lo"), (count + k) // 2 - 1)
                    for kk in range(2):
                        nc.vector.tensor_scalar(v[:, kk, :], B[:, bk, kk * SEQ:(kk + 1) * SEQ], a[:, k + kk:k + kk + 1],
                                                b[:, k + kk:k + kk + 1], ALU.mult, ALU.add).then_inc(sem("affine"), 1)
                    dve.wait_ge(sem("affine"), count + k + 2)
                    nc.vector.tensor_tensor(lo[:, k:k + 2, :], v, hi[:, k:k + 2, :].bitcast(F32), ALU.subtract).then_inc(sem("affine_lo"), 1)

            split_to(U_IN2)
            scaled_identity(4, 4)
            dve.wait_ge(sem("ada_cols"), 1)
            for i, v in enumerate((0, 3)):
                link(nc.vector.tensor_tensor(ada_col[:, 16 * i:16 * i + 16], B[:, 0, 16 * i:16 * i + 16],
                                             vec[:, V_BADA + 8 * v:V_BADA + 8 * v + 16], ALU.add))
                nc.vector.scalar_tensor_tensor((gate_a1, gate_a2)[i], ada_col[:, 16 * i + 8:16 * i + 16], 1.0,
                                               vec[:, (V_NORM1, V_NORM2)[i]:(V_NORM1, V_NORM2)[i] + 8], ALU.add, ALU.mult)\
                    .then_inc(sem(f"mod_{i + 1}"), 1)
            nc.vector.tensor_scalar(vec[:, V_GN:V_GN + 8], vec[:, V_GN:V_GN + 8], 0.5, None, ALU.mult).then_inc(sem("gn_half"), 1)
            dve.wait_ge(sem("mod_1"), 1)
            split_to(U_IN2 + 1)
            wide_lo_affine((2, 3), xT_hi, xT_lo, 0, gate_a1, ada_col[:, 0:8], 0)
            split_to(U_IN2 + 2)
            wide_lo_affine((4, 5), xT_hi, xT_lo, 4, gate_a1, ada_col[:, 0:8], 0)
            split_to(U_IN2 + AHEAD)
            for t in range(TILES):
                nc.vector.tensor_scalar(h[:, t, :], pg[:, t, :], rstd[:, 3, t:t + 1], None, ALU.mult).then_inc(sem("y_ready"), 1)

            def rotate(x1, x2, cos, sin, shape):
                n = int(np.prod(shape))
                names = dict(zip("abc", shape))
                v = [temp[:, i, 0:n].rearrange("p (a b c) -> p a b c", **names) for i in range(3)]
                nc.vector.tensor_tensor(v[0], x1, cos, ALU.mult)
                nc.vector.tensor_tensor(v[1], x2, sin, ALU.mult)
                link(nc.vector.tensor_tensor(v[2], x1, sin, ALU.mult))
                nc.vector.tensor_tensor(x1, v[0], v[1], ALU.subtract)
                link(nc.vector.tensor_tensor(x2, x2, cos, ALU.mult))
                nc.vector.tensor_tensor(x2, v[2], x2, ALU.add).then_inc(sem("roped"), 1)

            def rope(k, heads):
                v = nat[:, k % 2, :, 0:heads * HD].rearrange("p t (h d) -> p t h d", d=HD)
                tab = [cst[:, c:c + 16].rearrange("p (t d) -> p t d", t=2)[:, :, None, :].to_broadcast([P, 2, heads, 8]) for c in (C_COS_A, C_SIN_A)]
                rotate(v[:, :, :, 0:8], v[:, :, :, 8:16], *tab, (2, heads, 8))

            def rope_full(k):
                v = nat[:, k % 2, :, :].rearrange("p t (h d) -> p t h d", d=R_DK)
                tab = [cst[:, c:c + P].rearrange("p (t d) -> p t d", t=2)[:, :, None, :].to_broadcast([P, 2, R_HEADS, 64]) for c in (C_COS_R, C_SIN_R)]
                rotate(v[:, :, :, 0:64], v[:, :, :, 64:128], *tab, (2, R_HEADS, 64))

            TOP_ROUNDS = (21, 22, 23, 25, 26, 27, 29, 30)
            ROPE = {4: (4, HEADS), 8: (5, 2), 12: (6, HEADS), 16: (7, HEADS)}
            COPY = {8: (4, iqT, (6, 7), 2), 12: (5, ikT, (6,), 1), 16: (6, qsT, (6, 7), 2), 20: (7, ksT, (6, 7), 2),
                    28: (8, qrT, (6, 7), 2), 32: (9, krT, (6, 7), 2)}
            for q in range(60):
                u = U_IN2 + q
                split_to(u + AHEAD)
                c = q // 4
                if q in COPY:
                    copy_T(*COPY[q])
                if q in ROPE:
                    dve.wait_ge(sem("evac"), 9 + c)
                    rope(*ROPE[q])
                if q in (24, 28):
                    dve.wait_ge(sem("evac"), 9 + c)
                    rope_full(8 if q == 24 else 9)
                if 13 <= q < 21:
                    i = q - 13
                    if i == 0:
                        link(nc.vector.tensor_scalar(score, causal, -1.0, 0.0, ALU.mult, ALU.add))
                    else:
                        dve.wait_ge(sem("index_sum"), i)
                    dve.wait_ge(sem("index_relu"), i + 1)
                    for t, (k0, k1) in enumerate(TILE_KEYS):
                        last = nc.vector.scalar_tensor_tensor(score[:, k0:k1], prob[:, i % 2, k0:k1], iw[:, t, i:i + 1], score[:, k0:k1],
                                                              ALU.mult, ALU.add)
                    last.then_inc(sem("index_sum"), 1)
                if q in TOP_ROUNDS:
                    i = TOP_ROUNDS.index(q)
                    if i == 0:
                        dve.wait_ge(sem("index_sum"), HEADS)
                    src = work if i else score
                    for t, (k0, k1) in enumerate(TILE_KEYS):
                        last = nc.vector.max(top8[:, t, :], src[:, k0:k1])
                    link(last)
                    for t, (k0, k1) in enumerate(TILE_KEYS):
                        last = nc.vector.match_replace(work[:, k0:k1], top8[:, t, :], src[:, k0:k1], TAKEN)
                    link(last)
                if q == 31:
                    link(nc.vector.tensor_scalar(work, work, TAKEN / 2, BIG, ALU.is_gt, ALU.mult))
                    nc.vector.tensor_tensor(selected[:, :], work, causal, ALU.max).then_inc(sem("selected"), 1)
                if 33 <= q < 41:
                    head_min(q - 17, False)
                if 34 <= q < 42:
                    head_norm(q - 18, False)
                if q in (37, 39, 41, 43):
                    head_out_lo((q - 37) // 2 + 8, (q - 37) // 2)
                if q in (40, 44):
                    dve.wait_ge(sem("evac"), 9 + c)
                    for t in range(TILES):
                        v = gr[:, t, 512 * (c - 10):512 * (c - 9)]
                        nc.vector.scalar_tensor_tensor(v, v, 1.0, B[:, 2 * ((c - 1) % 2) + t, :], ALU.add, ALU.mult).then_inc(sem("gr_done"), 1)
                if q >= 44 and (q - 44) % 3 == 0 and (q - 44) // 3 < R_HEADS:
                    i = (q - 44) // 3
                    dve.wait_ge(sem("decay_in"), 16)
                    dve.wait_ge(sem("kq_done"), i + 1)
                    if i >= 2:
                        dve.wait_ge(sem("av_done"), i - 1)
                    nc.vector.tensor_tensor(prob[:, i % 2, :], B[:, 4 + i % 2, 0:KEYS], decay[:, i, :], ALU.mult).then_inc(sem("decayed"), 1)
                if q >= 46 and (q - 46) % 3 == 0 and (q - 46) // 3 < R_HEADS:
                    i = (q - 46) // 3
                    dve.wait_ge(sem("av_done"), i + 1)
                    for t in range(TILES):
                        last = nc.vector.bn_stats(bns[:, i, t, :], B[:, 6 + i % 2, t * R_DV:(t + 1) * R_DV])
                    link(last)
                    for t in range(TILES):
                        last = nc.vector.bn_aggr(mv[:, i, t, :], bns[:, i, t, :])
                    link(last)
                    nc.vector.tensor_scalar(gvar[:, i, :], mv[:, i, :, 1], EPS, None, ALU.add).then_inc(sem("gvar"), 1)
                if q >= 47 and (q - 47) % 3 == 0 and (q - 47) // 3 < R_HEADS:
                    i = (q - 47) // 3
                    dve.wait_ge(sem("grstd"), i + 1)
                    nc.vector.scalar_tensor_tensor(gshift[:, i, :], mv[:, i, :, 0], -1.0, grstd[:, i, :], ALU.mult, ALU.mult)\
                        .then_inc(sem("gshift"), 1)
                if q >= 48 and (q - 48) % 3 == 0 and (q - 48) // 3 < R_HEADS:
                    i = (q - 48) // 3
                    dve.wait_ge(sem("og_done"), i + 1)
                    for t in range(TILES):
                        v = gr[:, t, i * R_DV:(i + 1) * R_DV]
                        nc.vector.tensor_tensor(v, nat[:, i % 2, t, 0:R_DV], v, ALU.mult).then_inc(sem("y_gated"), 1)

            wide_lo((4, 5), xT_hi, xT_lo, 0, V_GN)
            wide_lo((6, 7), xT_hi, xT_lo, 4, V_GN)

            def gate_branch2(g, half, bank):
                for t in range(TILES):
                    v = gates2[g, half][:, t, :]
                    nc.vector.scalar_tensor_tensor(v, v, 1.0, B[:, bank + t, :], ALU.add, ALU.mult).then_inc(sem("gated"), 1)

            def merge2(half, count):
                for t in range(TILES):
                    dve.wait_ge(sem("gated"), count + t + 1)
                    nc.vector.tensor_tensor(nat[:, half, t, :], gates2[0, half][:, t, :], gates2[1, half][:, t, :], ALU.add)\
                        .then_inc(sem("mixed_done"), 1)

            def add_gated(t, half, bank, g, i):
                v = temp[:, i % 2, :]
                if i >= 2:
                    dve.wait_ge(sem("h_done"), 12 + 4 * g + i - 1)
                link(nc.vector.tensor_tensor(v, B[:, bank, :], gate_b[:, g, 512 * half:512 * half + 512], ALU.mult))
                hv = h[:, t, 512 * half:512 * half + 512]
                nc.vector.tensor_tensor(hv, v, hv, ALU.add).then_inc(sem("h_done"), 1)

            split_to(U_RP + 2)
            dve.wait_ge(sem("evac"), 24)
            dve.wait_ge(units_used, U_BR2 + 4)
            gate_branch2(0, 0, 2)
            gate_branch2(0, 1, 0)
            split_to(U_RP + 2 + AHEAD)
            dve.wait_ge(units_used, U_RP + 4)
            gate_branch2(1, 0, 4)
            split_to(U_RP + 6)
            merge2(0, 12)
            split_to(U_WO)
            wide_lo((2, 3), sT_hi, sT_lo, 0)
            split_to(U_WO + 1)
            dve.wait_ge(units_used, U_WO)
            gate_branch2(1, 1, 6)
            split_to(U_WO + 2)
            merge2(1, 14)
            split_to(U_WO + 1 + AHEAD)
            wide_lo((0, 1), sT_hi, sT_lo, 4)
            split_to(U_WO + 5 + AHEAD)
            dve.wait_ge(units_used, U_WO + 6)
            for t in range(TILES):
                add_gated(t, 0, 4 + t, 0, t)
            split_to(U_WO + 7)
            dve.wait_ge(sem("last_first_tile"), 3)
            add_gated(0, 1, 6, 0, 2)
            dve.wait_ge(units_used, U_WO + 8)
            add_gated(1, 1, 7, 0, 3)
            mean_square(5, 24).then_inc(sem("ms_done"), 1)
            scaled_identity(5, 5)
            split_to(U_FN + 1)
            wide_lo_affine((2, 3), xT_hi, xT_lo, 0, gate_a2, ada_col[:, 16:24], 8)
            wide_lo_affine((4, 5), xT_hi, xT_lo, 4, gate_a2, ada_col[:, 16:24], 8)

            def ffn_lo(par, count):
                dve.wait_ge(sem("ffn_hi"), count)
                nc.vector.tensor_tensor(sT_lo[:, 2 * par:2 * par + 2, :], B[:, 2 + par, :].rearrange("p (k n) -> p k n", k=2),
                                        sT_hi[:, 2 * par:2 * par + 2, :].bitcast(F32), ALU.subtract).then_inc(sem("ffn_lo"), 1)

            def ffn_hidden(par, count):
                dve.wait_ge(sem("ffn_tanh"), count)
                a = ffn_gate[:, par, :].rearrange("p (t n) -> p t n", t=2)
                nc.vector.scalar_tensor_tensor(a, a, 1.0, B[:, 0:2, 0:256], ALU.add, ALU.mult).then_inc(sem("ffn_silu"), 1)
                dve.wait_ge(sem("ffn_silu"), count)
                nc.vector.tensor_tensor(ffn_hid[:, par, :].rearrange("p (t n) -> p t n", t=2), B[:, 0:2, 256:512], a, ALU.mult)\
                    .then_inc(sem("ffn_hid"), 1)

            split_to(U_FN + 3 + FFN_AHEAD)
            ffn_hidden(0, 1)
            ffn_lo(0, 1)
            with dve.Fori(0, (FN_CHUNKS - 1) // 2) as i:
                def ffn_split(q):
                    u = U_FNL + q
                    dve.wait_ge(hi_done, i * 12 + (u + 1))
                    nc.vector.tensor_tensor(w_lo[:, u % SPLIT, :, :], raw[:, st.slot[u], :, :],
                                            w_hi[:, u % SPLIT, :, :].bitcast(F32), ALU.subtract).then_inc(lo_done, 1)

                for half in range(2):
                    for q in range(FFN_AHEAD, 4 + FFN_AHEAD):
                        ffn_split(6 * half + q)
                    ffn_hidden(1 - half, i * 2 + (half + 2))
                    for q in range(4 + FFN_AHEAD, 6 + FFN_AHEAD):
                        ffn_split(6 * half + q)
                    ffn_lo(1 - half, i * 2 + (half + 2))
            done[0] = U_FNE + FFN_AHEAD
            split_to(U_END - 1)
            def final_mean_square(t):
                dve.wait_ge(sem("squares"), 26 + 2 * t)
                nc.vector.scalar_tensor_tensor(ms[:, 6, t:t + 1], sq[:, 6, 0, t:t + 1], EPS, sq[:, 6, 1, t:t + 1], ALU.add,
                                               ALU.add).then_inc(sem("ms_done"), 1)

            def final_norm(t):
                dve.wait_ge(sem("rstd_done"), 6 + t)
                for half in range(2):
                    hv = h[:, t, 512 * half:512 * half + 512]
                    nc.vector.scalar_tensor_tensor(hv, hv, rstd[:, 6, t:t + 1], grow2[:, 512 * half:512 * half + 512], ALU.mult,
                                                   ALU.mult).then_inc(sem("y_ready"), 1)

            for t in range(TILES):
                for half in range(2):
                    if t and half:
                        final_mean_square(0)
                    dve.wait_ge(sem("ffn_out"), 2 * t + half + 1)
                    add_gated(t, half, 4 + t + 2 * half, 1, 2 * t + half)
            dve.wait_ge(sem("grow2_in"), 16)
            final_norm(0)
            final_mean_square(1)
            final_norm(1)

        @block.tensor
        def _(pe):
            def mm3(bank, xh, xl, wh, wl, start, stop):
                nc.tensor.matmul(bank, xh, wh, start=start, stop=False)
                nc.tensor.matmul(bank, xh, wl, start=False, stop=False)
                return nc.tensor.matmul(bank, xl, wh, start=False, stop=stop)

            def unit_pair(u, xh, xl, kt0, banks, first, last, n=None):
                n = spans(u) if n is None else n
                s = u % SPLIT
                for kk in range(2):
                    for t in range(TILES):
                        rows = slice(t * P, (t + 1) * P)
                        m = mm3(B[:, banks[t], 0:n], xh[:, kt0 + kk, rows], xl[:, kt0 + kk, rows],
                                w_hi[:, s, kk, 0:n], w_lo[:, s, kk, 0:n], first and kk == 0, last and kk == 1)
                m.then_inc(units_used, 1)

            def last_unit(u, xh, xl, kt0, banks):
                s = u % SPLIT
                for t in range(TILES):
                    rows = slice(t * P, (t + 1) * P)
                    for kk in range(2):
                        m = mm3(B[:, banks[t], :], xh[:, kt0 + kk, rows], xl[:, kt0 + kk, rows], w_hi[:, s, kk, :], w_lo[:, s, kk, :],
                                False, kk == 1)
                    m.then_inc(units_used if t else sem("last_first_tile"), 1)

            def unit_wide(u, xh, xl, kt, banks, first, last):
                s = u % SPLIT
                for t in range(TILES):
                    rows = slice(t * P, (t + 1) * P)
                    for half in range(2):
                        m = mm3(B[:, banks[t][half], :], xh[:, kt, rows], xl[:, kt, rows], w_hi[:, s, half, :], w_lo[:, s, half, :],
                                first, last)
                m.then_inc(units_used, 1)

            def transposes(banks, src, name, nk=2):
                for i, b in enumerate(banks):
                    for kk in range(nk):
                        for t in range(TILES):
                            m = nc.tensor.transpose(B[:, b, kk * SEQ + t * P:kk * SEQ + (t + 1) * P], src(t, 2 * i + kk), ident)
                    m.then_inc(sem(name), 1)

            def head_slices(n):
                return 64 * (n % 2), 64 * (n % 2) + 64, (n % HEADS) // 2

            def head_pt(n):
                pe.wait_ge(sem("probs_done"), n + 1)
                if n:
                    pe.wait_ge(sem("pt_copied"), n)
                for i, (k0, q0) in enumerate(((0, 0), (P, P), (2 * P, 2 * P))):
                    m = nc.tensor.transpose(B[:, 6, i * P:(i + 1) * P], prob[:, n % 2, k0:k0 + P], ident)
                m.then_inc(sem("pt_done"), 1)

            def head_pv(n, v, c0):
                pe.wait_ge(sem("pt_copied"), n + 1)
                m_ = n // 2
                if n % 2 == 0 and m_ >= 1:
                    pe.wait_ge(sem("aT_lo"), m_)
                p0 = 64 * (n % 2)
                f0 = (m_ % 2) * SEQ
                nc.tensor.matmul(B[p0:p0 + 64, 7, f0:f0 + SEQ], v[:, 0, c0:c0 + HD], probT[:, n % 2, 0:SEQ], start=True, stop=False)
                nc.tensor.matmul(B[p0:p0 + 64, 7, f0 + P:f0 + SEQ], v[:, 1, c0:c0 + HD], probT[:, n % 2, SEQ:KEYS],
                                 start=False, stop=True).then_inc(sem("pv_done"), 1)

            pe.wait_ge(sem("ident_in"), 16)
            pe.wait_ge(sem("g_mix_in"), 16)
            nc.tensor.transpose(B[:, 7, 0:8], vrows[0:8, :], ident[0:8, 0:8]).then_inc(sem("vec_T"), 1)
            pe.wait_ge(sem("x_in0"), 32)
            transposes((0, 1), lambda t, k: h[:, t, k * P:(k + 1) * P], "wt_done")
            pe.wait_ge(sem("x_in1"), 32)
            transposes((2, 3), lambda t, k: h[:, t, (4 + k) * P:(5 + k) * P], "wt_done")
            for c in range(5):
                banks = (2 * (c % 2), 2 * (c % 2) + 1)
                for kp in range(4):
                    u = 4 * c + kp
                    if c == 0:
                        pe.wait_ge(sem("wt_lo"), max(kp + 1, 2))
                    elif c == 1 and kp == 0:
                        pe.wait_ge(sem("wt_lo"), 4)
                    if c >= 2 and kp == 0:
                        pe.wait_ge(sem("evac"), c - 1)
                    pe.wait_ge(lo_done, u + 1)
                    unit_pair(u, xT_hi, xT_lo, 2 * kp, banks, kp == 0, kp == 3)
                if c == 0:
                    pe.wait_ge(sem("vectors_in"), 112)
                    pe.wait_ge(sem("vec_done"), 1)
                    nc.tensor.transpose(B[:, 7, 0:V_ROWS], vrows[0:V_ROWS, :], ident[0:V_ROWS, 0:V_ROWS]).then_inc(sem("vec_T"), 1)
                if c >= 1:
                    k = c - 1
                    pe.wait_ge(sem("evac"), c)
                    if k:
                        pe.wait_ge(sem("natT_copied"), k)
                    if k == 0:
                        transposes((4,), lambda t, kk: nat[:, 0, t, kk * P:(kk + 1) * P], "natT_bank")
                    else:
                        transposes((4, 5), lambda t, kk: nat[:, k % 2, t, kk * P:(kk + 1) * P], "natT_bank")
                if c == 2:
                    pe.wait_ge(sem("log_f"), 2)
                    pe.wait_ge(sem("consts_in"), 16)
                    pe.wait_ge(sem("ones"), 1)
                    nc.tensor.matmul(B[0:LO_ROW + HEADS, 7, 0:P], lf[:, 0, :], upper, start=True, stop=True)
                    nc.tensor.matmul(B[0:LO_ROW + HEADS, 7, P:SEQ], lf[:, 0, :], ones, start=True, stop=False)
                    nc.tensor.matmul(B[0:LO_ROW + HEADS, 7, P:SEQ], lf[:, 1, :], upper, start=False, stop=True).then_inc(sem("cum_done"), 1)
            for n in range(2 * HEADS + 4):
                u = 20 + n
                c = u // 4
                kp = u % 4
                if n < 16:
                    if kp == 0:
                        pe.wait_ge(sem("evac"), c - 1)
                    pe.wait_ge(lo_done, u + 1)
                    unit_pair(u, xT_hi, xT_lo, 2 * kp, (2 * (c % 2), 2 * (c % 2) + 1), kp == 0, kp == 3)
                else:
                    i = n - 16
                    if i == 0:
                        pe.wait_ge(sem("aT_lo"), 4)
                        pe.wait_ge(sem("evac"), 8)
                    if i == 2:
                        pe.wait_ge(sem("evac"), 9)
                    pe.wait_ge(lo_done, u + 1)
                    unit_pair(u, sT_hi, sT_lo, 2 * (i % 2), ((2, 3), (0, 1))[i // 2], i % 2 == 0, i % 2 == 1)
                if n < 16:
                    if n == 0:
                        pe.wait_ge(sem("tables"), 1)
                        pe.wait_ge(sem("natT_copied"), 4)
                        pe.wait_ge(sem("cum_lo"), 1)
                    if n >= 2:
                        pe.wait_ge(sem("exp_done"), n - 1)
                    p0, p1, kq = head_slices(n)
                    if n < HEADS:
                        qT, kT, kk = qaT, kaT, n // 4
                    else:
                        qT, kT, kk = qbT, kbT, kq
                    for t, (k0, k1) in enumerate(TILE_KEYS):
                        s = B[:, 4 + n % 2, k0:k1]
                        rows = slice(t * P, (t + 1) * P)
                        nc.tensor.matmul(s, qT[p0:p1, kq, rows], kT[p0:p1, kk, 0:k1 - k0], start=True, stop=False)
                        if n < HEADS:
                            m = nc.tensor.matmul(s, slope_id[:, n, :], swa_dist[:, k0:k1], start=False, stop=True)
                        else:
                            hh = n - HEADS
                            nc.tensor.matmul(s, pick[:, hh, :], cum[:, 0, 0:k1 - k0], start=False, stop=False)
                            for kb in range(k0, k1, P):
                                nc.tensor.matmul(B[:, 4 + n % 2, kb:kb + P], cum[:, 1, rows], pick[:, hh, :],
                                                 start=False, stop=False)
                            m = nc.tensor.matmul(s, identr[:, :], causal_r[:, k0:k1], start=False, stop=True)
                    m.then_inc(sem("scores_done"), 1)
                if 0 <= n - 2 < 16:
                    head_pt(n - 2)
                if 0 <= n - 3 < 16:
                    k = n - 3
                    if k < HEADS:
                        head_pv(k, va, HD * (k // 4))
                    else:
                        head_pv(k, vb, HD * (k - HEADS))
            pe.wait_ge(sem("aT_lo"), 8)
            for i in range(4):
                u = U_BR + 4 + i
                pe.wait_ge(lo_done, u + 1)
                unit_pair(u, sT_hi, sT_lo, 4 + 2 * (i % 2), ((4, 5), (6, 7))[i // 2], i % 2 == 0, i % 2 == 1)
                if i == 2:
                    pe.wait_ge(sem("mixed_done"), 2)
                    transposes((2, 3), lambda t, k: nat[:, 0, t, k * P:(k + 1) * P], "wt_done")

            def half_rows(src, half):
                return lambda t, k: src[:, t, half * 512 + k * P:half * 512 + (k + 1) * P]

            for i, (half, kp) in enumerate(SQUARE):
                if half == 0:
                    pe.wait_ge(sem("wt_lo"), 4 + kp + 1)
                elif kp == 0:
                    pe.wait_ge(sem("mixed_done"), 4)
                pe.wait_ge(lo_done, U_MO + i + 1)
                if i == 7:
                    last_unit(U_MO + i, xT_hi, xT_lo, 6, (6, 7))
                else:
                    unit_pair(U_MO + i, xT_hi, xT_lo, 2 * kp, (4 + 2 * half, 5 + 2 * half), kp == 0, kp == 3)
                if i == 1:
                    pe.wait_ge(sem("mixed_done"), 4)
                    transposes((0, 1), lambda t, k: nat[:, 1, t, k * P:(k + 1) * P], "wt_done")
                if i == 6:
                    pe.wait_ge(sem("h_done"), 2)
                    transposes((2, 3), half_rows(h, 0), "wt_done")
            def hidden_T():
                transposes((2, 3), lambda t, k: nat[:, 1, t, k * P:(k + 1) * P], "hid_T")

            for kp in range(4):
                u = U_FF + kp
                pe.wait_ge(sem("wt_lo"), 8 + kp + 1)
                pe.wait_ge(lo_done, u + 1)
                unit_pair(u, sT_hi, sT_lo, 2 * kp, (0, 1), kp == 0, kp == 3)
                if kp == 0:
                    pe.wait_ge(sem("h_done"), 4)
                    transposes((4, 5), half_rows(h, 1), "wt_done")
            acc = ((4, 6), (5, 7))
            for b in (4, 5, 6, 7):
                nc.tensor.matmul(B[:, b, :], zero_r[:, :], sT_hi[:, 0:2, :].rearrange("p k n -> p (k n)"), start=True, stop=False)
            pe.wait_ge(sem("squared"), 2)
            hidden_T()
            with pe.Fori(1, FF_CHUNKS) as j:
                for r in range(4):
                    pe.wait_ge(lo_done, j * 8 + (U_FFL + r - 7))
                    unit_pair(U_FFL + r, sT_hi, sT_lo, 2 * r, (0, 1), r == 0, r == 3, 512)
                for r in range(4):
                    if r == 0:
                        pe.wait_ge(sem("hid_lo"), j * 2 - 1)
                    pe.wait_ge(lo_done, j * 8 + (U_FFL + r - 3))
                    unit_wide(U_FFL + 4 + r, xT_hi, xT_lo, r, acc, False, False)
                    if r == 1:
                        pe.wait_ge(sem("hid_lo"), j * 2)
                        pe.wait_ge(sem("squared"), j * 2 + 2)
                        hidden_T()
            pe.wait_ge(sem("p_in"), 16)
            transposes((0,), lambda t, k: p_sb[:, t, k * P:(k + 1) * P], "pT_done")
            for r in range(4):
                if r % 2 == 0:
                    pe.wait_ge(sem("hid_lo"), 2 * FF_CHUNKS - 1 + r // 2)
                pe.wait_ge(lo_done, U_FFE + r + 1)
                unit_wide(U_FFE + r, xT_hi, xT_lo, r, acc, False, r == 3)
            pe.wait_ge(sem("pT_lo"), 1)
            for r in range(2):
                pe.wait_ge(lo_done, U_PP + r + 1)
                unit_wide(U_PP + r, xT_hi, xT_lo, 4 + r, ((0, 1), (2, 3)), r == 0, r == 1)
                pe.wait_ge(sem("h_done"), 6 + 2 * r)
                transposes(((4, 5), (6, 7))[r], half_rows(h, r), "wt_done")
            for i in range(8):
                half, kp = i // 4, i % 4
                if half == 0:
                    pe.wait_ge(sem("wt_lo"), 12 + (kp + 1 if kp else 2))
                pe.wait_ge(lo_done, U_PG + i + 1)
                if i == 7:
                    last_unit(U_PG + i, sT_hi, sT_lo, 6, (6, 7))
                else:
                    unit_pair(U_PG + i, sT_hi, sT_lo, 2 * kp, (4 + 2 * half, 5 + 2 * half), kp == 0, kp == 3)
                if i in (2, 4):
                    j = i // 2 - 1
                    pe.wait_ge(sem("ada_lo"), j + 1)
                    if j == 0:
                        pe.wait_ge(sem("pp0_done"), 1)
                    for k in range(4):
                        row = 4 * j + k
                        onehot = one_row[:, 7 - row:15 - row]
                        nc.tensor.matmul(B[0:8, 0, :], onehot, ada_hi[:, k * 512:(k + 1) * 512], start=row == 0, stop=False)
                        m = nc.tensor.matmul(B[0:8, 0, :], onehot, ada_lo[:, k * 512:(k + 1) * 512], start=False, stop=row == 7)
                    m.then_inc(sem("ada_rows"), 1)
            pe.wait_ge(sem("ada_rows_in"), 16)
            nc.tensor.transpose(B[:, 0, 0:32], vrows[0:32, :], ident[0:32, 0:32]).then_inc(sem("ada_cols"), 1)

            pe.wait_ge(sem("ada_lo"), 4)
            pe.wait_ge(sem("pg_exp"), 4)
            for i in range(4):
                g, c0 = i // 2, 512 * (i % 2)
                nc.tensor.matmul(B[:, 4 + i, :], ones_r[:, :], ada_hi[:, g * D + c0:g * D + c0 + 512], start=True, stop=False)
                nc.tensor.matmul(B[:, 4 + i, :], ones_r[:, :], ada_lo[:, g * D + c0:g * D + c0 + 512], start=False, stop=True)\
                    .then_inc(sem("gate_sum"), 1)

            def normed_T(banks, src, half, scales):
                for i, b in enumerate(banks):
                    for kk in range(2):
                        k = 4 * half + 2 * i + kk
                        for t in range(TILES):
                            if scales is not None:
                                pe.wait_ge(sem("rstd_id"), scales + t + 1)
                            m = nc.tensor.matmul(B[:, b, kk * SEQ + t * P:kk * SEQ + (t + 1) * P], src[:, t, k * P:(k + 1) * P],
                                                 rstd_id[:, t, :], start=True, stop=True)
                        scales = None
                    m.then_inc(sem("wt_done"), 1)

            pe.wait_ge(sem("hg_done"), 4)
            normed_T((2, 3), pg, 0, 0)
            pe.wait_ge(sem("gate_b"), 2)
            normed_T((4, 5), pg, 1, None)
            NAT_T = {7: (4, (6, 7), 2), 11: (5, (6,), 1), 15: (6, (6, 7), 2), 19: (7, (6, 7), 2), 27: (8, (6, 7), 2), 31: (9, (6, 7), 2)}
            for q in range(60):
                u = U_IN2 + q
                c, kp = q // 4, q % 4
                if c == 0:
                    pe.wait_ge(sem("affine_lo"), kp + 1)
                elif kp == 0 and c >= 2:
                    pe.wait_ge(sem("evac"), 9 + c - 1)
                    if c in (11, 12):
                        pe.wait_ge(sem("gr_done"), 2 * (c - 10))
                pe.wait_ge(lo_done, u + 1)
                unit_pair(u, xT_hi, xT_lo, 2 * kp, (2 * (c % 2), 2 * (c % 2) + 1), kp == 0, kp == 3)
                if q in NAT_T:
                    k, banks, nk = NAT_T[q]
                    if q == 7:
                        pe.wait_ge(sem("gate_b"), 4)
                    pe.wait_ge(sem("roped"), k - 3)
                    pe.wait_ge(sem("natT_copied"), k)
                    transposes(banks, lambda t, kk: nat[:, k % 2, t, kk * P:(kk + 1) * P], "natT_bank", nk)
                if 13 <= q < 21:
                    i = q - 13
                    if i == 0:
                        pe.wait_ge(sem("natT_copied"), 6)
                    if i >= 2:
                        pe.wait_ge(sem("index_relu"), i - 1)
                    p0 = 64 * (i % 2)
                    for t, (k0, k1) in enumerate(TILE_KEYS):
                        m = nc.tensor.matmul(B[:, 4 + i % 2, k0:k1], iqT[p0:p0 + 64, i // 2, t * P:(t + 1) * P],
                                             ikT[p0:p0 + 64, 0, 0:k1 - k0], start=True, stop=True)
                    m.then_inc(sem("index_done"), 1)
                if 33 <= q < 41:
                    n = q - 17
                    if n == 16:
                        pe.wait_ge(sem("selected"), 1)
                        pe.wait_ge(sem("index_relu"), HEADS)
                        pe.wait_ge(sem("natT_copied"), 8)
                    else:
                        pe.wait_ge(sem("exp_done"), n - 1)
                    p0, p1, kq = head_slices(n)
                    for t, (k0, k1) in enumerate(TILE_KEYS):
                        s = B[:, 4 + n % 2, k0:k1]
                        nc.tensor.matmul(s, qsT[p0:p1, kq, t * P:(t + 1) * P], ksT[p0:p1, kq, 0:k1 - k0], start=True, stop=False)
                        m = nc.tensor.matmul(s, identr[:, :], selected[:, k0:k1], start=False, stop=True)
                    m.then_inc(sem("scores_done"), 1)
                if 35 <= q < 43:
                    if q == 35:
                        pe.wait_ge(sem("natT_copied"), 10)
                    head_pt(q - 19)
                if 36 <= q < 44:
                    head_pv(q - 20, vs, HD * (q - 36))
                if q >= 44 and (q - 44) % 3 == 0 and (q - 44) // 3 < R_HEADS:
                    i = (q - 44) // 3
                    pe.wait_ge(sem("exp_done"), 24)
                    if i >= 2:
                        pe.wait_ge(sem("decayed"), i - 1)
                    nc.tensor.matmul(B[:, 4 + i % 2, 0:SEQ], krT[:, i, 0:P], qrT[:, i, :], start=True, stop=True)
                    nc.tensor.matmul(B[:, 4 + i % 2, SEQ:KEYS], krT[:, i, P:SEQ], qrT[:, i, P:SEQ], start=True, stop=True)\
                        .then_inc(sem("kq_done"), 1)
                if q >= 46 and (q - 46) % 3 == 0 and (q - 46) // 3 < R_HEADS:
                    i = (q - 46) // 3
                    pe.wait_ge(sem("decayed"), i + 1)
                    if i == 0:
                        pe.wait_ge(sem("aT_lo"), 12)
                    if i >= 2:
                        pe.wait_ge(sem("og_done"), i - 1)
                    o = B[:, 6 + i % 2, :]
                    v0, v1 = vr[:, 0, i * R_DV:(i + 1) * R_DV], vr[:, 1, i * R_DV:(i + 1) * R_DV]
                    w = prob[:, i % 2, :]
                    nc.tensor.matmul(o[:, 0:R_DV], w[:, 0:P], v0, start=True, stop=True)
                    nc.tensor.matmul(o[:, R_DV:2 * R_DV], w[:, P:SEQ], v0, start=True, stop=False)
                    nc.tensor.matmul(o[:, R_DV:2 * R_DV], w[:, SEQ:KEYS], v1, start=False, stop=True).then_inc(sem("av_done"), 1)
            pe.wait_ge(sem("decayed"), R_HEADS)
            pe.wait_ge(sem("y_gated"), 2 * R_HEADS)
            transposes((4, 5), half_rows(gr, 0), "wt_done")
            pe.wait_ge(sem("gn_half"), 1)
            transposes((6, 7), half_rows(gr, 1), "wt_done")
            for i in range(4):
                u = U_BR2 + i
                if i % 2 == 0:
                    pe.wait_ge(sem("evac"), 23 + i // 2)
                pe.wait_ge(lo_done, u + 1)
                unit_pair(u, sT_hi, sT_lo, 2 * (i % 2), ((2, 3), (0, 1))[i // 2], i % 2 == 0, i % 2 == 1)
            for i in range(8):
                u = U_RP + i
                kp = i % 4
                pe.wait_ge(sem("wt_lo"), 20 if i == 4 else 16 + max(kp + 1, 2))
                pe.wait_ge(lo_done, u + 1)
                unit_pair(u, xT_hi, xT_lo, 2 * kp, ((4, 5), (6, 7))[i // 4], kp == 0, kp == 3)
                if i == 6:
                    pe.wait_ge(sem("mixed_done"), 6)
                    transposes((2, 3), lambda t, k: nat[:, 0, t, k * P:(k + 1) * P], "wt_done")
            for i, (half, kp) in enumerate(SQUARE):
                if half == 0:
                    pe.wait_ge(sem("wt_lo"), 20 + kp + 1)
                pe.wait_ge(lo_done, U_WO + i + 1)
                if i == 7:
                    last_unit(U_WO + i, sT_hi, sT_lo, 6, (6, 7))
                else:
                    unit_pair(U_WO + i, sT_hi, sT_lo, 2 * kp, (4 + 2 * half, 5 + 2 * half), kp == 0, kp == 3)
                if i == 1:
                    pe.wait_ge(sem("mixed_done"), 8)
                    transposes((0, 1), lambda t, k: nat[:, 1, t, k * P:(k + 1) * P], "wt_done")
            pe.wait_ge(sem("h_done"), 16)
            normed_T((2, 3), h, 0, 2)
            normed_T((4, 5), h, 1, None)

            def ffn_T(par):
                for kk in range(2):
                    for t in range(TILES):
                        m = nc.tensor.transpose(B[:, 2 + par, kk * SEQ + t * P:kk * SEQ + (t + 1) * P],
                                                ffn_hid[:, par, t * 256 + kk * P:t * 256 + (kk + 1) * P], ident)
                m.then_inc(sem("ffn_T"), 1)

            for kp in range(4):
                pe.wait_ge(sem("affine_lo"), 4 + kp + 1)
                pe.wait_ge(lo_done, U_FN + kp + 1)
                unit_pair(U_FN + kp, xT_hi, xT_lo, 2 * kp, (0, 1), kp == 0, kp == 3)
            for b in (4, 5, 6, 7):
                nc.tensor.matmul(B[:, b, :], zero_r[:, :], xT_hi[:, 0:2, :].rearrange("p k n -> p (k n)"), start=True, stop=False)
            pe.wait_ge(sem("ffn_hid"), 1)
            ffn_T(0)
            with pe.Fori(0, (FN_CHUNKS - 1) // 2) as i:
                for half in range(2):
                    for e in range(6):
                        u = U_FNL + 6 * half + e
                        if e == 4:
                            pe.wait_ge(sem("ffn_lo"), i * 2 + (half + 1))
                        pe.wait_ge(lo_done, i * 12 + (u + 1))
                        if e < 4:
                            unit_pair(u, xT_hi, xT_lo, 2 * e, (0, 1), e == 0, e == 3, 512)
                        else:
                            unit_wide(u, sT_hi, sT_lo, 2 * half + e - 4, acc, False, False)
                        if e == 4:
                            pe.wait_ge(sem("ffn_hid"), i * 2 + (half + 2))
                            ffn_T(1 - half)
            pe.wait_ge(sem("ffn_lo"), FN_CHUNKS)
            pe.wait_ge(lo_done, U_FNE + 2)
            for t in range(TILES):
                rows = slice(t * P, (t + 1) * P)
                for half in range(2):
                    for e in range(2):
                        k = (U_FNE + e) % SPLIT
                        m = mm3(B[:, acc[t][half], :], sT_hi[:, e, rows], sT_lo[:, e, rows], w_hi[:, k, half, :], w_lo[:, k, half, :],
                                False, e == 1)
                    m.then_inc(sem("ffn_out"), 1)


_INS = ["x", "p", "g_mix", "w_in", "b_forget", "swa_sinks", "w_br_swa", "w_br_fox", "w_mix_out", "g_mlp", "w_ff1", "w_ff2",
        "g_ple", "w_ple_gate", "w_ple_proj", "g_final", "c_2", "w_ada_2", "b_ada_2", "norm1_w_2", "w_in_2", "w_attn_proj_2",
        "w_ret_proj_2", "gn_w_2", "w_out_2", "norm2_w_2", "w_ffn_gate_2", "w_ffn_up_2", "w_ffn_down_2", "final_norm_w_2"]


def kernel(**inputs):
    import concourse.bacc as bacc
    from concourse.bass_utils import run_bass_kernel_spmd

    nc = bacc.Bacc("TRN2", target_bir_lowering=False, num_devices=1)
    arrays, args = {}, []

    def give(name, a):
        arrays[f"in_{name}_dram"] = a
        args.append(nc.dram_tensor(f"in_{name}_dram", a.shape, F32, kind="ExternalInput").ap())

    for name in _INS:
        give(name, np.ascontiguousarray(inputs[name]))
    tables, decay = constants()
    give("tables", tables)
    give("decay", decay)
    args.append(nc.dram_tensor("out_0_dram", (1, SEQ, D), F32, kind="ExternalOutput").ap())
    build(nc, *args)
    return run_bass_kernel_spmd(nc, [arrays], core_ids=[0]).results[0]["out_0_dram"]
```
